# Optimizing a Trainium2 kernel written in Bass

```python
import math
import jax, jax.numpy as jnp
from jax import lax
import numpy as np

D_MODEL = 1024
BATCH = 1
SEQ = 256
DEPTH = 2

MEM_LEN = 256
CHUNK = 64
Q_BLOCK = 128
ROPE_THETA = 10000.0
EPS = 1e-6
NEG_BIG = -1e30

DIFF_HEADS = 8
DIFF_HD = 64
DIFF_VD = 2 * DIFF_HD
DIFF_W = DIFF_HEADS * DIFF_VD

LRU_W = D_MODEL
LRU_BLOCKS = 8
LRU_BW = LRU_W // LRU_BLOCKS
CONV_W = 4
RG_C = 8.0

XATTN_HEADS = 4
XATTN_HD = D_MODEL // XATTN_HEADS
XATTN_W = XATTN_HEADS * XATTN_HD

N_BRANCH = 3
D_FF = 4 * D_MODEL

IN_SPLITS = (
    2 * DIFF_HEADS * DIFF_HD,
    2 * DIFF_HEADS * DIFF_HD,
    DIFF_W,
    LRU_W,
    LRU_W,
    XATTN_W,
    N_BRANCH * D_MODEL,
)
N_IN = sum(IN_SPLITS)


def rms_norm(x, g):
    xf = x.astype(jnp.float32)
    y = xf * lax.rsqrt(jnp.mean(xf * xf, axis=-1, keepdims=True) + EPS)
    return (y * g.astype(jnp.float32)).astype(x.dtype)

def in_projection(h, w):
    outs = []
    start = 0
    for n in IN_SPLITS:
        outs.append(h @ w[:, start:start + n])
        start += n
    return outs

def rope_tables(seq_len):
    half = DIFF_HD // 2
    pos = jnp.arange(seq_len, dtype=jnp.float32)
    inv = 1.0 / (ROPE_THETA ** (jnp.arange(half, dtype=jnp.float32) / half))
    ang = pos[:, None] * inv[None, :]
    return jnp.cos(ang), jnp.sin(ang)

def apply_rope(t, cos, sin):
    half = DIFF_HD // 2
    c = cos[:, None, None, :]
    s = sin[:, None, None, :]
    tf = t.astype(jnp.float32)
    t1, t2 = tf[..., :half], tf[..., half:]
    return jnp.concatenate([t1 * c - t2 * s, t2 * c + t1 * s], axis=-1).astype(t.dtype)

def diff_attention(q, k, v, lam, subln_g, lam_init):
    B, S = q.shape[0], q.shape[1]
    nq = S // Q_BLOCK
    scale = DIFF_HD ** -0.5
    qt = q.transpose(3, 0, 2, 1, 4)
    kt = k.transpose(3, 0, 2, 1, 4)
    k1, k2 = kt[0], kt[1]
    vt = v.transpose(0, 2, 1, 3)
    qblocks = qt.reshape(2, B, DIFF_HEADS, nq, Q_BLOCK, DIFF_HD).transpose(3, 0, 1, 2, 4, 5)
    key_chunk = jnp.arange(S) // CHUNK

    def block(args):
        qb, idx = args
        q_chunk = (idx * Q_BLOCK + jnp.arange(Q_BLOCK)) // CHUNK
        mask = key_chunk[None, :] <= q_chunk[:, None]
        s1 = jnp.einsum('bhqd,bhkd->bhqk', qb[0], k1).astype(jnp.float32) * scale
        s2 = jnp.einsum('bhqd,bhkd->bhqk', qb[1], k2).astype(jnp.float32) * scale
        p1 = jax.nn.softmax(jnp.where(mask, s1, NEG_BIG), axis=-1)
        p2 = jax.nn.softmax(jnp.where(mask, s2, NEG_BIG), axis=-1)
        p = p1 - lam * p2
        return jnp.einsum('bhqk,bhkv->bhqv', p.astype(vt.dtype), vt)

    out = lax.map(block, (qblocks, jnp.arange(nq)))
    out = out.transpose(1, 0, 3, 2, 4).reshape(B, S, DIFF_HEADS, DIFF_VD)
    out = rms_norm(out, subln_g) * (1.0 - lam_init)
    return out.reshape(B, S, DIFF_W)

def causal_conv(x, w, b):
    S = x.shape[1]
    xp = jnp.pad(x, ((0, 0), (CONV_W - 1, 0), (0, 0)))
    y = xp[:, 0:S] * w[0]
    for t in range(1, CONV_W):
        y = y + xp[:, t:t + S] * w[t]
    return y + b

def rg_lru(x, wa, ba, wi, bi, lam):
    B, S, W = x.shape
    xf = x.astype(jnp.float32)
    xb = xf.reshape(B, S, LRU_BLOCKS, LRU_BW)
    r = jax.nn.sigmoid(jnp.einsum('bsnc,ncd->bsnd', xb, wa.astype(jnp.float32)).reshape(B, S, W)
                       + ba.astype(jnp.float32))
    i = jax.nn.sigmoid(jnp.einsum('bsnc,ncd->bsnd', xb, wi.astype(jnp.float32)).reshape(B, S, W)
                       + bi.astype(jnp.float32))
    log_a = -RG_C * r * jax.nn.softplus(-lam.astype(jnp.float32))
    a = jnp.exp(log_a)
    u = jnp.sqrt(-jnp.expm1(2.0 * log_a)) * (i * xf)

    def combine(left, right):
        a_l, u_l = left
        a_r, u_r = right
        return a_l * a_r, a_r * u_l + u_r

    _, hs = lax.associative_scan(combine, (a, u), axis=1)
    return hs.astype(x.dtype)

def memory_attention(zq, mem, g_mem, w_kv):
    B, S = zq.shape[0], zq.shape[1]
    M = mem.shape[1]
    q = zq.reshape(B, S, XATTN_HEADS, XATTN_HD)
    kv = (rms_norm(mem, g_mem) @ w_kv).reshape(B, M, 2, XATTN_HEADS, XATTN_HD)
    s = jnp.einsum('bshd,bmhd->bhsm', q, kv[:, :, 0]).astype(jnp.float32) * (XATTN_HD ** -0.5)
    p = jax.nn.softmax(s, axis=-1)
    o = jnp.einsum('bhsm,bmhd->bshd', p.astype(q.dtype), kv[:, :, 1])
    return o.reshape(B, S, XATTN_W)

def first_inputs(seed: int = 0) -> dict:
    key = jax.random.key(seed)
    ks = iter(jax.random.split(key, 40))
    f32 = jnp.float32

    def nrm(shape, scale):
        return jax.random.normal(next(ks), shape, f32) * scale

    def gain(shape):
        return 1.0 + 0.05 * jax.random.normal(next(ks), shape, f32)

    x = jax.random.normal(next(ks), (BATCH, SEQ, D_MODEL), f32)
    mem = jax.random.normal(next(ks), (BATCH, MEM_LEN, D_MODEL), f32)
    u = jax.random.uniform(next(ks), (DEPTH, LRU_W), f32, minval=0.9, maxval=0.999)
    a0 = u ** (1.0 / RG_C)
    rg_lambda = jnp.log(a0) - jnp.log1p(-a0)
    return {
        'x': x,
        'mem': mem,
        'norm_mix_pre': gain((DEPTH, D_MODEL)),
        'norm_mix_post': gain((DEPTH, D_MODEL)),
        'norm_mlp_pre': gain((DEPTH, D_MODEL)),
        'norm_mlp_post': gain((DEPTH, D_MODEL)),
        'norm_mem': gain((DEPTH, D_MODEL)),
        'w_in': nrm((DEPTH, D_MODEL, N_IN), D_MODEL ** -0.5),
        'b_gate': nrm((DEPTH, N_BRANCH, D_MODEL), 0.1),
        'lambda_q1': nrm((DEPTH, DIFF_HD), 0.1),
        'lambda_k1': nrm((DEPTH, DIFF_HD), 0.1),
        'lambda_q2': nrm((DEPTH, DIFF_HD), 0.1),
        'lambda_k2': nrm((DEPTH, DIFF_HD), 0.1),
        'diff_subln': gain((DEPTH, DIFF_VD)),
        'conv_w': nrm((DEPTH, CONV_W, LRU_W), CONV_W ** -0.5),
        'conv_b': nrm((DEPTH, LRU_W), 0.02),
        'rg_wa': nrm((DEPTH, LRU_BLOCKS, LRU_BW, LRU_BW), LRU_BW ** -0.5),
        'rg_ba': nrm((DEPTH, LRU_W), 0.1),
        'rg_wi': nrm((DEPTH, LRU_BLOCKS, LRU_BW, LRU_BW), LRU_BW ** -0.5),
        'rg_bi': nrm((DEPTH, LRU_W), 0.1),
        'rg_lambda': rg_lambda,
        'w_kv_mem': nrm((DEPTH, D_MODEL, 2 * XATTN_W), D_MODEL ** -0.5),
        'w_proj_attn': nrm((DEPTH, DIFF_W, D_MODEL), DIFF_W ** -0.5),
        'w_proj_lru': nrm((DEPTH, LRU_W, D_MODEL), LRU_W ** -0.5),
        'w_proj_mem': nrm((DEPTH, XATTN_W, D_MODEL), XATTN_W ** -0.5),
        'w_out': nrm((DEPTH, D_MODEL, D_MODEL), D_MODEL ** -0.5),
        'w_mlp_up': nrm((DEPTH, D_MODEL, D_FF), D_MODEL ** -0.5),
        'w_mlp_down': nrm((DEPTH, D_FF, D_MODEL), D_FF ** -0.5),
    }

def first_block(x, mem, norm_mix_pre, norm_mix_post, norm_mlp_pre, norm_mlp_post, norm_mem,
              w_in, b_gate, lambda_q1, lambda_k1, lambda_q2, lambda_k2, diff_subln,
              conv_w, conv_b, rg_wa, rg_ba, rg_wi, rg_bi, rg_lambda, w_kv_mem,
              w_proj_attn, w_proj_lru, w_proj_mem, w_out, w_mlp_up, w_mlp_down):
    B, S, _ = x.shape
    cos, sin = rope_tables(S)
    for l in range(DEPTH):
        h = rms_norm(x, norm_mix_pre[l])
        zq, zk, zv, zx, zy, zxq, zg = in_projection(h, w_in[l])

        q = apply_rope(zq.reshape(B, S, DIFF_HEADS, 2, DIFF_HD), cos, sin)
        k = apply_rope(zk.reshape(B, S, DIFF_HEADS, 2, DIFF_HD), cos, sin)
        v = zv.reshape(B, S, DIFF_HEADS, DIFF_VD)
        lam_init = 0.8 - 0.6 * math.exp(-0.3 * l)
        lam = (jnp.exp(jnp.sum(lambda_q1[l].astype(jnp.float32) * lambda_k1[l].astype(jnp.float32)))
               - jnp.exp(jnp.sum(lambda_q2[l].astype(jnp.float32) * lambda_k2[l].astype(jnp.float32)))
               + lam_init)
        y_attn = diff_attention(q, k, v, lam, diff_subln[l], lam_init)

        xc = causal_conv(zx, conv_w[l], conv_b[l])
        y_lru = rg_lru(xc, rg_wa[l], rg_ba[l], rg_wi[l], rg_bi[l], rg_lambda[l]) * jax.nn.gelu(zy)

        y_mem = memory_attention(zxq, mem, norm_mem[l], w_kv_mem[l])

        gates = jax.nn.sigmoid(zg.reshape(B, S, N_BRANCH, D_MODEL) + b_gate[l])
        merged = (gates[:, :, 0] * (y_attn @ w_proj_attn[l])
                  + gates[:, :, 1] * (y_lru @ w_proj_lru[l])
                  + gates[:, :, 2] * (y_mem @ w_proj_mem[l]))
        x = x + rms_norm(merged @ w_out[l], norm_mix_post[l])

        h = rms_norm(x, norm_mlp_pre[l])
        a = jax.nn.relu(h @ w_mlp_up[l])
        x = x + rms_norm((a * a) @ w_mlp_down[l], norm_mlp_post[l])
    return x


DEPTH_2 = 1

HEAD_DIM = 64
N_SB = 4
N_MOBA = 4
N_FOX = 4
N_DSA = 4
BRANCH_W = 4 * HEAD_DIM
N_BRANCH_2 = 4
MOBA_BLOCK = 256
MOBA_TOPK = 3
MOBA_Q_CHUNK = 32
DSA_TOPK = 256
IDX_HEADS = 8
IDX_DIM = 32
T5_BUCKETS = 32
T5_MAX_DIST = 128
D_FF_2 = 2816
CONV_W_2 = 3
RMS_EPS = 1e-6
NEG_BIG_2 = -1e30

IN_SIZES = (
    [BRANCH_W] * 3
    + [BRANCH_W] * 3
    + [BRANCH_W] * 3 + [N_FOX]
    + [BRANCH_W, HEAD_DIM, HEAD_DIM]
    + [IDX_HEADS * IDX_DIM, IDX_DIM, IDX_HEADS]
)
P_IN = int(sum(IN_SIZES))
IN_SPLITS_2 = tuple(int(v) for v in np.cumsum(IN_SIZES)[:-1])


def rmsnorm(x, g):
    xf = x.astype(jnp.float32)
    y = xf * lax.rsqrt(jnp.mean(xf * xf, axis=-1, keepdims=True) + RMS_EPS)
    return (y * g.astype(jnp.float32)).astype(x.dtype)

def to_heads(t, n):
    b, s, _ = t.shape
    return t.reshape(b, s, n, HEAD_DIM).transpose(0, 2, 1, 3)

def merge_heads(o):
    b, h, s, d = o.shape
    return o.transpose(0, 2, 1, 3).reshape(b, s, h * d)

def t5_bucket(n):
    n = jnp.maximum(n, 0)
    max_exact = T5_BUCKETS // 2
    nf = jnp.maximum(n, 1).astype(jnp.float32)
    large = max_exact + (jnp.log(nf / max_exact) / math.log(T5_MAX_DIST / max_exact)
                         * (T5_BUCKETS - max_exact)).astype(jnp.int32)
    large = jnp.minimum(large, T5_BUCKETS - 1)
    return jnp.where(n < max_exact, n, large)

def stick_breaking_attention(q, k, v):
    s_len = q.shape[2]
    scale = HEAD_DIM ** -0.5
    outs = []
    for i in range(s_len // Q_BLOCK):
        t0, t1 = i * Q_BLOCK, (i + 1) * Q_BLOCK
        z = jnp.einsum('bhqd,bhkd->bhqk', q[:, :, t0:t1], k[:, :, :t1]).astype(jnp.float32) * scale
        strict = jnp.arange(t1)[None, :] < jnp.arange(t0, t1)[:, None]
        log_neg = jnp.where(strict, jax.nn.log_sigmoid(-z), 0.0)
        excl = lax.cumsum(log_neg, axis=3, reverse=True) - log_neg
        w = jnp.where(strict, jnp.exp(jax.nn.log_sigmoid(z) + excl), 0.0)
        outs.append(jnp.einsum('bhqk,bhkd->bhqd', w.astype(v.dtype), v[:, :, :t1]))
    return jnp.concatenate(outs, axis=2)

def forgetting_attention(q, k, v, f_logit):
    s_len = q.shape[2]
    scale = HEAD_DIM ** -0.5
    c = jnp.cumsum(jax.nn.log_sigmoid(f_logit.astype(jnp.float32)), axis=1).transpose(0, 2, 1)
    outs = []
    for i in range(s_len // Q_BLOCK):
        t0, t1 = i * Q_BLOCK, (i + 1) * Q_BLOCK
        logits = jnp.einsum('bhqd,bhkd->bhqk', q[:, :, t0:t1], k[:, :, :t1]).astype(jnp.float32) * scale
        logits = logits + c[:, :, t0:t1, None] - c[:, :, None, :t1]
        causal = jnp.arange(t1)[None, :] <= jnp.arange(t0, t1)[:, None]
        p = jax.nn.softmax(jnp.where(causal, logits, NEG_BIG_2), axis=-1)
        outs.append(jnp.einsum('bhqk,bhkd->bhqd', p.astype(v.dtype), v[:, :, :t1]))
    return jnp.concatenate(outs, axis=2)

def moba_attention(q, k, v, bias_table):
    b, h, s_len, d = q.shape
    scale = HEAD_DIM ** -0.5
    nb = -(-s_len // MOBA_BLOCK)
    pad = nb * MOBA_BLOCK - s_len
    kp = jnp.pad(k, ((0, 0), (0, 0), (0, pad), (0, 0)))
    vp = jnp.pad(v, ((0, 0), (0, 0), (0, pad), (0, 0)))
    kb = kp.reshape(b, h, nb, MOBA_BLOCK, d)
    vb = vp.reshape(b, h, nb, MOBA_BLOCK, d)
    kmean = jnp.mean(kb.astype(jnp.float32), axis=3).astype(k.dtype)
    topk = min(MOBA_TOPK, nb)
    table_t = bias_table.T
    bi = jnp.arange(b)[:, None, None, None]
    hi = jnp.arange(h)[None, :, None, None]

    def chunk(ci):
        t0 = ci * MOBA_Q_CHUNK
        qc = lax.dynamic_slice_in_dim(q, t0, MOBA_Q_CHUNK, axis=2)
        tpos = t0 + jnp.arange(MOBA_Q_CHUNK)
        own = t0 // MOBA_BLOCK
        gate = jnp.einsum('bhqd,bhnd->bhqn', qc, kmean).astype(jnp.float32)
        past = jnp.arange(nb) < own
        gate = jnp.where(past, gate, -jnp.inf)
        _, gidx = lax.top_k(gate, topk)
        sel_valid = gidx < own
        ks = kb[bi, hi, gidx]
        vs = vb[bi, hi, gidx]
        s_sel = jnp.einsum('bhqd,bhqnkd->bhqnk', qc, ks).astype(jnp.float32) * scale
        kpos = gidx[..., None] * MOBA_BLOCK + jnp.arange(MOBA_BLOCK)
        bucket = t5_bucket(tpos[None, None, :, None, None] - kpos)
        s_sel = s_sel + table_t[hi[..., None], bucket].astype(jnp.float32)
        s_sel = jnp.where(sel_valid[..., None], s_sel, NEG_BIG_2)
        ko = lax.dynamic_slice_in_dim(kp, own * MOBA_BLOCK, MOBA_BLOCK, axis=2)
        vo = lax.dynamic_slice_in_dim(vp, own * MOBA_BLOCK, MOBA_BLOCK, axis=2)
        kpos_own = own * MOBA_BLOCK + jnp.arange(MOBA_BLOCK)
        dist_own = tpos[:, None] - kpos_own[None, :]
        s_own = jnp.einsum('bhqd,bhkd->bhqk', qc, ko).astype(jnp.float32) * scale
        s_own = s_own + table_t[:, t5_bucket(dist_own)].astype(jnp.float32)[None]
        s_own = jnp.where(dist_own >= 0, s_own, NEG_BIG_2)
        logits = jnp.concatenate([s_sel.reshape(b, h, MOBA_Q_CHUNK, topk * MOBA_BLOCK), s_own], axis=-1)
        p = jax.nn.softmax(logits, axis=-1).astype(v.dtype)
        p_sel = p[..., :topk * MOBA_BLOCK].reshape(b, h, MOBA_Q_CHUNK, topk, MOBA_BLOCK)
        p_own = p[..., topk * MOBA_BLOCK:]
        return (jnp.einsum('bhqnk,bhqnkd->bhqd', p_sel, vs)
                + jnp.einsum('bhqk,bhkd->bhqd', p_own, vo))

    out = lax.map(chunk, jnp.arange(s_len // MOBA_Q_CHUNK))
    return out.transpose(1, 2, 0, 3, 4).reshape(b, h, s_len, d)

def dsa_attention(q, k, v, q_idx, k_idx, w_idx, bias_table):
    b, h, s_len, d = q.shape
    scale = HEAD_DIM ** -0.5
    ksel = min(DSA_TOPK, s_len // 4)
    table_t = bias_table.T
    bi = jnp.arange(b)[:, None, None]
    outs = []
    for i in range(s_len // Q_BLOCK):
        t0, t1 = i * Q_BLOCK, (i + 1) * Q_BLOCK
        kk = min(ksel, t1)
        tpos = jnp.arange(t0, t1)
        isc = jax.nn.relu(jnp.einsum('bqhe,bke->bqhk', q_idx[:, t0:t1], k_idx[:, :t1]))
        isc = jnp.einsum('bqh,bqhk->bqk', w_idx[:, t0:t1], isc).astype(jnp.float32)
        admissible = jnp.arange(t1)[None, :] <= tpos[:, None]
        _, idx = lax.top_k(jnp.where(admissible, isc, -jnp.inf), kk)
        dist = tpos[None, :, None] - idx
        ks = k[bi, idx]
        vs = v[bi, idx]
        logits = jnp.einsum('bhqd,bqkd->bhqk', q[:, :, t0:t1], ks).astype(jnp.float32) * scale
        logits = logits + table_t[:, t5_bucket(dist)].transpose(1, 0, 2, 3).astype(jnp.float32)
        logits = jnp.where((dist >= 0)[:, None], logits, NEG_BIG_2)
        p = jax.nn.softmax(logits, axis=-1).astype(v.dtype)
        outs.append(jnp.einsum('bhqk,bqkd->bhqd', p, vs))
    return jnp.concatenate(outs, axis=2)

def token_mixer(xn, w_in, fox_b_f, t5_bias, w_gate, w_branch, w_out):
    b, s_len, _ = xn.shape
    proj = xn @ w_in
    (sb_q, sb_k, sb_v, mb_q, mb_k, mb_v, fx_q, fx_k, fx_v, fx_f,
     ds_q, ds_k, ds_v, ix_q, ix_k, ix_w) = jnp.split(proj, IN_SPLITS_2, axis=-1)
    o_sb = stick_breaking_attention(to_heads(sb_q, N_SB), to_heads(sb_k, N_SB), to_heads(sb_v, N_SB))
    o_mb = moba_attention(to_heads(mb_q, N_MOBA), to_heads(mb_k, N_MOBA), to_heads(mb_v, N_MOBA),
                          t5_bias[:, :N_MOBA])
    o_fx = forgetting_attention(to_heads(fx_q, N_FOX), to_heads(fx_k, N_FOX), to_heads(fx_v, N_FOX),
                                fx_f + fox_b_f)
    o_ds = dsa_attention(to_heads(ds_q, N_DSA), ds_k, ds_v,
                         ix_q.reshape(b, s_len, IDX_HEADS, IDX_DIM), ix_k, ix_w, t5_bias[:, N_MOBA:])
    branches = (o_sb, o_mb, o_fx, o_ds)
    mixed = None
    for i in range(N_BRANCH_2):
        y = jax.nn.sigmoid(xn @ w_gate[i]) * (merge_heads(branches[i]) @ w_branch[i])
        mixed = y if mixed is None else mixed + y
    return mixed @ w_out

def conv_ffn(xn, w_up, conv_w, conv_b, w_down):
    s_len = xn.shape[1]
    hdn = xn @ w_up
    hp = jnp.pad(hdn, ((0, 0), (CONV_W_2 - 1, 0), (0, 0)))
    acc = conv_b
    for j in range(CONV_W_2):
        acc = acc + conv_w[j] * hp[:, j:j + s_len]
    g, u = jnp.split(acc, 2, axis=-1)
    return (jax.nn.gelu(g, approximate=False) * u) @ w_down

def second_inputs(seed: int = 0) -> dict:
    key = jax.random.key(seed)
    ks = jax.random.split(key, 14)
    nrm = jax.random.normal
    f32 = jnp.float32
    return {
        "x": nrm(ks[0], (BATCH, SEQ, D_MODEL), f32),
        "norm_mix_g": 1.0 + 0.02 * nrm(ks[1], (DEPTH_2, D_MODEL), f32),
        "norm_ffn_g": 1.0 + 0.02 * nrm(ks[2], (DEPTH_2, D_MODEL), f32),
        "norm_final_g": 1.0 + 0.02 * nrm(ks[3], (D_MODEL,), f32),
        "w_in": nrm(ks[4], (DEPTH_2, D_MODEL, P_IN), f32) * D_MODEL ** -0.5,
        "fox_b_f": 1.0 + 0.1 * nrm(ks[5], (DEPTH_2, N_FOX), f32),
        "t5_bias": 0.5 * nrm(ks[6], (T5_BUCKETS, N_MOBA + N_DSA), f32),
        "w_gate": nrm(ks[7], (DEPTH_2, N_BRANCH_2, D_MODEL, D_MODEL), f32) * D_MODEL ** -0.5,
        "w_branch": nrm(ks[8], (DEPTH_2, N_BRANCH_2, BRANCH_W, D_MODEL), f32) * BRANCH_W ** -0.5,
        "w_out": nrm(ks[9], (DEPTH_2, D_MODEL, D_MODEL), f32) * D_MODEL ** -0.5,
        "w_up": nrm(ks[10], (DEPTH_2, D_MODEL, 2 * D_FF_2), f32) * D_MODEL ** -0.5,
        "conv_w": nrm(ks[11], (DEPTH_2, CONV_W_2, 2 * D_FF_2), f32) * CONV_W_2 ** -0.5,
        "conv_b": 0.01 * nrm(ks[12], (DEPTH_2, 2 * D_FF_2), f32),
        "w_down": nrm(ks[13], (DEPTH_2, D_FF_2, D_MODEL), f32) * D_FF_2 ** -0.5,
    }

def second_block(x, norm_mix_g, norm_ffn_g, norm_final_g, w_in, fox_b_f, t5_bias,
              w_gate, w_branch, w_out, w_up, conv_w, conv_b, w_down):
    for l in range(DEPTH_2):
        x = x + token_mixer(rmsnorm(x, norm_mix_g[l]), w_in[l], fox_b_f[l], t5_bias,
                            w_gate[l], w_branch[l], w_out[l])
        x = x + conv_ffn(rmsnorm(x, norm_ffn_g[l]), w_up[l], conv_w[l], conv_b[l], w_down[l])
    return rmsnorm(x, norm_final_g)


def setup_inputs(seed=0):
    out = dict(first_inputs(seed))
    for name, value in second_inputs(seed + 1).items():
        if name != "x":
            out[name + "_2"] = value
    return out


def reference(
    x, mem, norm_mix_pre, norm_mix_post, norm_mlp_pre, norm_mlp_post, norm_mem, w_in, b_gate,
    lambda_q1, lambda_k1, lambda_q2, lambda_k2, diff_subln, conv_w, conv_b, rg_wa, rg_ba, rg_wi,
    rg_bi, rg_lambda, w_kv_mem, w_proj_attn, w_proj_lru, w_proj_mem, w_out, w_mlp_up,
    w_mlp_down, norm_mix_g_2, norm_ffn_g_2, norm_final_g_2, w_in_2, fox_b_f_2, t5_bias_2,
    w_gate_2, w_branch_2, w_out_2, w_up_2, conv_w_2, conv_b_2, w_down_2,
):
    x = first_block(
        x, mem, norm_mix_pre, norm_mix_post, norm_mlp_pre, norm_mlp_post, norm_mem, w_in,
        b_gate, lambda_q1, lambda_k1, lambda_q2, lambda_k2, diff_subln, conv_w, conv_b, rg_wa,
        rg_ba, rg_wi, rg_bi, rg_lambda, w_kv_mem, w_proj_attn, w_proj_lru, w_proj_mem, w_out,
        w_mlp_up, w_mlp_down,
    )
    return second_block(
        x, norm_mix_g_2, norm_ffn_g_2, norm_final_g_2, w_in_2, fox_b_f_2, t5_bias_2, w_gate_2,
        w_branch_2, w_out_2, w_up_2, conv_w_2, conv_b_2, w_down_2,
    )


_drawn_inputs = setup_inputs


def setup_inputs(seed=0):
    import zlib

    import numpy as np

    out = dict(_drawn_inputs(seed))
    spreads = {}
    factors = {'norm_mem': 5.793,
     'rg_ba': 5.621,
     'rg_bi': 2.695,
     'norm_mix_g_2': 6.228,
     'norm_ffn_g_2': 7.435,
     'norm_final_g_2': 8.051,
     'fox_b_f_2': 8.0,
     'conv_b_2': 28.933}
    for name, (base, spread) in spreads.items():
        noise = np.random.default_rng([zlib.crc32(name.encode()), seed]).standard_normal(out[name].shape)
        drawn = base * np.exp(spread * noise) if base else spread * noise
        out[name] = __import__('jax').numpy.asarray(drawn.astype(out[name].dtype))
    for name, factor in factors.items():
        out[name] = (out[name] * factor).astype(out[name].dtype)
    return out
```

```python
import math
from contextlib import ExitStack

import numpy as np

import concourse.bass as bass
from concourse import mybir
from concourse.alu_op_type import AluOpType as ALU

ACT = mybir.ActivationFunctionType
AX = mybir.AxisListType
F32 = mybir.dt.float32
F32R = mybir.dt.float32r
BF16 = mybir.dt.bfloat16

P = 128
D = 1024
S = 256
DEPTH = 2
KC = D // P
TB = S // P
EPS = 1e-6
NEG = -1e30
TILE = 2048
RAW, HI, LO = 4, 4, 2

A_HEADS, A_HD = 8, 64
X_HEADS, X_HD = 4, 256
A_FF = 4 * D
A_UP = A_FF // 256
B_FF = 2816
B_UP = B_FF // 256
B_HD = 64
B_TOPK = min(256, S // 4)
IDX_HEADS, IDX_HD = 8, 32
REPLACED = -3e38
OUTSIDE = -1e38

T_K, T_V, T_XQ, T_QK, T_AV, T_ZX, T_ZY = 0, 4, 8, 12, 20, 24, 28
T_GM, T_PM, T_GA, T_PA, T_GL, T_PL, T_OUT = 32, 36, 40, 44, 48, 52, 56
T_UP = 60
A_TILES = T_UP + 2 * A_UP
N_FEAT, N_TOK = 9, 4
T2_TOK = N_FEAT
T2_GATE = T2_TOK + N_TOK
T2_OUT = T2_GATE + 4 * 5
T2_FFN = T2_OUT + 4
B_TILES = T2_FFN + 3 * B_UP
N_TILES = DEPTH * A_TILES + B_TILES
SKEW = 3 * P
assert A_TILES % RAW == 0 and N_TILES % 2 == 0

_ACT_TILES = [t for t in range(T_UP) if not (T_QK <= t < T_AV or T_PM <= t < T_GA or T_PA <= t < T_GL or T_PL <= t < T_OUT)]
_DVE_TILES = [t for t in range(T_UP) if t not in _ACT_TILES]
ACT_EVAC = {t: n + 1 for n, t in enumerate(_ACT_TILES)}
DVE_EVAC = {t: n + 1 for n, t in enumerate(_DVE_TILES)}
N_ACT_EVAC, N_DVE_EVAC = len(_ACT_TILES), len(_DVE_TILES)

def _columns(*sizes):
    at, out = 0, {}
    for name, n in sizes:
        out[name] = at
        at += n
    return out, at


PA, _na = _columns(("mix_pre", 8), ("mlp_pre", 8), ("mem", 8), ("b_gate", 24), ("conv_w", 32), ("conv_b", 8),
                   ("rg_ba", 8), ("rg_bi", 8), ("rg_lambda", 8), ("subln", 1), ("one_minus_init", 1), ("init", 1),
                   ("lambda_q", 128), ("lambda_k", 128))
PB, _nb = _columns(("mix", 8), ("ffn", 8), ("fox_b", 4), ("conv_w", 3 * 4 * B_UP), ("conv_b", 4 * B_UP))
N_PAR = max(_na, _nb)

DVE_STEPS, ACT_STEPS = 53, 1


def build(nc, stream, x_in, mem_in, params, post_gain, rg_w, cos_in, sin_in, ident_in, masks_in, t5_in,
          final_gain, out):
    t5_rows = nc.dram_tensor("t5_rows", (8, 512), F32, kind="Internal").ap()
    t5_skewed = nc.dram_tensor("t5_skewed", (8, P, SKEW + 1), F32, kind="Internal").ap()
    with ExitStack() as ctx:
        def sb(name, shape, dt=F32):
            return ctx.enter_context(nc.sbuf_tensor(name, shape, dt))

        def sem(name):
            return ctx.enter_context(nc.semaphore(name))

        w_raw = sb("w_raw", [P, RAW, TILE])
        w_hi = sb("w_hi", [P, HI, TILE], F32R)
        w_lo = sb("w_lo", [P, LO, TILE], F32R)
        raw_loaded = [sem(f"raw_loaded{s}") for s in range(RAW)]
        hi_ready = sem("hi_ready")
        lo_ready = sem("lo_ready")
        tile_done = sem("tile_done")

        x = sb("x", [P, TB, D])
        op_hi = [sb("opA_hi", [P, KC, S], F32R), sb("opB_hi", [P, KC, S], F32R)]
        op_lo = [sb("opA_lo", [P, KC, S], F32R), sb("opB_lo", [P, KC, S], F32R)]
        B = [sb(f"B{n}", [P, 2080 if n == 0 else 2048]) for n in range(7)]
        merged = sb("merged", [P, 2048])
        gate = sb("gate", [P, 2048])
        expd = sb("expd", [P, 4, 256])
        probs_t = sb("probs_t", [P, 512])
        par = sb("par", [P, N_PAR])
        cos = sb("cos", [P, TB, 32])
        sin = sb("sin", [P, TB, 32])
        ident = sb("ident", [P, P])
        small = sb("small", [P, 96])
        rowmask = sb("rowmask", [P, P], BF16)
        colmask = sb("colmask", [P, 64], BF16)
        psum = ctx.enter_context(nc.psum_tensor("psum", [P, 8, 512], F32))

        def tok(buf):
            return buf[:, 0:2048].rearrange("p (b f) -> p b f", b=TB)

        def feat(buf):
            return buf[:, 0:2048].rearrange("p (c t) -> p c t", c=KC)

        k_mem, v_mem, q_t, k_t, v_a, q_mem, o_a = feat(B[0]), tok(B[1]), feat(B[2]), feat(B[3]), tok(B[4]), feat(B[5]), tok(B[6])
        zx = B[0][:, :].rearrange("p (c t) -> p c t", c=KC)
        xc, gz = feat(B[1]), feat(B[5])
        r_g, i_g, t_g, lru = feat(B[2]), feat(B[3]), feat(B[4]), feat(B[6])
        rgw = B[0][:, 0:2048].rearrange("p (g c d) -> p g c d", g=2, c=KC)
        y_tok = tok(B[1])
        gains = tok(B[4])
        relu_u, squared = B[2][:, 0:1024].rearrange("p (b n) -> p b n", b=2), B[3][:, 0:1024].rearrange("p (b n) -> p b n", b=2)
        rot = merged[:, 0:1024].rearrange("p (b n) -> p b n", b=2)
        rope_a, rope_b = gate[:, 0:512], gate[:, 512:1024]

        def sm(a, n=1):
            return small[:, a:a + n]
        SS, VAR, SD, RS, NMAX, ZSUM, RZ, R2 = 0, 16, 32, 48, 64, 68, 72, 76
        NLAM, GSUB, SP_POS, SP_NEG = 78, 79, 80, 88
        prep = sb("prep", [P, 160])

        consts_in, par_in, mem_in_sem, rgw_in, gain_in, out_done = (sem(n) for n in (
            "consts_in", "par_in", "mem_loaded", "rgw_in", "gain_in", "out_done"))
        layer_end = sem("layer_end")
        norm_ss, norm_var, norm_sd, norm_x = (sem(n) for n in ("norm_ss", "norm_var", "norm_sd", "norm_x"))
        turned = sem("turned")
        op_hi_done = sem("op_hi_done")
        op_ready = sem("op_ready")
        act_evac, dve_evac = sem("act_evac"), sem("dve_evac")
        par_d, par_a = sem("par_d"), sem("par_a")
        rope_turned, rope_evac, rope_ready = sem("rope_turned"), sem("rope_evac"), sem("rope_ready")
        x_scores, x_max, x_exp, x_probs, x_turned, x_pt, x_out = (sem("x_" + n) for n in (
            "scores", "max", "exp", "probs", "turned", "pt", "out"))
        d_scores, d_max, d_exp, d_probs, d_turned, d_pt, d_out, d_kept = (sem("d_" + n) for n in (
            "scores", "max", "exp", "probs", "turned", "pt", "out", "kept"))
        conv_done, rg_done, rg_evac, lru_ta, lru_v, lru_s, lru_y, gelu_done = (sem(n) for n in (
            "conv_done", "rg_done", "rg_evac", "lru_ta", "lru_v", "lru_s", "lru_y", "gelu_done"))
        lru_u = sem("lru_u")
        masks_ready = sem("masks_ready")
        post_ss, post_var, post_sd = (sem(n) for n in ("post_ss", "post_var", "post_sd"))
        x_ready = sem("x_ready")
        squared_done, ffn_hi = sem("squared_done"), sem("ffn_hi")
        zx_padded = sem("zx_padded")
        mem_gate, merged_part = sem("mem_gate"), sem("merged_part")
        relu_done, up_used, ffn_ready, ffn_used = sem("relu_done"), sem("up_used"), sem("ffn_ready"), sem("ffn_used")
        dve_step, act_step = sem("dve_step"), sem("act_step")

        MEM_OP, MIX_OP, X_OP, SUB_OP, LRU_OP, OUT_OP, MLP_OP, N_OPS = 1, 2, 3, 7, 8, 9, 10, 10
        TURNS = 4 * 4

        f_b = [feat(B[0])[:, c, :] for c in range(8)] + [feat(B[1])[:, c, :] for c in range(8)] \
            + [B[2][:, c * S:(c + 1) * S] for c in range(2)]
        SB_Q, SB_K, MB_Q, MB_K, FX_Q, FX_K, DS_Q, DS_K, IX_K, IX_Q = 0, 2, 4, 6, 8, 10, 12, 14, 15, 16
        v_b = tok(B[3])
        V_COL, W_COL, F_COL = (0, 256, 512, 768), 832, 840
        bias_b = [B[4 + h // 4][:, (h % 4) * 512:(h % 4 + 1) * 512].rearrange("p (b n) -> p b n", b=TB) for h in range(8)]
        index = B[2][:, 512:1024].rearrange("p (b n) -> p b n", b=TB)
        minus_c_row = B[2][:, 1024:2048].rearrange("p (h n) -> p h n", h=4)
        log_f_wide = merged[:, 0:1024].rearrange("p (a n) -> p a n", n=P)
        up_to, ones_p, neg_from, neg_all, before01, before_neg, causal = (
            B[6][:, n * P:(n + 1) * P] for n in range(7))
        log_f, c_col = prep[:, 16:24], prep[:, 24:32]
        padded = B[0][:, 0:2064].rearrange("p (s c t) -> p s c t", s=2, c=4)
        conved = B[1][:, 0:2048].rearrange("p (s c t) -> p s c t", s=2, c=4)
        gelu_g = B[2][:, 0:1024].rearrange("p (s n) -> p s n", s=2)
        gated = B[3][:, 0:1024].rearrange("p (s n) -> p s n", s=2)

        (t5_loaded, t5_rows_ready, t5_evac, t5_stored, t5_skewed_in, bias_in, b_masks_in, final_in) = (sem(n) for n in (
            "t5_loaded", "t5_rows_ready", "t5_evac", "t5_stored", "t5_skewed_in", "bias_in", "b_masks_in", "final_in"))
        b_ss, b_var, b_sd, b_x, b_turned, b_hi, b_ready = (sem("b_" + n) for n in (
            "ss", "var", "sd", "x", "turned", "hi", "ready"))
        b_evac_a, b_evac_d = sem("b_evac_a"), sem("b_evac_d")
        ix_scores, ix_relu, ix_added = sem("ix_scores"), sem("ix_relu"), sem("ix_added")
        f_in, f_ln, f_wide, c_sums, c_kept = (sem(n) for n in ("f_in", "f_ln", "f_wide", "c_sums", "c_kept"))
        sb_z, sb_ln, sb_masked, sb_summed, sb_w = (sem("sb_" + n) for n in ("z", "ln", "masked", "summed", "w"))
        s_scores, s_max, s_exp, s_probs, s_turned, s_pt = (sem("s_" + n) for n in (
            "scores", "max", "exp", "probs", "turned", "pt"))
        b_out = sem("b_out")
        b_mixed = sem("b_mixed")
        out_part, x_b = sem("out_part"), sem("x_b")
        pads_zero = sem("pads_zero")
        f_evac, f_conv, f_gelu, f_gated, f_hi, f_ready = (sem("f_" + n) for n in ("evac", "conv", "gelu", "gated", "hi", "ready"))
        b_step = sem("b_step")

        class Steps:
            def __init__(self, eng, s, per_layer):
                self.eng, self.s, self.per_layer, self.base, self.n = eng, s, per_layer, 0, 0

            def __call__(self, ins):
                ins.then_inc(self.s, 1)
                self.n += 1
                self.eng.wait_ge(self.s, self.base + self.n)

        block = ctx.enter_context(nc.Block())

        @block.sync
        def _(sp):
            for s in range(RAW):
                sp.dma_start(w_raw[:, s, :], stream[s]).then_inc(raw_loaded[s], 16)
            sp.wait_ge(t5_evac, 1)
            sp.dma_start(t5_rows, B[1][0:8, 1024:1536]).then_inc(t5_stored, 16)
            sp.wait_ge(t5_stored, 16)
            for h in range(8):
                row = bass.AP(tensor=t5_rows.tensor, offset=t5_rows.offset + h * 512, ap=[[0, P], [1, SKEW]])
                sp.dma_start(t5_skewed[h, :, 0:SKEW], row).then_inc(t5_skewed_in, 16)
            groups = N_TILES // RAW
            with sp.Fori(1, groups) as g:
                for s in range(RAW):
                    sp.wait_ge(lo_ready, g * RAW + (s - RAW + 1))
                    sp.dma_start(w_raw[:, s, :], stream[g * RAW + s]).then_inc(raw_loaded[s], 16)
            for t in range(groups * RAW, N_TILES):
                sp.wait_ge(lo_ready, t - RAW + 1)
                sp.dma_start(w_raw[:, t % RAW, :], stream[t]).then_inc(raw_loaded[t % RAW], 16)
            sp.wait_ge(out_done, 16)

        @block.gpsimd
        def _(pool):
            def rest(t, s, first=False):
                pool.wait_ge(hi_ready, t + 1)
                if not first:
                    pool.wait_ge(tile_done, t - (LO - 1))
                nc.gpsimd.tensor_tensor(w_lo[:, s % LO, :], w_raw[:, s % RAW, :], w_hi[:, s % HI, :].bitcast(F32),
                                        ALU.subtract).then_inc(lo_ready, 1)

            for t in range(4):
                rest(t, t, t < LO)
            with pool.Fori(1, N_TILES // 4) as g:
                for s in range(4):
                    rest(g * 4 + s, s)
            for t in range(N_TILES // 4 * 4, N_TILES):
                rest(t, t)

        @block.tensor
        def _(pe):
            def passes(t, s, product):
                pe.wait_ge(hi_ready, t + 1)
                product(w_hi[:, s % HI, :], 0, True, False)
                product(w_hi[:, s % HI, :], 1, False, False)
                pe.wait_ge(lo_ready, t + 1)
                product(w_lo[:, s % LO, :], 0, False, True).then_inc(tile_done, 1)

            def col_feat(t, s, bank, op):
                parts = (op_hi[op], op_lo[op])

                def product(w, a, first, last):
                    w = w.rearrange("p (k n) -> p k n", k=KC)
                    for c in range(2):
                        for k in range(KC):
                            ins = nc.tensor.matmul(psum[:, bank, c * S:(c + 1) * S], w[:, k, c * P:(c + 1) * P],
                                                   parts[a][:, k, :], start=(first and c == 0 and k == 0),
                                                   stop=(last and k == KC - 1), skip_group_check=True)
                    return ins
                passes(t, s, product)

            def col_tok(t, s, bank, op):
                parts = (op_hi[op], op_lo[op])

                def product(w, a, first, last):
                    w = w.rearrange("p (k n) -> p k n", k=KC)
                    for b in range(TB):
                        for k in range(KC):
                            ins = nc.tensor.matmul(psum[:, bank, b * 256:(b + 1) * 256], parts[a][:, k, b * P:(b + 1) * P],
                                                   w[:, k, :], start=(first and b == 0 and k == 0),
                                                   stop=(last and k == KC - 1), skip_group_check=True)
                    return ins
                passes(t, s, product)

            def row_tok(t, s, slot, first_tile, last_tile):
                parts = (op_hi[1], op_lo[1])

                def product(w, a, first, last):
                    w = w.rearrange("p (k n) -> p k n", k=2)
                    for b in range(TB):
                        for n in range(2):
                            for k in range(2):
                                ins = nc.tensor.matmul(psum[:, 4 + 2 * b + n, :], parts[a][:, 2 * slot + k, b * P:(b + 1) * P],
                                                       w[:, k, n * 512:(n + 1) * 512], start=(first_tile and first and k == 0),
                                                       stop=(last_tile and last and k == 1), skip_group_check=True)
                    return ins
                passes(t, s, product)

            def turn(src, bank0):
                for c in range(KC):
                    for b in range(TB):
                        ins = nc.tensor.transpose(psum[:, bank0 + c // 2, (c % 2) * S + b * P:(c % 2) * S + (b + 1) * P],
                                                  src[:, b, c * P:(c + 1) * P], ident[:])
                    if c % 2:
                        ins.then_inc(turned, 1)

            pe.wait_ge(consts_in, 16 * 4)
            pe.wait_ge(masks_ready, 3)
            pe.wait_ge(t5_loaded, 16)
            nc.tensor.matmul(psum[0:8, 4, :], B[1][0:33, 512:520], B[1][0:33, 0:512], start=True, stop=True).then_inc(t5_rows_ready, 1)
            pe.wait_ge(t5_evac, 1)
            with pe.Fori(0, DEPTH) as l:
                T = l * A_TILES
                OP = l * N_OPS

                def tile(t, product, op):
                    if t >= 4:
                        if t - 4 in ACT_EVAC:
                            pe.wait_ge(act_evac, l * N_ACT_EVAC + ACT_EVAC[t - 4])
                        else:
                            pe.wait_ge(dve_evac, l * N_DVE_EVAC + DVE_EVAC[t - 4])
                    product(T + t, t, t % 4, op)

                pe.wait_ge(norm_x, l * 4 + 1)
                turn(tok(B[6]), 0)
                pe.wait_ge(op_ready, OP + MEM_OP)
                tile(0, col_feat, 1)
                tile(1, col_feat, 1)
                pe.wait_ge(norm_x, l * 4 + 2)
                turn(tok(gate), 4)
                tile(2, col_feat, 1)
                tile(3, col_feat, 1)
                for t in range(T_V, T_XQ):
                    tile(t, col_tok, 1)
                pe.wait_ge(op_ready, OP + MIX_OP)
                for t in range(T_XQ, T_QK):
                    tile(t, col_feat, 0)

                def rope_turn(i):
                    pe.wait_ge(rope_ready, l * 8 + i + 1)
                    if i:
                        pe.wait_ge(rope_evac, l * 8 + i)
                    for c in range(2):
                        for b in range(TB):
                            ins = nc.tensor.transpose(psum[:, 5, c * S + b * P:c * S + (b + 1) * P],
                                                      rot[:, i % 2, b * 256 + c * P:b * 256 + (c + 1) * P], ident[:])
                    ins.then_inc(rope_turned, 1)

                def x_score(h):
                    pe.wait_ge(act_evac, l * N_ACT_EVAC + ACT_EVAC[T_XQ + 3])
                    for b in range(TB):
                        for k in range(2):
                            ins = nc.tensor.matmul(psum[:, 4, b * 256:(b + 1) * 256], q_mem[:, 2 * h + k, b * P:(b + 1) * P],
                                                   k_mem[:, 2 * h + k, :], start=(k == 0), stop=(k == 1))
                    ins.then_inc(x_scores, 1)

                def x_turn(h):
                    pe.wait_ge(x_probs, l * X_HEADS + h + 1)
                    for k in range(TB):
                        for b in range(TB):
                            ins = nc.tensor.transpose(psum[:, 6, k * 256 + b * P:k * 256 + (b + 1) * P],
                                                      expd[:, b, k * P:(k + 1) * P], ident[:])
                    ins.then_inc(x_turned, 1)

                def x_values(h):
                    pe.wait_ge(x_pt, l * X_HEADS + h + 1)
                    if h:
                        pe.wait_ge(op_ready, OP + X_OP + h - 1)
                    for c in range(2):
                        for k in range(TB):
                            ins = nc.tensor.matmul(psum[:, 7, c * S:(c + 1) * S], v_mem[:, k, h * X_HD + c * P:h * X_HD + (c + 1) * P],
                                                   probs_t[:, k * 256:(k + 1) * 256], start=(k == 0), stop=(k == 1))
                    ins.then_inc(x_out, 1)

                for i in range(8):
                    tile(T_QK + i, col_tok, 0)
                    if i:
                        rope_turn(i - 1)
                    if i % 2 == 0:
                        if i:
                            x_values(i // 2 - 1)
                        x_score(i // 2)
                    else:
                        x_turn(i // 2)
                tile(T_AV, col_tok, 0)
                rope_turn(7)
                x_values(3)
                for t in range(T_AV + 1, T_ZX):
                    tile(t, col_tok, 0)

                def d_score(h):
                    if h == 0:
                        pe.wait_ge(rope_evac, l * 8 + 8)
                    for m in range(2):
                        q = slice(64 * m, 64 * m + 64)
                        for b in range(TB):
                            n = (b + 1) * P
                            nc.tensor.matmul(psum[:, 4 + m, b * 256:b * 256 + n], q_t[q, h, b * P:(b + 1) * P], k_t[q, h, 0:n],
                                             start=True, stop=False, skip_group_check=True)
                            ins = nc.tensor.matmul(psum[:, 4 + m, b * 256 + n - 64:b * 256 + n], rowmask[64 * m:64 * m + 1, :],
                                                   colmask[64 * m:64 * m + 1, :], start=False, stop=True, skip_group_check=True)
                    ins.then_inc(d_scores, 1)

                def d_turn(h):
                    pe.wait_ge(d_probs, l * A_HEADS + h + 1)
                    for b in range(TB):
                        nc.tensor.transpose(psum[:, 6, b * P:(b + 1) * P], expd[:, b, 0:P], ident[:])
                    nc.tensor.transpose(psum[:, 6, 256:384], expd[:, 1, P:2 * P], ident[:]).then_inc(d_turned, 1)

                def d_values(h):
                    pe.wait_ge(d_pt, l * A_HEADS + h + 1)
                    pe.wait_ge(act_evac, l * N_ACT_EVAC + ACT_EVAC[T_AV + 3])
                    if h:
                        pe.wait_ge(d_kept, l * A_HEADS + h)
                    v = slice(h * P, (h + 1) * P)
                    nc.tensor.matmul(psum[:, 7, 0:P], probs_t[:, 0:P], v_a[:, 0, v], start=True, stop=True)
                    nc.tensor.matmul(psum[:, 7, P:2 * P], probs_t[:, P:2 * P], v_a[:, 0, v], start=True, stop=False)
                    nc.tensor.matmul(psum[:, 7, P:2 * P], probs_t[:, 256:384], v_a[:, 1, v], start=False, stop=True).then_inc(d_out, 1)

                for h in range(A_HEADS):
                    t = T_ZX + 2 * h
                    d_score(h)
                    if t == T_PM:
                        pe.wait_ge(op_ready, OP + X_OP + 3)
                    tile(t, col_feat, 1 if t >= T_PM else 0)
                    d_turn(h)
                    tile(t + 1, col_feat, 1 if t >= T_PM else 0)
                    d_values(h)

                def rg(c):
                    if c == 0:
                        pe.wait_ge(rgw_in, l * 16 + 16)
                    if c == 3:
                        pe.wait_ge(d_kept, l * A_HEADS + A_HEADS)
                    if c >= 4:
                        pe.wait_ge(rg_evac, l * KC + c - 3)
                    for g in range(2):
                        ins = nc.tensor.matmul(psum[:, 4 + c % 4, g * S:(g + 1) * S], rgw[:, g, c, :], xc[:, c, :], start=True, stop=True)
                    ins.then_inc(rg_done, 1)

                for n in range(2):
                    tile(T_GA + n, col_feat, 0)
                    for c in range(4):
                        rg(4 * n + c)
                tile(T_GA + 2, col_feat, 0)
                pe.wait_ge(norm_x, l * 4 + 3)
                pe.wait_ge(rg_evac, l * KC + KC)
                turn(tok(B[6]), 4)
                tile(T_GA + 3, col_feat, 0)
                pe.wait_ge(op_ready, OP + SUB_OP)
                for t in range(T_PA, T_GL):
                    tile(t, col_feat, 1)
                for t in range(T_GL, T_PL):
                    tile(t, col_feat, 0)
                pe.wait_ge(op_ready, OP + LRU_OP)
                for t in range(T_PL, T_OUT):
                    tile(t, col_feat, 1)
                pe.wait_ge(op_ready, OP + OUT_OP)
                for t in range(T_OUT, T_UP):
                    tile(t, col_tok, 0)

                pe.wait_ge(norm_x, l * 4 + 4)
                turn(tok(gate), 4)
                pe.wait_ge(op_ready, OP + MLP_OP)

                def up(j, t, s, slot, first=False):
                    if not first:
                        pe.wait_ge(relu_done, l * A_UP + j - 1)
                    col_feat(T + t, s, slot, 0)

                def down(j, t, s, slot, first, last):
                    pe.wait_ge(ffn_ready, l * A_UP + j + 1)
                    row_tok(T + t, s, slot, first, last)

                up(0, T_UP, T_UP, 0, True)
                up(1, T_UP + 1, T_UP + 1, 1, True)
                down(0, T_UP + 2, T_UP + 2, 0, True, False)
                with pe.Fori(0, A_UP // 2 - 1) as i:
                    t0 = T_UP + 3
                    up(i * 2 + 2, i * 4 + t0, t0, 0)
                    down(i * 2 + 1, i * 4 + t0 + 1, t0 + 1, 1, False, False)
                    up(i * 2 + 3, i * 4 + t0 + 2, t0 + 2, 1)
                    down(i * 2 + 2, i * 4 + t0 + 3, t0 + 3, 0, False, False)
                down(A_UP - 1, A_TILES - 1, A_TILES - 1, 1, False, True)

            T0 = DEPTH * A_TILES

            def row_feat(t, s):
                parts = (op_hi[1], op_lo[1])

                def product(w, a, first, last):
                    w = w.rearrange("p (k n) -> p k n", k=2)
                    for c in range(KC):
                        for k in range(2):
                            ins = nc.tensor.matmul(psum[:, c // 2, (c % 2) * S:(c % 2 + 1) * S], w[:, k, c * P:(c + 1) * P],
                                                   parts[a][:, k, :], start=(first and c % 2 == 0 and k == 0),
                                                   stop=(last and k == 1), skip_group_check=True)
                    return ins
                passes(t, s, product)

            def turn_b():
                for c in range(KC):
                    for b in range(TB):
                        ins = nc.tensor.transpose(psum[:, 4 + c // 2, (c % 2) * S + b * P:(c % 2) * S + (b + 1) * P],
                                                  tok(gate)[:, b, c * P:(c + 1) * P], ident[:])
                    if c % 2:
                        ins.then_inc(b_turned, 1)

            pe.wait_ge(b_x, 1)
            turn_b()
            pe.wait_ge(b_ready, 1)
            for t in range(N_FEAT + N_TOK):
                if t >= 4:
                    pe.wait_ge(b_evac_a, t - 3)
                (col_feat if t < N_FEAT else col_tok)(T0 + t, t, t % 4, 0)

            def gate_tile(b, n):
                t = T2_GATE + 5 * b + n
                if b == 0:
                    pe.wait_ge(b_evac_a, N_FEAT + N_TOK)
                else:
                    pe.wait_ge(b_evac_d, 4 * (b - 1) + n + 1)
                col_feat(T0 + t, t, n, 0)

            def index_scores(h):
                if h >= 4:
                    pe.wait_ge(ix_relu, h - 3)
                r = slice(32 * (h % 4), 32 * (h % 4) + 32)
                for b in range(TB):
                    ins = nc.tensor.matmul(psum[:, 4 + h % 4, b * 256:b * 256 + (b + 1) * P], f_b[IX_Q + h // 4][r, b * P:(b + 1) * P],
                                           f_b[IX_K][r, 0:(b + 1) * P], start=True, stop=True)
                ins.then_inc(ix_scores, 1)

            pe.wait_ge(b_evac_a, N_FEAT + N_TOK)
            pe.wait_ge(b_masks_in, 16)
            for h in range(4):
                index_scores(h)
            gate_tile(0, 0)
            for h in range(4, IDX_HEADS):
                index_scores(h)
            pe.wait_ge(ix_relu, IDX_HEADS)
            pe.wait_ge(f_wide, 1)
            nc.tensor.matmul(psum[:, 4, 0:4], up_to, log_f[:, 0:4], start=True, stop=True)
            nc.tensor.matmul(psum[:, 4, 4:8], ones_p, log_f[:, 0:4], start=True, stop=False)
            nc.tensor.matmul(psum[:, 4, 4:8], up_to, log_f[:, 4:8], start=False, stop=True)
            for h in range(4):
                row = psum[:, 5 + h // 2, (h % 2) * S:(h % 2 + 1) * S]
                nc.tensor.matmul(row, log_f_wide[:, h, :], B[6][:, 0:2 * P], start=True, stop=False)
                ins = nc.tensor.matmul(row[:, P:2 * P], log_f_wide[:, 4 + h, :], up_to, start=False, stop=True)
            ins.then_inc(c_sums, 1)
            pe.wait_ge(c_kept, 2)

            def rows_of(h):
                return slice(64 * (h % 2), 64 * (h % 2) + 64)

            def values(b, h):
                if h == 0 and b:
                    pe.wait_ge(b_ready, 1 + b)
                col = V_COL[b] + (64 * h if b < 3 else 0)
                o = psum[rows_of(h), 7, (h // 2) * S:(h // 2 + 1) * S]
                nc.tensor.matmul(o, v_b[:, 0, col:col + 64], probs_t[:, 0:256], start=True, stop=False, skip_group_check=True)
                nc.tensor.matmul(o[:, P:2 * P], v_b[:, 1, col:col + 64], probs_t[:, 256:384], start=False, stop=True,
                                 skip_group_check=True).then_inc(b_out, 1)

            def sb_logits(h):
                r = rows_of(h)
                k, q = f_b[SB_K + h // 2], f_b[SB_Q + h // 2]
                nc.tensor.matmul(psum[:, 4 + h % 2, 0:256], k[r, 0:P], q[r, :], start=True, stop=False, skip_group_check=True)
                nc.tensor.matmul(psum[:, 4 + h % 2, 256:384], k[r, P:2 * P], q[r, P:2 * P], start=False, stop=False,
                                 skip_group_check=True).then_inc(sb_z, 1)

            def sb_sums(h):
                pe.wait_ge(sb_masked, h + 1)
                m = expd[:, 2 * (h % 2):2 * (h % 2) + 2, :].rearrange("p a n -> p (a n)")
                z = psum[:, 4 + h % 2, :]
                for dst, w, src in ((z[:, 0:P], ident[:], before_neg), (z[:, 256:384], ident[:], before_neg),
                                    (z[:, 0:256], neg_from, m[:, 0:256]), (z[:, P:256], neg_all, m[:, 256:384]),
                                    (z[:, 256:384], neg_from, m[:, 256:384])):
                    ins = nc.tensor.matmul(dst, w, src, start=False, stop=True, skip_group_check=True)
                ins.then_inc(sb_summed, 1)

            sb_logits(0)
            for h in range(4):
                if h < 3:
                    gate_tile(0, h + 1)
                sb_sums(h)
                if h < 3:
                    sb_logits(h + 1)
                pe.wait_ge(sb_w, h + 1)
                values(0, h)

            def s_score(b, h):
                g = 4 * (b - 1) + h
                if g >= 2:
                    pe.wait_ge(s_probs, g - 1)
                r = rows_of(h)
                q = f_b[(None, MB_Q, FX_Q, DS_Q)[b] + h // 2]
                k = f_b[DS_K] if b == 3 else f_b[(None, MB_K, FX_K)[b] + h // 2]
                for u in range(TB):
                    ins = nc.tensor.matmul(psum[:, 4 + h % 2, u * 256:u * 256 + (u + 1) * P], q[r, u * P:(u + 1) * P],
                                           k[r, 0:(u + 1) * P], start=True, stop=True)
                ins.then_inc(s_scores, 1)

            def s_turn(b, h):
                g = 4 * (b - 1) + h
                pe.wait_ge(s_probs, g + 1)
                e = 2 * (h % 2)
                for u in range(TB):
                    nc.tensor.transpose(psum[:, 6, u * P:(u + 1) * P], expd[:, e + u, 0:P], ident[:])
                nc.tensor.transpose(psum[:, 6, 256:384], expd[:, e + 1, P:2 * P], ident[:]).then_inc(s_turned, 1)

            def branch_product(b):
                pe.wait_ge(b_evac_a, N_FEAT + N_TOK + 4 * (b + 1))
                if b:
                    pe.wait_ge(b_evac_d, 4 * b)
                pe.wait_ge(b_ready, 2 + b)
                t = T2_GATE + 5 * b + 4
                row_feat(T0 + t, t)

            for b in range(1, 4):
                s_score(b, 0)
                branch_product(b - 1)
                for h in range(4):
                    gate_tile(b, h)
                    s_turn(b, h)
                    if h < 3:
                        s_score(b, h + 1)
                    pe.wait_ge(s_pt, 4 * (b - 1) + h + 1)
                    values(b, h)
            branch_product(3)

            pe.wait_ge(b_ready, 6)
            for n in range(4):
                pe.wait_ge(b_evac_d, 12 + n + 1)
                t = T2_OUT + n
                col_tok(T0 + t, t, n, 0)

            pe.wait_ge(b_x, 2)
            turn_b()
            pe.wait_ge(b_ready, 7)

            def f_up(j):
                t = T2_FFN + (0 if j == 0 else 2 + 3 * (j - 1))
                for n in range(2):
                    if j >= 2:
                        pe.wait_ge(f_evac, 2 * (j - 2) + n + 1)
                    col_feat(T0 + t + n, t + n, 2 * (j % 2) + n, 0)

            def f_down(j):
                t = T2_FFN + 3 * (j + 1) + 1 if j < B_UP - 1 else B_TILES - 1
                pe.wait_ge(f_ready, j + 1)
                row_tok(T0 + t, t, j % 2, j == 0, j == B_UP - 1)

            f_up(0)
            for j in range(1, B_UP):
                f_up(j)
                f_down(j - 1)
            f_down(B_UP - 1)

        @block.scalar
        def _(act):
            for dst, src in ((ident, ident_in), (cos, cos_in), (sin, sin_in), (x, x_in)):
                act.dma_start(dst[:], src).then_inc(consts_in, 16)
            act.dma_start(par[:], params[0]).then_inc(par_in, 16)
            act.dma_start(B[6][:], mem_in).then_inc(mem_in_sem, 16)
            act.dma_start(B[1][0:33, 0:520], t5_in).then_inc(t5_loaded, 16)
            act.wait_ge(consts_in, 16 * 4)
            step = Steps(act, act_step, ACT_STEPS)

            def squares(src, col, signal):
                for b in range(TB):
                    ins = nc.scalar.activation(tok(gate)[:, b, :], src(b), ACT.Square, accum_out=sm(SS + col + b))
                ins.then_inc(signal, 1)

            with act.Fori(0, DEPTH) as l:
                T = l * A_TILES
                step.base, step.n = l * ACT_STEPS, 0

                def root(norm, col, n):
                    act.wait_ge(norm_var, l * 4 + norm)
                    nc.scalar.activation(sm(SD + col, n), sm(VAR + col, n), ACT.Sqrt).then_inc(norm_sd, 1)

                def operand_hi(which, norm, bank0, gain):
                    for c in range(KC):
                        if c % 2 == 0:
                            act.wait_ge(turned, l * TURNS + norm * 4 + c // 2 + 1)
                        nc.scalar.activation(op_hi[which][:, c, :], psum[:, bank0 + c // 2, (c % 2) * S:(c % 2 + 1) * S],
                                             ACT.Identity, scale=gain(c)).then_inc(op_hi_done, 1)

                def empty(t, dst, scale=1.0):
                    act.wait_ge(tile_done, T + t + 1)
                    src = psum[:, t % 4, :].rearrange("p (a n) -> p a n", a=2)
                    nc.scalar.activation(dst, src, ACT.Identity, scale=scale).then_inc(act_evac, 1)

                def empty_gate(t, func, branch, n):
                    act.wait_ge(tile_done, T + t + 1)
                    for c in range(2):
                        col = PA["b_gate"] + branch * KC + 2 * n + c
                        ins = nc.scalar.activation(feat(gate)[:, 2 * n + c, :], psum[:, t % 4, c * S:(c + 1) * S], func,
                                                   bias=par[:, col:col + 1])
                    ins.then_inc(act_evac, 1)

                act.wait_ge(mem_in_sem, l * 16 + 16)
                act.wait_ge(par_in, l * 16 + 16)
                squares(lambda b: tok(B[6])[:, b, :], 0, norm_ss)
                act.wait_ge(x_ready, l * 2 + 1)
                act.wait_ge(norm_ss, l * 3 + 1)
                squares(lambda b: x[:, b, :], 2, norm_ss)
                root(1, 0, 2)
                root(2, 2, 2)
                operand_hi(1, 0, 0, lambda c: par[:, PA["mem"] + c:PA["mem"] + c + 1])
                operand_hi(0, 1, 4, lambda c: par[:, PA["mix_pre"] + c:PA["mix_pre"] + c + 1])
                act.wait_ge(par_d, l + 1)
                step(nc.scalar.activation(prep[:, 0:8], prep[:, 0:8], ACT.Exp))
                nc.scalar.activation(prep[:, 16:18], prep[:, 8:10], ACT.Exp).then_inc(par_a, 1)
                nc.scalar.activation(prep[:, 0:8], prep[:, 0:8], ACT.Ln, bias=1.0).then_inc(par_a, 1)

                for n in range(4):
                    empty(T_K + n, k_mem[:, 2 * n:2 * n + 2, :])
                act.wait_ge(t5_skewed_in, 8 * 16)
                for n in range(4):
                    empty(T_V + n, v_mem[:, :, n * 256:(n + 1) * 256])
                for n in range(4):
                    empty(T_XQ + n, q_mem[:, 2 * n:2 * n + 2, :], X_HD ** -0.5)

                def empty_rope(i):
                    act.wait_ge(rope_turned, l * 8 + i + 1)
                    dst, scale = (q_t, A_HD ** -0.5) if i < 4 else (k_t, 1.0)
                    nc.scalar.activation(dst[:, 2 * (i % 4):2 * (i % 4) + 2, :], psum[:, 5, :].rearrange("p (a n) -> p a n", a=2),
                                         ACT.Identity, scale=scale).then_inc(rope_evac, 1)

                def x_exps(h):
                    act.wait_ge(x_max, l * X_HEADS + h + 1)
                    for b in range(TB):
                        ins = nc.scalar.activation(expd[:, b, :], psum[:, 4, b * 256:(b + 1) * 256], ACT.Exp,
                                                   bias=sm(NMAX + b), accum_out=sm(ZSUM + b))
                    ins.then_inc(x_exp, 1)

                def x_empty_turned(h):
                    act.wait_ge(x_turned, l * X_HEADS + h + 1)
                    nc.scalar.activation(probs_t[:], psum[:, 6, :], ACT.Identity).then_inc(x_pt, 1)

                def x_hi(h):
                    act.wait_ge(x_out, l * X_HEADS + h + 1)
                    nc.scalar.activation(op_hi[1][:, 2 * h:2 * h + 2, :], psum[:, 7, :].rearrange("p (a n) -> p a n", a=2),
                                         ACT.Identity).then_inc(op_hi_done, 1)

                for i in range(8):
                    if i:
                        empty_rope(i - 1)
                    if i % 2 == 0:
                        if i:
                            x_hi(i // 2 - 1)
                        x_exps(i // 2)
                    else:
                        x_empty_turned(i // 2)
                empty(T_AV, v_a[:, :, 0:256])
                empty_rope(7)
                x_hi(3)
                for n in range(1, 4):
                    empty(T_AV + n, v_a[:, :, n * 256:(n + 1) * 256])

                def empty_during_heads(t):
                    if t < T_ZY:
                        n = t - T_ZX
                        empty(t, zx[:, 2 * n:2 * n + 2, 4:260])
                    elif t < T_GM:
                        n = t - T_ZY
                        empty(t, gz[:, 2 * n:2 * n + 2, :])
                    elif t < T_PM:
                        empty_gate(t, ACT.Identity, 2, t - T_GM)

                for h in range(A_HEADS):
                    t = T_ZX + 2 * h
                    act.wait_ge(d_max, l * A_HEADS + h + 1)
                    for m in range(2):
                        for b in range(TB):
                            n = (b + 1) * P
                            ins = nc.scalar.activation(expd[:, 2 * m + b, 0:n], psum[:, 4 + m, b * 256:b * 256 + n], ACT.Exp,
                                                       bias=sm(NMAX + 2 * m + b), accum_out=sm(ZSUM + 2 * m + b))
                    ins.then_inc(d_exp, 1)
                    empty_during_heads(t)
                    act.wait_ge(d_turned, l * A_HEADS + h + 1)
                    nc.scalar.activation(probs_t[:, 0:384], psum[:, 6, 0:384], ACT.Identity).then_inc(d_pt, 1)
                    empty_during_heads(t + 1)
                    if t + 2 == T_PM:
                        act.wait_ge(act_evac, l * N_ACT_EVAC + ACT_EVAC[T_PM - 1])
                        nc.scalar.activation(gate[:], gate[:], ACT.Sigmoid).then_inc(mem_gate, 1)
                    if h == 6:
                        act.wait_ge(conv_done, l * 4 + 4)
                        act.dma_start(B[0][:, 0:2048], rg_w[l]).then_inc(rgw_in, 16)
                    act.wait_ge(d_out, l * A_HEADS + h + 1)
                    nc.scalar.activation(o_a[:, :, h * P:(h + 1) * P], psum[:, 7, 0:256].rearrange("p (b n) -> p b n", b=TB),
                                         ACT.Identity).then_inc(d_kept, 1)

                act.wait_ge(norm_var, l * 4 + 3)
                nc.scalar.activation(prep[:, 48:64], prep[:, 32:48], ACT.Sqrt).then_inc(norm_sd, 1)
                act.wait_ge(dve_evac, l * N_DVE_EVAC + DVE_EVAC[T_PM + 3])

                def rg_sigmoids(c):
                    act.wait_ge(rg_done, l * KC + c + 1)
                    nc.scalar.activation(r_g[:, c, :], psum[:, 4 + c % 4, 0:S], ACT.Sigmoid,
                                         bias=par[:, PA["rg_ba"] + c:PA["rg_ba"] + c + 1])
                    nc.scalar.activation(i_g[:, c, :], psum[:, 4 + c % 4, S:2 * S], ACT.Sigmoid,
                                         bias=par[:, PA["rg_bi"] + c:PA["rg_bi"] + c + 1]).then_inc(rg_evac, 1)

                for n in range(2):
                    empty_gate(T_GA + n, ACT.Sigmoid, 0, n)
                    for c in range(4):
                        rg_sigmoids(4 * n + c)
                empty_gate(T_GA + 2, ACT.Sigmoid, 0, 2)
                operand_hi(1, 2, 4, lambda c: sm(GSUB))
                empty_gate(T_GA + 3, ACT.Sigmoid, 0, 3)
                for c in range(KC):
                    nc.scalar.activation(t_g[:, c, :], r_g[:, c, :], ACT.Tanh, scale=sm(SP_POS + c))
                    ins = nc.scalar.activation(r_g[:, c, :], r_g[:, c, :], ACT.Exp, scale=sm(SP_NEG + c))
                ins.then_inc(lru_ta, 1)
                nc.scalar.activation(B[5][:], B[5][:], ACT.Gelu_apprx_tanh).then_inc(gelu_done, 1)
                act.wait_ge(lru_v, l + 1)
                nc.scalar.activation(B[4][:], B[4][:], ACT.Sqrt).then_inc(lru_s, 1)
                act.wait_ge(lru_u, l + 1)
                act.dma_start(B[4][:], post_gain[l]).then_inc(gain_in, 16)
                act.wait_ge(dve_evac, l * N_DVE_EVAC + DVE_EVAC[T_PA + 3])
                act.wait_ge(lru_y, l + 1)
                nc.scalar.activation(op_hi[1][:].rearrange("p c t -> p (c t)"), B[6][:], ACT.Identity).then_inc(op_hi_done, 1)
                for n in range(4):
                    empty_gate(T_GL + n, ACT.Sigmoid, 1, n)
                for n in range(4):
                    act.wait_ge(merged_part, l * 4 + n + 1)
                    nc.scalar.activation(op_hi[0][:, 2 * n:2 * n + 2, :], feat(merged)[:, 2 * n:2 * n + 2, :],
                                         ACT.Identity).then_inc(op_hi_done, 1)
                for n in range(4):
                    empty(T_OUT + n, y_tok[:, :, n * 256:(n + 1) * 256])
                act.wait_ge(act_evac, l * N_ACT_EVAC + N_ACT_EVAC)
                act.wait_ge(dve_evac, l * N_DVE_EVAC + N_DVE_EVAC)
                squares(lambda b: y_tok[:, b, :], 4, post_ss)
                act.wait_ge(post_var, l * 2 + 1)
                nc.scalar.activation(sm(SD + 4, 2), sm(VAR + 4, 2), ACT.Sqrt).then_inc(post_sd, 1)
                act.wait_ge(x_ready, l * 2 + 2)
                squares(lambda b: x[:, b, :], 6, norm_ss)
                root(4, 6, 2)
                operand_hi(0, 3, 4, lambda c: par[:, PA["mlp_pre"] + c:PA["mlp_pre"] + c + 1])
                act.wait_ge(op_ready, l * N_OPS + MLP_OP)
                act.dma_start(par[:], params[l + 1]).then_inc(par_in, 16)
                act.dma_start(B[6][:], mem_in).then_inc(mem_in_sem, 16)

                def relu(j, t, slot, first=False):
                    act.wait_ge(tile_done, T + (t + 1))
                    if not first:
                        act.wait_ge(squared_done, l * A_UP + (j - 1))
                    nc.scalar.activation(relu_u[:, slot, :], psum[:, slot, :], ACT.Relu).then_inc(relu_done, 1)

                relu(0, T_UP, 0, True)
                relu(1, T_UP + 1, 1, True)
                with act.Fori(0, A_UP // 2 - 1) as i:
                    relu(i * 2 + 2, i * 4 + (T_UP + 3), 0)
                    relu(i * 2 + 3, i * 4 + (T_UP + 5), 1)
                act.wait_ge(tile_done, T + A_TILES)
                squares(lambda b: psum[:, 4 + 2 * b:6 + 2 * b, :].rearrange("p a n -> p (a n)"), 8, post_ss)
                act.wait_ge(post_var, l * 2 + 2)
                nc.scalar.activation(sm(SD + 8, 2), sm(VAR + 8, 2), ACT.Sqrt).then_inc(post_sd, 1)
                assert step.n == ACT_STEPS, step.n

            T0 = DEPTH * A_TILES
            act.wait_ge(par_in, 16 * (DEPTH + 1))
            act.wait_ge(t5_stored, 16)
            act.wait_ge(mem_in_sem, 16 * (DEPTH + 1))
            act.wait_ge(x_ready, 2 * DEPTH + 1)
            act.dma_start(B[6][:, 0:7 * P], masks_in).then_inc(b_masks_in, 16)
            for h in range(8):
                for u in range(TB):
                    src = bass.AP(tensor=t5_skewed.tensor, offset=t5_skewed.offset + h * P * (SKEW + 1) + 255 - u * P,
                                  ap=[[SKEW, P], [1, (u + 1) * P]])
                    act.dma_start(bias_b[h][:, u, 0:(u + 1) * P], src).then_inc(bias_in, 16)

            def squares_b(col):
                for b in range(TB):
                    ins = nc.scalar.activation(tok(gate)[:, b, :], x[:, b, :], ACT.Square, accum_out=sm(SS + col + b))
                ins.then_inc(b_ss, 1)

            def root_b(n, col):
                act.wait_ge(b_var, n)
                nc.scalar.activation(sm(SD + col, 2), sm(VAR + col, 2), ACT.Sqrt).then_inc(b_sd, 1)

            def operand_hi_b(n, name):
                for c in range(KC):
                    if c % 2 == 0:
                        act.wait_ge(b_turned, 4 * (n - 1) + c // 2 + 1)
                    nc.scalar.activation(op_hi[0][:, c, :], psum[:, 4 + c // 2, (c % 2) * S:(c % 2 + 1) * S], ACT.Identity,
                                         scale=par[:, PB[name] + c:PB[name] + c + 1]).then_inc(b_hi, 1)

            squares_b(0)
            root_b(1, 0)
            operand_hi_b(1, "mix")
            for t in range(N_FEAT):
                act.wait_ge(tile_done, T0 + t + 1)
                dst = B[t // 4][:, (t % 4) * 512:(t % 4 + 1) * 512]
                is_query = 2 * t in (SB_Q, MB_Q, FX_Q, DS_Q)
                nc.scalar.activation(dst, psum[:, t % 4, :], ACT.Identity, scale=B_HD ** -0.5 if is_query else 1.0).then_inc(b_evac_a, 1)
            for n in range(N_TOK):
                act.wait_ge(tile_done, T0 + N_FEAT + n + 1)
                nc.scalar.activation(v_b[:, :, n * 256:(n + 1) * 256], psum[:, (N_FEAT + n) % 4, :].rearrange("p (b n) -> p b n", b=TB),
                                     ACT.Identity).then_inc(b_evac_a, 1)

            def empty_gate_b(b, n):
                act.wait_ge(tile_done, T0 + T2_GATE + 5 * b + n + 1)
                if b:
                    act.wait_ge(b_mixed, b)
                nc.scalar.activation(gate[:, n * 512:(n + 1) * 512], psum[:, n, :], ACT.Sigmoid).then_inc(b_evac_a, 1)

            def index_relu(h):
                act.wait_ge(ix_scores, h + 1)
                if h >= 2:
                    act.wait_ge(ix_added, h - 1)
                nc.scalar.activation(expd[:, 2 * (h % 2), 0:P], psum[:, 4 + h % 4, 0:P], ACT.Relu)
                nc.scalar.activation(expd[:, 2 * (h % 2) + 1, :], psum[:, 4 + h % 4, 256:512], ACT.Relu).then_inc(ix_relu, 1)

            for h in range(4):
                index_relu(h)
            empty_gate_b(0, 0)
            for h in range(4, IDX_HEADS):
                index_relu(h)
            act.preload_act_table_set("natural_log_exp_and_others")
            act.wait_ge(f_in, 1)
            nc.scalar.activation(prep[:, 8:16], prep[:, 8:16], ACT.Exp).then_inc(f_ln, 1)
            act.wait_ge(f_ln, 1)
            nc.scalar.activation(prep[:, 8:16], prep[:, 8:16], ACT.Ln, bias=1.0).then_inc(f_ln, 1)
            act.wait_ge(c_sums, 1)
            nc.scalar.activation(c_col, psum[:, 4, 0:8], ACT.Identity).then_inc(c_kept, 1)
            nc.scalar.activation(minus_c_row.rearrange("p h n -> p (h n)"), psum[:, 5:7, :].rearrange("p a n -> p (a n)"),
                                 ACT.Identity, scale=-1.0).then_inc(c_kept, 1)

            def sb_softplus_tail(h):
                act.wait_ge(sb_z, h + 1)
                a = expd[:, 2 * (h % 2):2 * (h % 2) + 2, :].rearrange("p a n -> p (a n)")[:, 0:384]
                if h == 0:
                    act.wait_ge(ix_added, IDX_HEADS)
                for k, (src, func, bias) in enumerate(((psum[:, 4 + h % 2, 0:384], ACT.Abs, 0.0), (a, ACT.Exp, 0.0), (a, ACT.Ln, 1.0))):
                    nc.scalar.activation(a, src, func, bias=bias, scale=-1.0 if k == 1 else 1.0).then_inc(sb_ln, 1)
                    if k < 2:
                        act.wait_ge(sb_ln, 3 * h + k + 1)

            def sb_weights(h):
                act.wait_ge(sb_summed, h + 1)
                if h:
                    act.wait_ge(b_out, h)
                nc.scalar.activation(probs_t[:, 0:384], psum[:, 4 + h % 2, 0:384], ACT.Exp).then_inc(sb_w, 1)

            def branch_hi(b):
                act.wait_ge(b_out, 4 * (b + 1))
                if b:
                    act.wait_ge(tile_done, T0 + T2_GATE + 5 * b)
                nc.scalar.activation(op_hi[1][:, 0:2, :], psum[:, 7, :].rearrange("p (a t) -> p a t", a=2), ACT.Identity).then_inc(b_hi, 1)

            sb_softplus_tail(0)
            for h in range(4):
                if h < 3:
                    empty_gate_b(0, h + 1)
                sb_weights(h)
                if h < 3:
                    sb_softplus_tail(h + 1)
            branch_hi(0)

            def s_exps(b, h):
                g = 4 * (b - 1) + h
                act.wait_ge(s_max, g + 1)
                e = 2 * (h % 2)
                for u in range(TB):
                    ins = nc.scalar.activation(expd[:, e + u, 0:(u + 1) * P], expd[:, e + u, 0:(u + 1) * P], ACT.Exp,
                                               bias=sm(NMAX + e + u), accum_out=sm(ZSUM + e + u))
                ins.then_inc(s_exp, 1)

            def s_empty_turned(b, h):
                g = 4 * (b - 1) + h
                act.wait_ge(s_turned, g + 1)
                if h:
                    act.wait_ge(b_out, 4 * b + h)
                nc.scalar.activation(probs_t[:, 0:384], psum[:, 6, 0:384], ACT.Identity).then_inc(s_pt, 1)

            for b in range(1, 4):
                s_exps(b, 0)
                for h in range(4):
                    empty_gate_b(b, h)
                    s_empty_turned(b, h)
                    if h < 3:
                        s_exps(b, h + 1)
                branch_hi(b)

            for n in range(4):
                act.wait_ge(out_part, n + 1)
                nc.scalar.activation(op_hi[0][:, 2 * n:2 * n + 2, :], feat(merged)[:, 2 * n:2 * n + 2, :], ACT.Identity).then_inc(b_hi, 1)
            act.wait_ge(x_b, 1)
            act.dma_start(merged[:, 0:D], final_gain).then_inc(final_in, 16)
            squares_b(2)
            root_b(2, 2)
            operand_hi_b(2, "ffn")
            act.wait_ge(pads_zero, 1)
            for j in range(B_UP):
                t = T2_FFN + (0 if j == 0 else 2 + 3 * (j - 1))
                for n in range(2):
                    act.wait_ge(tile_done, T0 + t + n + 1)
                    if j >= 2 and n == 0:
                        act.wait_ge(f_conv, j - 1)
                    nc.scalar.activation(padded[:, j % 2, 2 * n:2 * n + 2, 2:2 + S],
                                         psum[:, 2 * (j % 2) + n, :].rearrange("p (a t) -> p a t", a=2), ACT.Identity).then_inc(f_evac, 1)
                act.wait_ge(f_conv, j + 1)
                if j >= 2:
                    act.wait_ge(f_gated, j - 1)
                nc.scalar.activation(gelu_g[:, j % 2, :], conved[:, j % 2, 0:2, :].rearrange("p a t -> p (a t)"), ACT.Gelu).then_inc(f_gelu, 1)
            act.wait_ge(x_b, 2)
            squares_b(4)
            root_b(3, 4)
            act.wait_ge(x_b, 3)
            act.dma_start(out, y_tok).then_inc(out_done, 16)

        @block.vector
        def _(dve):
            step = Steps(dve, dve_step, DVE_STEPS)

            def split(t, s, round_of_slot):
                dve.wait_ge(raw_loaded[s], round_of_slot * 16 + 16)
                nc.vector.tensor_copy(w_hi[:, s, :], w_raw[:, s, :]).then_inc(hi_ready, 1)

            for s in range(HI):
                split(s, s, 0)
            nc.vector.memset(rowmask[:], 0.0).then_inc(masks_ready, 1)
            nc.vector.memset(colmask[:], NEG).then_inc(masks_ready, 1)
            dve.wait_ge(masks_ready, 2)
            nc.vector.memset(rowmask[:, 0:64], 1.0).then_inc(masks_ready, 1)
            dve.wait_ge(consts_in, 16 * 4)
            dve.wait_ge(t5_rows_ready, 1)
            nc.vector.tensor_copy(B[1][0:8, 1024:1536], psum[0:8, 4, :]).then_inc(t5_evac, 1)
            nc.vector.sem_inc(x_ready, 1)

            with dve.Fori(0, DEPTH) as l:
                T = l * A_TILES
                OP = l * N_OPS
                step.base, step.n = l * DVE_STEPS, 0
                his = [0]

                def hi_part(n=1):
                    his[0] += n
                    dve.wait_ge(op_hi_done, l * 41 + his[0])

                def after(t, evac=None):
                    dve.wait_ge(tile_done, T + t + 1)
                    if evac:
                        evac()
                    split(T + t + 4, (t + 4) % 4, l * (A_TILES // 4) + (t + 4) // 4)

                def variance(signal, dst, src, n):
                    nc.vector.tensor_scalar(dst, src, 1.0 / n, EPS, ALU.mult, ALU.add).then_inc(signal, 1)

                def normalize(norm, col, src, dst):
                    dve.wait_ge(norm_sd, l * 4 + norm)
                    step(nc.vector.reciprocal(sm(RS + col, 2), sm(SD + col, 2)))
                    for b in range(TB):
                        ins = nc.vector.tensor_scalar(tok(dst)[:, b, :], src(b), sm(RS + col + b), None, ALU.mult)
                    ins.then_inc(norm_x, 1)

                def operand_lo(which, bank0, gain):
                    for c in range(KC):
                        if c % 2 == 0:
                            hi_part(2)
                        ins = nc.vector.scalar_tensor_tensor(
                            op_lo[which][:, c, :], psum[:, bank0 + c // 2, (c % 2) * S:(c % 2 + 1) * S], gain(c),
                            op_hi[which][:, c, :].bitcast(F32), ALU.mult, ALU.subtract)
                    ins.then_inc(op_ready, 1)

                dve.wait_ge(norm_ss, l * 3 + 1)
                variance(norm_var, sm(VAR, 2), sm(SS, 2), D)
                dve.wait_ge(norm_ss, l * 3 + 2)
                variance(norm_var, sm(VAR + 2, 2), sm(SS + 2, 2), D)
                normalize(1, 0, lambda b: tok(B[6])[:, b, :], B[6])
                normalize(2, 2, lambda b: x[:, b, :], gate)
                operand_lo(1, 0, lambda c: par[:, PA["mem"] + c:PA["mem"] + c + 1])
                operand_lo(0, 4, lambda c: par[:, PA["mix_pre"] + c:PA["mix_pre"] + c + 1])

                lam = par[:, PA["rg_lambda"]:PA["rg_lambda"] + 8]
                nc.vector.scalar_tensor_tensor(prep[:, 0:8], lam, -1.0, lam, ALU.mult, ALU.min)
                nc.vector.tensor_scalar(prep[:, 24:32], lam, 0.0, -1.0, ALU.min, ALU.mult)
                step(nc.vector.tensor_tensor(prep[:, 32:160], par[:, PA["lambda_q"]:PA["lambda_q"] + 128],
                                             par[:, PA["lambda_k"]:PA["lambda_k"] + 128], ALU.mult))
                nc.vector.tensor_reduce(prep[:, 8:10], prep[:, 32:160].rearrange("p (a n) -> p a n", a=2), AX.X,
                                        ALU.add).then_inc(par_d, 1)
                nc.vector.tensor_tensor(sm(GSUB), par[:, PA["subln"]:PA["subln"] + 1],
                                        par[:, PA["one_minus_init"]:PA["one_minus_init"] + 1], ALU.mult)
                dve.wait_ge(par_a, l * 2 + 2)
                step(nc.vector.tensor_tensor(sm(NLAM), prep[:, 17:18], prep[:, 16:17], ALU.subtract))
                nc.vector.tensor_tensor(sm(NLAM), sm(NLAM), par[:, PA["init"]:PA["init"] + 1], ALU.subtract)
                step(nc.vector.tensor_tensor(prep[:, 0:8], prep[:, 0:8], prep[:, 24:32], ALU.add))
                nc.vector.tensor_scalar(sm(SP_POS, 8), prep[:, 0:8], 8.0, None, ALU.mult)
                step(nc.vector.tensor_scalar(sm(SP_NEG, 8), prep[:, 0:8], -8.0, None, ALU.mult))

                for t in range(T_K, T_QK):
                    after(t)

                def rope(i):
                    def evac():
                        bank = (T_QK + i) % 4
                        if i >= 2:
                            dve.wait_ge(rope_turned, l * 8 + i - 1)
                        if i:
                            dve.wait_ge(rope_ready, l * 8 + i)
                        for b in range(TB):
                            z = psum[:, bank, b * 256:(b + 1) * 256]
                            zg = z.rearrange("p (g h n) -> p g h n", g=4, h=2)
                            za = rope_a[:, b * 256:(b + 1) * 256]
                            zb = rope_b[:, b * 256:(b + 1) * 256].rearrange("p (g h n) -> p g h n", g=4, h=2)
                            nc.vector.tensor_tensor(za.rearrange("p (g n) -> p g n", n=32), z.rearrange("p (g n) -> p g n", n=32),
                                                    cos[:, b:b + 1, :].to_broadcast([P, 8, 32]), ALU.mult)
                            s4 = sin[:, b:b + 1, :].to_broadcast([P, 4, 32])
                            nc.vector.scalar_tensor_tensor(zb[:, :, 0, :], zg[:, :, 1, :], -1.0, s4, ALU.mult, ALU.mult)
                            ins = nc.vector.tensor_tensor(zb[:, :, 1, :], zg[:, :, 0, :], s4, ALU.mult)
                        ins.then_inc(dve_evac, 1)
                        dve.wait_ge(dve_evac, l * N_DVE_EVAC + i + 1)
                        nc.vector.tensor_tensor(rot[:, i % 2, :], rope_a, rope_b, ALU.add).then_inc(rope_ready, 1)
                    return evac

                def x_softmax(h):
                    dve.wait_ge(x_scores, l * X_HEADS + h + 1)
                    nc.vector.tensor_reduce(sm(NMAX, 2), psum[:, 4, :].rearrange("p (b n) -> p b n", b=TB), AX.X, ALU.max,
                                            negate=True).then_inc(x_max, 1)
                    dve.wait_ge(x_exp, l * X_HEADS + h + 1)
                    step(nc.vector.reciprocal(sm(RZ, 2), sm(ZSUM, 2)))
                    for b in range(TB):
                        ins = nc.vector.tensor_scalar(expd[:, b, :], expd[:, b, :], sm(RZ + b), None, ALU.mult)
                    ins.then_inc(x_probs, 1)

                def x_lo(h):
                    hi_part()
                    nc.vector.tensor_tensor(op_lo[1][:, 2 * h:2 * h + 2, :], psum[:, 7, :].rearrange("p (a n) -> p a n", a=2),
                                            op_hi[1][:, 2 * h:2 * h + 2, :].bitcast(F32), ALU.subtract).then_inc(op_ready, 1)

                for i in range(8):
                    after(T_QK + i, rope(i))
                    if i % 2 == 0:
                        x_softmax(i // 2)
                        if i:
                            x_lo(i // 2 - 1)
                after(T_AV)
                x_lo(3)
                nc.vector.memset(zx[:, :, 0:4], 0.0).then_inc(zx_padded, 1)
                for t in range(T_AV + 1, T_ZX):
                    after(t)

                def add_branch(t0, n, first, last=False):
                    def evac():
                        cols = slice(n * 512, (n + 1) * 512)
                        if first:
                            nc.vector.tensor_tensor(merged[:, cols], psum[:, (t0 + n) % 4, :], gate[:, cols], ALU.mult).then_inc(dve_evac, 1)
                            return
                        prod = expd[:, 0:2, :].rearrange("p a n -> p (a n)")
                        if last and n:
                            dve.wait_ge(merged_part, l * 4 + n)
                        nc.vector.tensor_tensor(prod, psum[:, (t0 + n) % 4, :], gate[:, cols], ALU.mult).then_inc(dve_evac, 1)
                        dve.wait_ge(dve_evac, l * N_DVE_EVAC + DVE_EVAC[t0 + n])
                        ins = nc.vector.tensor_tensor(merged[:, cols], merged[:, cols], prod, ALU.add)
                        if last:
                            ins.then_inc(merged_part, 1)
                        else:
                            step(ins)
                    return evac

                def conv(c0):
                    for k in range(4):
                        for c in (c0, c0 + 1):
                            w = par[:, PA["conv_w"] + k * KC + c:PA["conv_w"] + k * KC + c + 1]
                            src = zx[:, c, 1 + k:1 + k + S]
                            if k == 0:
                                ins = nc.vector.tensor_scalar(xc[:, c, :], src, w, par[:, PA["conv_b"] + c:PA["conv_b"] + c + 1],
                                                              ALU.mult, ALU.add)
                            else:
                                ins = nc.vector.scalar_tensor_tensor(xc[:, c, :], src, w, xc[:, c, :], ALU.mult, ALU.add)
                        if k < 3:
                            step(ins)
                    ins.then_inc(conv_done, 1)

                for h in range(A_HEADS):
                    t = T_ZX + 2 * h
                    dve.wait_ge(d_scores, l * A_HEADS + h + 1)
                    for b in range(TB):
                        n = (b + 1) * P
                        ins = nc.vector.tensor_reduce(small[:, NMAX + b:NMAX + b + 3:2], psum[:, 4:6, b * 256:b * 256 + n], AX.X,
                                                      ALU.max, negate=True)
                    ins.then_inc(d_max, 1)
                    dve.wait_ge(d_exp, l * A_HEADS + h + 1)
                    step(nc.vector.reciprocal(sm(RZ, 4), sm(ZSUM, 4)))
                    nc.vector.tensor_scalar(sm(R2, 2), sm(RZ + 2, 2), sm(NLAM), None, ALU.mult)
                    for b in range(TB):
                        ins = nc.vector.tensor_scalar(expd[:, b, 0:(b + 1) * P], expd[:, b, 0:(b + 1) * P], sm(RZ + b), None, ALU.mult)
                    step(ins)
                    for b in range(TB):
                        n = (b + 1) * P
                        ins = nc.vector.scalar_tensor_tensor(expd[:, b, 0:n], expd[:, 2 + b, 0:n], sm(R2 + b), expd[:, b, 0:n],
                                                             ALU.mult, ALU.add)
                    ins.then_inc(d_probs, 1)
                    for u in (t, t + 1):
                        if u >= T_PM:
                            if u == T_PM:
                                dve.wait_ge(mem_gate, l + 1)
                            after(u, add_branch(T_PM, u - T_PM, True))
                        else:
                            after(u)
                    if 2 <= h < 6:
                        dve.wait_ge(act_evac, l * N_ACT_EVAC + ACT_EVAC[T_ZX + h - 2])
                        if h == 2:
                            dve.wait_ge(zx_padded, l + 1)
                        conv(2 * (h - 2))

                dve.wait_ge(d_kept, l * A_HEADS + A_HEADS)
                step(nc.vector.tensor_tensor(B[4][:], B[6][:], B[6][:], ALU.mult))
                step(nc.vector.tensor_reduce(prep[:, 32:48], B[4][:].rearrange("p (a n) -> p a n", n=P), AX.X, ALU.add))
                variance(norm_var, prep[:, 32:48], prep[:, 32:48], P)
                dve.wait_ge(norm_sd, l * 4 + 3)
                step(nc.vector.reciprocal(prep[:, 48:64], prep[:, 48:64]))
                heads = B[6][:].rearrange("p (a n) -> p a n", n=P)
                nc.vector.tensor_tensor(heads, heads, prep[:, 48:64].unsqueeze(2).to_broadcast([P, 16, P]), ALU.mult).then_inc(norm_x, 1)
                after(T_GA)
                after(T_GA + 1)
                after(T_GA + 2)
                operand_lo(1, 4, lambda c: sm(GSUB))
                after(T_GA + 3)

                dve.wait_ge(lru_ta, l + 1)
                step(nc.vector.tensor_tensor(B[6][:], B[2][:], B[2][:], ALU.mult))
                nc.vector.scalar_tensor_tensor(B[4][:], B[6][:], 1.0, B[4][:], ALU.add, ALU.mult).then_inc(lru_v, 1)
                after(T_PA, add_branch(T_PA, 0, False))
                step(nc.vector.tensor_tensor(B[3][:], B[3][:], B[1][:], ALU.mult))
                dve.wait_ge(lru_s, l + 1)
                nc.vector.tensor_tensor(B[3][:], B[3][:], B[4][:], ALU.mult).then_inc(lru_u, 1)
                after(T_PA + 1, add_branch(T_PA, 1, False))
                dve.wait_ge(lru_u, l + 1)
                for c in range(KC):
                    ins = nc.vector.tensor_tensor_scan(lru[:, c, :], r_g[:, c, :], i_g[:, c, :], 0.0, ALU.mult, ALU.add)
                step(ins)
                after(T_PA + 2, add_branch(T_PA, 2, False))
                dve.wait_ge(gelu_done, l + 1)
                nc.vector.tensor_tensor(B[6][:], B[6][:], B[5][:], ALU.mult).then_inc(lru_y, 1)
                after(T_PA + 3, add_branch(T_PA, 3, False))
                hi_part()
                nc.vector.tensor_tensor(op_lo[1][:].rearrange("p c t -> p (c t)"), B[6][:],
                                        op_hi[1][:].rearrange("p c t -> p (c t)").bitcast(F32), ALU.subtract).then_inc(op_ready, 1)
                for t in range(T_GL, T_PL):
                    after(t)
                for n in range(4):
                    after(T_PL + n, add_branch(T_PL, n, False, True))
                    hi_part()
                    ins = nc.vector.tensor_tensor(op_lo[0][:, 2 * n:2 * n + 2, :], feat(merged)[:, 2 * n:2 * n + 2, :],
                                                  op_hi[0][:, 2 * n:2 * n + 2, :].bitcast(F32), ALU.subtract)
                ins.then_inc(op_ready, 1)
                for t in range(T_OUT, T_UP):
                    after(t)

                def add_normed(k, src):
                    col = 4 + 4 * k
                    dve.wait_ge(post_ss, l * 2 + k + 1)
                    variance(post_var, sm(VAR + col, 2), sm(SS + col, 2), D)
                    dve.wait_ge(post_sd, l * 2 + k + 1)
                    step(nc.vector.reciprocal(sm(RS + col, 2), sm(SD + col, 2)))
                    if k == 0:
                        dve.wait_ge(gain_in, l * 16 + 16)
                    for b in range(TB):
                        ins = nc.vector.scalar_tensor_tensor(y_tok[:, b, :], src(b), sm(RS + col + b), gains[:, k, :], ALU.mult, ALU.mult)
                    step(ins)
                    for b in range(TB):
                        ins = nc.vector.tensor_tensor(x[:, b, :], x[:, b, :], y_tok[:, b, :], ALU.add)
                    ins.then_inc(x_ready, 1)

                add_normed(0, lambda b: y_tok[:, b, :])
                dve.wait_ge(x_ready, l * 2 + 2)
                dve.wait_ge(norm_ss, l * 3 + 3)
                variance(norm_var, sm(VAR + 6, 2), sm(SS + 6, 2), D)
                normalize(4, 6, lambda b: x[:, b, :], gate)
                operand_lo(0, 4, lambda c: par[:, PA["mlp_pre"] + c:PA["mlp_pre"] + c + 1])

                def after_mlp(t, i=None):
                    if i is None:
                        dve.wait_ge(tile_done, T + (t + 1))
                        split(None, (t + 4) % 4, l * (A_TILES // 4) + (t + 4) // 4)
                    else:
                        dve.wait_ge(tile_done, T + i * 4 + (t + 1))
                        split(None, (t + 4) % 4, l * (A_TILES // 4) + i + (t + 4) // 4)

                def hidden(j, slot):
                    dve.wait_ge(relu_done, l * A_UP + (j + 1))
                    nc.vector.tensor_tensor(squared[:, slot, :], relu_u[:, slot, :], relu_u[:, slot, :], ALU.mult).then_inc(squared_done, 1)
                    dve.wait_ge(squared_done, l * A_UP + (j + 1))
                    hi = op_hi[1][:, 2 * slot:2 * slot + 2, :].rearrange("p a t -> p (a t)")
                    lo = op_lo[1][:, 2 * slot:2 * slot + 2, :].rearrange("p a t -> p (a t)")
                    nc.vector.tensor_copy(hi, squared[:, slot, :]).then_inc(ffn_hi, 1)
                    dve.wait_ge(ffn_hi, l * A_UP + (j + 1))
                    nc.vector.tensor_tensor(lo, squared[:, slot, :], hi.bitcast(F32), ALU.subtract).then_inc(ffn_ready, 1)

                after_mlp(T_UP)
                hidden(0, 0)
                after_mlp(T_UP + 1)
                hidden(1, 1)
                after_mlp(T_UP + 2)
                with dve.Fori(0, A_UP // 2 - 1) as i:
                    after_mlp(T_UP + 3, i)
                    hidden(i * 2 + 2, 0)
                    after_mlp(T_UP + 4, i)
                    after_mlp(T_UP + 5, i)
                    hidden(i * 2 + 3, 1)
                    after_mlp(T_UP + 6, i)
                after_mlp(A_TILES - 1)
                add_normed(1, lambda b: psum[:, 4 + 2 * b:6 + 2 * b, :].rearrange("p a n -> p (a n)"))
                assert step.n == DVE_STEPS, step.n

            T0 = DEPTH * A_TILES
            bstep = Steps(dve, b_step, 0)
            bhis = [0]

            def hi_b(n=1):
                bhis[0] += n
                dve.wait_ge(b_hi, bhis[0])

            def after_b(t, evac=None):
                dve.wait_ge(tile_done, T0 + t + 1)
                if evac:
                    evac()
                if T0 + t + 4 < N_TILES:
                    split(T0 + t + 4, (t + 4) % 4, (T0 + t + 4) // 4)

            def normalize_b(n, col, dst, gain=None):
                dve.wait_ge(b_ss, n)
                nc.vector.tensor_scalar(sm(VAR + col, 2), sm(SS + col, 2), 1.0 / D, EPS, ALU.mult, ALU.add).then_inc(b_var, 1)
                dve.wait_ge(b_sd, n)
                bstep(nc.vector.reciprocal(sm(RS + col, 2), sm(SD + col, 2)))
                for b in range(TB):
                    if gain is None:
                        ins = nc.vector.tensor_scalar(tok(dst)[:, b, :], x[:, b, :], sm(RS + col + b), None, ALU.mult)
                    else:
                        ins = nc.vector.scalar_tensor_tensor(tok(dst)[:, b, :], x[:, b, :], sm(RS + col + b), gain, ALU.mult, ALU.mult)
                return ins

            def operand_lo_b(name):
                for c in range(KC):
                    if c % 2 == 0:
                        hi_b(2)
                    ins = nc.vector.scalar_tensor_tensor(
                        op_lo[0][:, c, :], psum[:, 4 + c // 2, (c % 2) * S:(c % 2 + 1) * S], par[:, PB[name] + c:PB[name] + c + 1],
                        op_hi[0][:, c, :].bitcast(F32), ALU.mult, ALU.subtract)
                ins.then_inc(b_ready, 1)

            normalize_b(1, 0, gate).then_inc(b_x, 1)
            operand_lo_b("mix")
            for t in range(N_FEAT + N_TOK):
                after_b(t)

            dve.wait_ge(b_evac_a, N_FEAT + N_TOK)
            dve.wait_ge(b_masks_in, 16)
            f = prep[:, 0:8].rearrange("p (b h) -> p b h", b=TB)
            bstep(nc.vector.tensor_tensor(f, v_b[:, :, F_COL:F_COL + 4],
                                          par[:, PB["fox_b"]:PB["fox_b"] + 4].unsqueeze(1).to_broadcast([P, TB, 4]), ALU.add))
            nc.vector.scalar_tensor_tensor(prep[:, 8:16], prep[:, 0:8], -1.0, prep[:, 0:8], ALU.mult, ALU.min).then_inc(f_in, 1)

            def index_add(h):
                dve.wait_ge(ix_relu, h + 1)
                for u in range(TB):
                    n = (u + 1) * P
                    w = v_b[:, u, W_COL + h:W_COL + h + 1]
                    r = expd[:, 2 * (h % 2) + u, 0:n]
                    if h == 0:
                        ins = nc.vector.tensor_scalar(index[:, u, 0:n], r, w, None, ALU.mult)
                    else:
                        ins = nc.vector.scalar_tensor_tensor(index[:, u, 0:n], r, w, index[:, u, 0:n], ALU.mult, ALU.add)
                ins.then_inc(ix_added, 1)
                dve.wait_ge(ix_added, h + 1)

            for h in range(4):
                index_add(h)
            after_b(T2_GATE)
            for h in range(4, IDX_HEADS):
                index_add(h)
            dve.wait_ge(f_ln, 2)
            bstep(nc.vector.scalar_tensor_tensor(log_f, prep[:, 0:8], 0.0, prep[:, 8:16], ALU.min, ALU.subtract))
            nc.vector.tensor_copy(log_f_wide, log_f.unsqueeze(2).to_broadcast([P, 8, P])).then_inc(f_wide, 1)
            for u in range(TB):
                own = index[:, u, u * P:(u + 1) * P]
                ins = nc.vector.scalar_tensor_tensor(own, causal, OUTSIDE / NEG, own, ALU.mult, ALU.add)
            bstep(ins)

            def take_eight():
                for u in range(TB):
                    ins = nc.vector.max(sm(SS + 8 * u, 8), index[:, u, 0:(u + 1) * P])
                bstep(ins)
                for u in range(TB):
                    s = index[:, u, 0:(u + 1) * P]
                    ins = nc.vector.match_replace(s, sm(SS + 8 * u, 8), s, REPLACED)
                bstep(ins)

            def sb_mask(h):
                dve.wait_ge(sb_ln, 3 * h + 3)
                m = expd[:, 2 * (h % 2):2 * (h % 2) + 2, :].rearrange("p a n -> p (a n)")
                bstep(nc.vector.scalar_tensor_tensor(m[:, 0:384], psum[:, 4 + h % 2, 0:384], 0.0, m[:, 0:384], ALU.max, ALU.add))
                nc.vector.tensor_tensor(m[:, 0:P], m[:, 0:P], before01, ALU.mult)
                nc.vector.tensor_tensor(m[:, 256:384], m[:, 256:384], before01, ALU.mult).then_inc(sb_masked, 1)

            def branch_lo(b):
                hi_b()
                nc.vector.tensor_tensor(op_lo[1][:, 0:2, :], psum[:, 7, :].rearrange("p (a t) -> p a t", a=2),
                                        op_hi[1][:, 0:2, :].bitcast(F32), ALU.subtract).then_inc(b_ready, 1)

            def mix_branch(b):
                def evac():
                    for n in range(4):
                        cols = slice(n * 512, (n + 1) * 512)
                        dst = gate if b else merged
                        ins = nc.vector.tensor_tensor(dst[:, cols], psum[:, n, :], gate[:, cols], ALU.mult).then_inc(b_evac_d, 1)
                    dve.wait_ge(b_evac_d, 4 * (b + 1))
                    if b == 0:
                        nc.vector.sem_inc(b_mixed, 1)
                        return
                    for n in range(4):
                        cols = slice(n * 512, (n + 1) * 512)
                        ins = nc.vector.tensor_tensor(merged[:, cols], merged[:, cols], gate[:, cols], ALU.add)
                        if b == 3:
                            ins.then_inc(out_part, 1)
                    if b < 3:
                        ins.then_inc(b_mixed, 1)
                        dve.wait_ge(b_mixed, b + 1)
                return evac

            sb_mask(0)
            for h in range(4):
                if h < 3:
                    after_b(T2_GATE + 1 + h)
                take_eight()
                if h < 3:
                    sb_mask(h + 1)
            branch_lo(0)

            def s_softmax(b, h):
                g = 4 * (b - 1) + h
                dve.wait_ge(s_scores, g + 1)
                e = 2 * (h % 2)
                if b == 1 and h == 0:
                    dve.wait_ge(bias_in, 16 * 16)
                for u in range(TB):
                    n = (u + 1) * P
                    sc, dst = psum[:, 4 + h % 2, u * 256:u * 256 + n], expd[:, e + u, 0:n]
                    if b == 2:
                        ins = nc.vector.scalar_tensor_tensor(dst, sc, c_col[:, 4 * u + h:4 * u + h + 1], minus_c_row[:, h, 0:n], ALU.add, ALU.add)
                    else:
                        ins = nc.vector.tensor_tensor(dst, sc, bias_b[h + (4 if b == 3 else 0)][:, u, 0:n], ALU.add)
                bstep(ins)
                if b == 2:
                    for u in range(TB):
                        own = expd[:, e + u, u * P:(u + 1) * P]
                        ins = nc.vector.tensor_tensor(own, own, causal, ALU.add)
                    bstep(ins)
                for u in range(TB):
                    ins = nc.vector.tensor_reduce(sm(NMAX + e + u), expd[:, e + u, 0:(u + 1) * P], AX.X, ALU.max, negate=True)
                ins.then_inc(s_max, 1)
                dve.wait_ge(s_exp, g + 1)
                bstep(nc.vector.reciprocal(sm(RZ + e, 2), sm(ZSUM + e, 2)))
                for u in range(TB):
                    p = expd[:, e + u, 0:(u + 1) * P]
                    ins = nc.vector.tensor_scalar(p, p, sm(RZ + e + u), None, ALU.mult)
                ins.then_inc(s_probs, 1)

            def keep_taken(h):
                for u in range(TB):
                    n = (u + 1) * P
                    ins = nc.vector.scalar_tensor_tensor(bias_b[4 + h][:, u, 0:n], index[:, u, 0:n], -NEG, bias_b[4 + h][:, u, 0:n],
                                                         ALU.mult, ALU.add)
                return ins

            for b in range(1, 4):
                s_softmax(b, 0)
                after_b(T2_GATE + 5 * b - 1, mix_branch(b - 1))
                for h in range(4):
                    if h < 3 and h:
                        pass
                    after_b(T2_GATE + 5 * b + h)
                    if b == 1:
                        take_eight()
                    if b == 2:
                        if h == 0:
                            for u in range(TB):
                                s = index[:, u, 0:(u + 1) * P]
                                ins = nc.vector.tensor_scalar(s, s, REPLACED, 1.0, ALU.is_equal, ALU.subtract)
                            bstep(ins)
                        bstep(keep_taken(h))
                    if h < 3:
                        s_softmax(b, h + 1)
                branch_lo(b)
            after_b(T2_GATE + 19, mix_branch(3))
            for n in range(4):
                hi_b()
                ins = nc.vector.tensor_tensor(op_lo[0][:, 2 * n:2 * n + 2, :], feat(merged)[:, 2 * n:2 * n + 2, :],
                                              op_hi[0][:, 2 * n:2 * n + 2, :].bitcast(F32), ALU.subtract)
            ins.then_inc(b_ready, 1)

            def add_out(n):
                def evac():
                    dst = x[:, :, n * 256:(n + 1) * 256]
                    nc.vector.tensor_tensor(dst, dst, psum[:, n, :].rearrange("p (b n) -> p b n", b=TB), ALU.add)\
                        .then_inc(x_b if n == 3 else b_step, 1)
                    if n < 3:
                        bstep.n += 1
                return evac

            for n in range(4):
                after_b(T2_OUT + n, add_out(n))
            dve.wait_ge(x_b, 1)
            normalize_b(2, 2, gate).then_inc(b_x, 1)
            nc.vector.memset(padded[:, :, :, 0:2], 0.0).then_inc(pads_zero, 1)
            operand_lo_b("ffn")

            def f_convolve(j):
                dve.wait_ge(f_evac, 2 * j + 2)
                if j >= 2:
                    dve.wait_ge(f_gated, j - 1)
                for k in range(3):
                    for i in range(4):
                        w = PB["conv_w"] + (k * B_UP + j) * 4 + i
                        src, acc = padded[:, j % 2, i, k:k + S], conved[:, j % 2, i, :]
                        if k == 0:
                            cb = PB["conv_b"] + 4 * j + i
                            ins = nc.vector.tensor_scalar(acc, src, par[:, w:w + 1], par[:, cb:cb + 1], ALU.mult, ALU.add)
                        else:
                            ins = nc.vector.scalar_tensor_tensor(acc, src, par[:, w:w + 1], acc, ALU.mult, ALU.add)
                    if k < 2:
                        bstep(ins)
                ins.then_inc(f_conv, 1)

            def f_operand(j):
                dve.wait_ge(f_gelu, j + 1)
                s = j % 2
                u = conved[:, s, 2:4, :].rearrange("p a t -> p (a t)")
                dve.wait_ge(f_conv, j + 1)
                if j >= 2:
                    dve.wait_ge(f_ready, j - 1)
                nc.vector.tensor_tensor(gated[:, s, :], gelu_g[:, s, :], u, ALU.mult).then_inc(f_gated, 1)
                dve.wait_ge(f_gated, j + 1)
                hi = op_hi[1][:, 2 * s:2 * s + 2, :].rearrange("p a t -> p (a t)")
                lo = op_lo[1][:, 2 * s:2 * s + 2, :].rearrange("p a t -> p (a t)")
                nc.vector.tensor_copy(hi, gated[:, s, :]).then_inc(f_hi, 1)
                dve.wait_ge(f_hi, j + 1)
                nc.vector.tensor_tensor(lo, gated[:, s, :], hi.bitcast(F32), ALU.subtract).then_inc(f_ready, 1)

            for j in range(B_UP):
                t = T2_FFN + (0 if j == 0 else 2 + 3 * (j - 1))
                after_b(t)
                after_b(t + 1)
                f_convolve(j)
                if j:
                    after_b(t + 2)
                f_operand(j)
            after_b(B_TILES - 1)
            for b in range(TB):
                ins = nc.vector.tensor_tensor(x[:, b, :], x[:, b, :], psum[:, 4 + 2 * b:6 + 2 * b, :].rearrange("p a n -> p (a n)"), ALU.add)
            ins.then_inc(x_b, 1)
            dve.wait_ge(x_b, 2)
            dve.wait_ge(final_in, 16)
            normalize_b(3, 4, B[1], merged[:, 0:D]).then_inc(x_b, 1)


def _col_tiles(w):
    n = w.shape[1] // 256
    return w.reshape(KC, P, n, 256).transpose(2, 1, 0, 3).reshape(n, P, TILE)


def _row_tiles(w):
    n = w.shape[0] // 256
    return w.reshape(n, 2, P, D).transpose(0, 2, 1, 3).reshape(n, P, TILE)


def _feat_vector(v):
    return np.ascontiguousarray(v.reshape(-1, P).T)


def _weight_stream(a):
    stream = np.empty((N_TILES, P, TILE), np.float32)
    at = 0

    def put(tiles):
        nonlocal at
        stream[at:at + len(tiles)] = tiles
        at += len(tiles)

    for l in range(DEPTH):
        q, k, v, zx, zy, xq, g = np.split(a["w_in"][l], np.cumsum([D] * 6), axis=1)
        put(_col_tiles(a["w_kv_mem"][l]))
        for w in (xq, q, k, v, zx, zy):
            put(_col_tiles(w))
        for branch, w in ((2, "w_proj_mem"), (0, "w_proj_attn"), (1, "w_proj_lru")):
            put(_col_tiles(g[:, branch * D:(branch + 1) * D]))
            put(_col_tiles(a[w][l]))
        put(_col_tiles(a["w_out"][l]))
        ups, downs = _col_tiles(a["w_mlp_up"][l]), _row_tiles(a["w_mlp_down"][l])
        put(ups[0:1])
        for j in range(A_UP):
            if j + 1 < A_UP:
                put(ups[j + 1:j + 2])
            put(downs[j:j + 1])
    assert at == DEPTH * A_TILES
    _block_b_tiles(a, put)
    assert at == N_TILES
    return stream


def _rope_tables():
    half = A_HD // 2
    inv = (np.float32(1.0) / (np.float32(10000.0) ** (np.arange(half, dtype=np.float32) / np.float32(half)))).astype(np.float32)
    ang = np.arange(S, dtype=np.float32)[:, None] * inv[None, :]
    both = [f(ang).astype(np.float32).reshape(TB, P, half).transpose(1, 0, 2) for f in (np.cos, np.sin)]
    return [np.ascontiguousarray(t) for t in both]


def _params(a):
    par = np.zeros((DEPTH + 1, P, N_PAR), np.float32)

    def put(l, table, name, v):
        par[l, :, table[name]:table[name] + v.shape[1]] = v

    for l in range(DEPTH):
        init = 0.8 - 0.6 * math.exp(-0.3 * l)
        for name, v in (("mix_pre", a["norm_mix_pre"]), ("mlp_pre", a["norm_mlp_pre"]), ("mem", a["norm_mem"]),
                        ("b_gate", a["b_gate"]), ("conv_w", a["conv_w"]), ("conv_b", a["conv_b"]), ("rg_ba", a["rg_ba"]),
                        ("rg_bi", a["rg_bi"]), ("rg_lambda", a["rg_lambda"]), ("subln", a["diff_subln"])):
            put(l, PA, name, _feat_vector(v[l]))
        put(l, PA, "one_minus_init", np.full((P, 1), 1.0 - init, np.float32))
        put(l, PA, "init", np.full((P, 1), init, np.float32))
        for name, pair in (("lambda_q", ("lambda_q1", "lambda_q2")), ("lambda_k", ("lambda_k1", "lambda_k2"))):
            row = np.concatenate([a[n][l] for n in pair])
            put(l, PA, name, np.broadcast_to(row, (P, 128)))
    _block_b_params(a, lambda name, v: put(DEPTH, PB, name, v))
    return par


B_SIZES = [256] * 9 + [4, 256, 64, 64, 256, 32, 8]


def _block_b_tiles(a, put):
    (sq, sk, sv, mq, mk, mv, fq, fk, fv, ff, dq, dk, dv, iq, ik, iw) = np.split(a["w_in_2"][0], np.cumsum(B_SIZES)[:-1], axis=1)
    pad = lambda w, n: np.concatenate([w, np.zeros((D, n - w.shape[1]), np.float32)], axis=1)
    put(_col_tiles(pad(np.concatenate([sq, sk, mq, mk, fq, fk, dq, dk, dk, ik, ik, ik, ik, iq], axis=1), N_FEAT * 256)))
    put(_col_tiles(pad(np.concatenate([sv, mv, fv, dv, iw, ff], axis=1), N_TOK * 256)))
    for b in range(4):
        put(_col_tiles(a["w_gate_2"][0, b]))
        put(_row_tiles(a["w_branch_2"][0, b]))
    put(_col_tiles(a["w_out_2"][0]))
    gs, us = _col_tiles(a["w_up_2"][0][:, :B_FF]), _col_tiles(a["w_up_2"][0][:, B_FF:])
    downs = _row_tiles(a["w_down_2"][0])
    put(gs[0:1])
    put(us[0:1])
    for j in range(B_UP):
        if j + 1 < B_UP:
            put(gs[j + 1:j + 2])
            put(us[j + 1:j + 2])
        put(downs[j:j + 1])


def _block_b_params(a, put):
    put("mix", _feat_vector(a["norm_mix_g_2"][0]))
    put("ffn", _feat_vector(a["norm_ffn_g_2"][0]))
    put("fox_b", np.broadcast_to(a["fox_b_f_2"][0], (P, 4)))
    for name, v in (("conv_w", a["conv_w_2"][0]), ("conv_b", a["conv_b_2"][0])):
        v = v.reshape(-1, 2, B_UP, 2, P).transpose(0, 2, 1, 3, 4)
        put(name, _feat_vector(v))


def _masks():
    p, j = np.arange(P)[:, None], np.arange(P)[None, :]
    one = np.ones((P, P))
    m = [p <= j, one, -(p >= j).astype(float), -one, p < j, np.where(p < j, 0.0, NEG), np.where(j <= p, 0.0, NEG)]
    return np.ascontiguousarray(np.stack(m, axis=1).astype(np.float32).reshape(P, 7 * P))


def _t5_constants():
    n = 255 - np.arange(512)
    near = np.maximum(n, 1).astype(np.float32)
    large = 16 + (np.log(near / np.float32(16)) / np.float32(math.log(128 / 16)) * np.float32(16)).astype(np.int32)
    bucket = np.where(np.maximum(n, 0) < 16, np.maximum(n, 0), np.minimum(large, 31))
    rows = np.zeros((33, 512), np.float32)
    rows[bucket, np.arange(512)] = 1.0
    rows[32] = np.where(n < 0, NEG, 0.0)
    return rows


def kernel(**a):
    import concourse.bacc as bacc
    from concourse.bass_utils import run_bass_kernel_spmd

    a = {k: np.asarray(v) for k, v in a.items()}

    def tok(v):
        return np.ascontiguousarray(v.reshape(TB, P, -1).transpose(1, 0, 2))

    cos, sin = _rope_tables()
    arrays = {
        "stream": _weight_stream(a), "x_in": tok(a["x"][0]), "mem_in": tok(a["mem"][0]).reshape(P, TB * D), "params": _params(a),
        "post_gain": np.ascontiguousarray(np.broadcast_to(
            np.stack([a["norm_mix_post"], a["norm_mlp_post"]], 1).reshape(DEPTH, 1, 2 * D), (DEPTH, P, 2 * D))),
        "rg_w": np.ascontiguousarray(np.stack([a["rg_wa"], a["rg_wi"]], 1).transpose(0, 3, 1, 2, 4).reshape(DEPTH, P, 2048)),
        "cos_in": cos, "sin_in": sin, "ident_in": np.eye(P, dtype=np.float32), "masks_in": _masks(),
        "t5_in": np.concatenate([_t5_constants(), np.concatenate([a["t5_bias_2"], np.ones((1, 8), np.float32)])], axis=1),
        "final_gain": np.ascontiguousarray(np.broadcast_to(a["norm_final_g_2"], (P, D))),
    }
    nc = bacc.Bacc("TRN2", target_bir_lowering=False, num_devices=1)
    args = {k: nc.dram_tensor(k, v.shape, mybir.dt.from_np(v.dtype), kind="ExternalInput").ap() for k, v in arrays.items()}
    args["out"] = nc.dram_tensor("out", (P, TB, D), F32, kind="ExternalOutput").ap()
    build(nc, **args)
    got = run_bass_kernel_spmd(nc, [arrays], core_ids=[0]).results[0]["out"]
    return got.transpose(1, 0, 2).reshape(1, S, D)
```

```python
import math
from contextlib import ExitStack

import numpy as np

import concourse.bass as bass
from concourse import mybir
from concourse.alu_op_type import AluOpType as ALU

ACT = mybir.ActivationFunctionType
AX = mybir.AxisListType
F32 = mybir.dt.float32
F32R = mybir.dt.float32r
BF16 = mybir.dt.bfloat16

P = 128
D = 1024
S = 256
DEPTH = 2
KC = D // P
TB = S // P
EPS = 1e-6
NEG = -1e30
TILE = 2048
RAW, HI, LO = 4, 4, 2

A_HEADS, A_HD = 8, 64
X_HEADS, X_HD = 4, 256
A_FF = 4 * D
A_UP = A_FF // 256
B_FF = 2816
B_UP = B_FF // 256
B_HD = 64
B_TOPK = min(256, S // 4)
IDX_HEADS, IDX_HD = 8, 32
REPLACED = -3e38
OUTSIDE = -1e38

T_K, T_V, T_XQ, T_QK, T_AV, T_ZX, T_ZY = 0, 4, 8, 12, 20, 24, 28
T_GM, T_PM, T_GA, T_PA, T_GL, T_PL, T_OUT = 32, 36, 40, 44, 48, 52, 56
T_UP = 60
A_TILES = T_UP + 2 * A_UP
N_FEAT, N_TOK = 9, 4
T2_TOK = N_FEAT
T2_GATE = T2_TOK + N_TOK
T2_OUT = T2_GATE + 4 * 5
T2_FFN = T2_OUT + 4
B_TILES = T2_FFN + 3 * B_UP
N_TILES = DEPTH * A_TILES + B_TILES
SKEW = 3 * P
assert A_TILES % RAW == 0 and N_TILES % 2 == 0

_ACT_TILES = [t for t in range(T_UP) if not (T_QK <= t < T_AV or T_PM <= t < T_GA or T_PA <= t < T_GL or T_PL <= t)]
_DVE_TILES = [t for t in range(T_UP - 1) if t not in _ACT_TILES]
ACT_EVAC = {t: n + 1 for n, t in enumerate(_ACT_TILES)}
DVE_EVAC = {t: n + 1 for n, t in enumerate(_DVE_TILES)}
N_ACT_EVAC, N_DVE_EVAC = len(_ACT_TILES), len(_DVE_TILES)

def _columns(*sizes):
    at, out = 0, {}
    for name, n in sizes:
        out[name] = at
        at += n
    return out, at


PA, _na = _columns(("mix_pre", 8), ("mlp_pre", 8), ("mem", 8), ("b_gate", 24), ("conv_w", 32), ("conv_b", 8),
                   ("rg_ba", 8), ("rg_bi", 8), ("rg_lambda", 8), ("subln", 1), ("one_minus_init", 1), ("init", 1),
                   ("lambda_q", 128), ("lambda_k", 128))
PB, _nb = _columns(("mix", 8), ("ffn", 8), ("fox_b", 4), ("conv_w", 3 * 4 * B_UP), ("conv_b", 4 * B_UP))
N_PAR = max(_na, _nb)

DVE_STEPS, ACT_STEPS = 53, 1


def build(nc, stream, x_in, mem_in, params, post_gain, rg_w, cos_in, sin_in, ident_in, masks_in, t5_in,
          final_gain, out):
    mem_normed = nc.dram_tensor("mem_normed", (P, KC * S), F32, kind="Internal").ap()
    t5_rows = nc.dram_tensor("t5_rows", (8, 512), F32, kind="Internal").ap()
    t5_skewed = nc.dram_tensor("t5_skewed", (8, P, SKEW + 1), F32, kind="Internal").ap()
    with ExitStack() as ctx:
        def sb(name, shape, dt=F32):
            return ctx.enter_context(nc.sbuf_tensor(name, shape, dt))

        def sem(name):
            return ctx.enter_context(nc.semaphore(name))

        w_raw = sb("w_raw", [P, RAW, TILE])
        w_hi = sb("w_hi", [P, HI, TILE], F32R)
        w_lo = sb("w_lo", [P, LO, TILE], F32R)
        raw_loaded = [sem(f"raw_loaded{s}") for s in range(RAW)]
        hi_ready = sem("hi_ready")
        lo_ready = sem("lo_ready")
        half_done = sem("half_done")
        tile_done = sem("tile_done")

        x = sb("x", [P, TB, D])
        op_hi = [sb("opA_hi", [P, KC, S], F32R), sb("opB_hi", [P, KC, S], F32R)]
        op_lo = [sb("opA_lo", [P, KC, S], F32R), sb("opB_lo", [P, KC, S], F32R)]
        B = [sb(f"B{n}", [P, 2080 if n == 0 else 2048]) for n in range(7)]
        merged = sb("merged", [P, 2048])
        gate = sb("gate", [P, 2048])
        expd = sb("expd", [P, 4, 256])
        probs_t = sb("probs_t", [P, 512])
        par = sb("par", [P, N_PAR])
        cos = sb("cos", [P, TB, 32])
        sin = sb("sin", [P, TB, 32])
        ident = sb("ident", [P, P])
        small = sb("small", [P, 96])
        rowmask = sb("rowmask", [P, P], BF16)
        colmask = sb("colmask", [P, 64], BF16)
        diag = sb("diag", [P, TB, P])
        eps = sb("eps", [P, 1])
        psum = ctx.enter_context(nc.psum_tensor("psum", [P, 8, 512], F32))

        def tok(buf):
            return buf[:, 0:2048].rearrange("p (b f) -> p b f", b=TB)

        def feat(buf):
            return buf[:, 0:2048].rearrange("p (c t) -> p c t", c=KC)

        k_mem, v_mem, q_t, k_t, v_a, q_mem, o_a = feat(B[0]), tok(B[1]), feat(B[2]), feat(B[3]), tok(B[4]), feat(B[5]), tok(B[6])
        zx = B[0][:, :].rearrange("p (c t) -> p c t", c=KC)
        xc, gz = feat(B[1]), feat(B[5])
        r_g, i_g, t_g, lru = feat(B[2]), feat(B[3]), feat(B[4]), feat(B[6])
        rgw = B[0][:, 0:2048].rearrange("p (g c d) -> p g c d", g=2, c=KC)
        y_tok = tok(B[1])
        gains = tok(B[4])
        relu_u, squared = B[2][:, 0:1024].rearrange("p (b n) -> p b n", b=2), B[3][:, 0:1024].rearrange("p (b n) -> p b n", b=2)
        rot = merged[:, 0:1024].rearrange("p (b n) -> p b n", b=2)
        rope_a, rope_b = gate[:, 0:512], gate[:, 512:1024]

        def sm(a, n=1):
            return small[:, a:a + n]
        SS, VAR, SD, RS, NMAX, ZSUM, RZ, R2 = 0, 16, 32, 48, 64, 68, 72, 76
        NLAM, GSUB, SP_POS, SP_NEG = 78, 79, 80, 88
        prep = sb("prep", [P, 160])

        ident_loaded, rope_in, x_loaded, par_in, mem_loaded, rgw_in, gain_in, out_done = (sem(n) for n in (
            "ident_loaded", "rope_in", "x_loaded", "par_in", "mem_loaded", "rgw_in", "gain_in", "out_done"))
        mem_half_in = [sem(f"mem_half_in{b}") for b in range(TB)]
        mem_copied, mem_stored = sem("mem_copied"), sem("mem_stored")
        norm_ss, sub_ss, norm_sd, norm_x = (sem(n) for n in ("norm_ss", "sub_ss", "norm_sd", "norm_x"))
        turned = sem("turned")
        op_hi_done = sem("op_hi_done")
        op_ready = sem("op_ready")
        act_evac, dve_evac = sem("act_evac"), sem("dve_evac")
        par_d, par_a = sem("par_d"), sem("par_a")
        rope_turned, rope_evac, rope_ready = sem("rope_turned"), sem("rope_evac"), sem("rope_ready")
        x_scores, x_max, x_exp, x_probs, x_turned, x_pt, x_out = (sem("x_" + n) for n in (
            "scores", "max", "exp", "probs", "turned", "pt", "out"))
        d_scores, d_max, d_exp, d_probs, d_turned, d_pt, d_out, d_kept = (sem("d_" + n) for n in (
            "scores", "max", "exp", "probs", "turned", "pt", "out", "kept"))
        conv_done, rg_done, rg_evac, lru_ta, lru_v, lru_s, lru_y, gelu_done = (sem(n) for n in (
            "conv_done", "rg_done", "rg_evac", "lru_ta", "lru_v", "lru_s", "lru_y", "gelu_done"))
        lru_u = sem("lru_u")
        masks_ready = sem("masks_ready")
        out_ss, post_ss, post_var, post_sd, post_gained = (sem(n) for n in ("out_ss", "post_ss", "post_var", "post_sd", "post_gained"))
        x_ready = sem("x_ready")
        squared_done, ffn_hi = sem("squared_done"), sem("ffn_hi")
        zx_padded = sem("zx_padded")
        mem_gate, merged_part = sem("mem_gate"), sem("merged_part")
        relu_done, up_used, ffn_ready, ffn_used = sem("relu_done"), sem("up_used"), sem("ffn_ready"), sem("ffn_used")
        dve_step, act_step, rs_ready = sem("dve_step"), sem("act_step"), sem("rs_ready")

        MEM_OP, MIX_OP, X_OP, SUB_OP, LRU_OP, OUT_OP, MLP_OP, N_OPS = 0, 1, 2, 3, 4, 5, 6, 7
        B_MIX, B_BRANCH, B_OUT, B_FFN = 0, 4, 8, 12
        MIX, SUB, MLP, N_NORMS = 1, 2, 3, 3
        OUT_BANKS = (3, 0)
        NORM_AT, NORM_COUNT = {MIX: 2, SUB: 4, MLP: 5}, 5

        f_b = [feat(B[0])[:, c, :] for c in range(8)] + [feat(B[1])[:, c, :] for c in range(8)] \
            + [B[2][:, c * S:(c + 1) * S] for c in range(2)]
        SB_Q, SB_K, MB_Q, MB_K, FX_Q, FX_K, DS_Q, DS_K, IX_K, IX_Q = 0, 2, 4, 6, 8, 10, 12, 14, 15, 16
        v_b = tok(B[3])
        V_COL, W_COL, F_COL = (0, 256, 512, 768), 832, 840
        bias_b = [B[4 + h // 4][:, (h % 4) * 512:(h % 4 + 1) * 512].rearrange("p (b n) -> p b n", b=TB) for h in range(8)]
        index = B[2][:, 512:1024].rearrange("p (b n) -> p b n", b=TB)
        minus_c_row = B[2][:, 1024:2048].rearrange("p (h n) -> p h n", h=4)
        log_f_wide = merged[:, 0:1024].rearrange("p (a n) -> p a n", n=P)
        up_to, ones_p, neg_from, neg_all, before01, before_neg, causal = (
            B[6][:, n * P:(n + 1) * P] for n in range(7))
        log_f, c_col = prep[:, 16:24], prep[:, 24:32]
        padded = B[0][:, 0:2064].rearrange("p (s c t) -> p s c t", s=2, c=4)
        conved = B[1][:, 0:2048].rearrange("p (s c t) -> p s c t", s=2, c=4)
        gelu_g = B[2][:, 0:1024].rearrange("p (s n) -> p s n", s=2)
        gated = B[3][:, 0:1024].rearrange("p (s n) -> p s n", s=2)

        (t5_loaded, t5_rows_ready, t5_evac, t5_stored, t5_skewed_in, bias_in, b_masks_in, final_in) = (sem(n) for n in (
            "t5_loaded", "t5_rows_ready", "t5_evac", "t5_stored", "t5_skewed_in", "bias_in", "b_masks_in", "final_in"))
        b_ss, b_sd, b_x, b_turned, b_hi, b_ready = (sem("b_" + n) for n in (
            "ss", "sd", "x", "turned", "hi", "ready"))
        b_bank = sem("b_bank")
        gate_open = sem("gate_open")
        x_part, xb_ss, xb_sum, y_done = sem("x_part"), sem("xb_ss"), sem("xb_sum"), sem("y_done")
        b_evac_a, b_evac_d = sem("b_evac_a"), sem("b_evac_d")
        ix_scores, ix_relu, ix_added = sem("ix_scores"), sem("ix_relu"), sem("ix_added")
        f_in, f_ln, f_wide, c_sums, c_kept = (sem(n) for n in ("f_in", "f_ln", "f_wide", "c_sums", "c_kept"))
        sb_z, sb_ln, sb_masked, sb_summed, sb_w = (sem("sb_" + n) for n in ("z", "ln", "masked", "summed", "w"))
        s_scores, s_max, s_exp, s_probs, s_turned, s_pt = (sem("s_" + n) for n in (
            "scores", "max", "exp", "probs", "turned", "pt"))
        b_out = sem("b_out")
        b_mixed = sem("b_mixed")
        out_part, x_b = sem("out_part"), sem("x_b")
        pads_zero = sem("pads_zero")
        f_evac, f_conv, f_gelu, f_gated, f_hi, f_ready = (sem("f_" + n) for n in ("evac", "conv", "gelu", "gated", "hi", "ready"))
        b_step = sem("b_step")

        class Steps:
            def __init__(self, eng, s, per_layer):
                self.eng, self.s, self.per_layer, self.base, self.n = eng, s, per_layer, 0, 0

            def __call__(self, ins):
                ins.then_inc(self.s, 1)
                self.n += 1
                self.eng.wait_ge(self.s, self.base + self.n)

        block = ctx.enter_context(nc.Block())

        @block.sync
        def _(sp):
            for b in range(TB):
                sp.dma_start(tok(B[6])[:, b, :], mem_in[:, b * D:(b + 1) * D]).then_inc(mem_half_in[b], 16)
            for s in range(RAW):
                sp.dma_start(w_raw[:, s, :], stream[s]).then_inc(raw_loaded[s], 16)
            sp.wait_ge(t5_evac, 1)
            sp.dma_start(t5_rows, B[1][0:8, 1024:1536]).then_inc(t5_stored, 16)
            sp.wait_ge(t5_stored, 16)
            for h in range(8):
                row = bass.AP(tensor=t5_rows.tensor, offset=t5_rows.offset + h * 512, ap=[[0, P], [1, SKEW]])
                sp.dma_start(t5_skewed[h, :, 0:SKEW], row).then_inc(t5_skewed_in, 16)
            groups = N_TILES // RAW
            with sp.Fori(1, groups) as g:
                for s in range(RAW):
                    sp.wait_ge(lo_ready, g * RAW + (s - RAW + 1))
                    sp.dma_start(w_raw[:, s, :], stream[g * RAW + s]).then_inc(raw_loaded[s], 16)
            for t in range(groups * RAW, N_TILES):
                sp.wait_ge(lo_ready, t - RAW + 1)
                sp.dma_start(w_raw[:, t % RAW, :], stream[t]).then_inc(raw_loaded[t % RAW], 16)
            sp.wait_ge(out_done, TB * 16)

        @block.gpsimd
        def _(pool):
            def rest(t, s, first=False):
                pool.wait_ge(hi_ready, t + 1)
                if not first:
                    pool.wait_ge(tile_done, t - (LO - 1))
                nc.gpsimd.tensor_tensor(w_lo[:, s % LO, :], w_raw[:, s % RAW, :], w_hi[:, s % HI, :].bitcast(F32),
                                        ALU.subtract).then_inc(lo_ready, 1)

            for t in range(4):
                rest(t, t, t < LO)
            with pool.Fori(1, N_TILES // 4) as g:
                for s in range(4):
                    rest(g * 4 + s, s)
            for t in range(N_TILES // 4 * 4, N_TILES):
                rest(t, t)

        @block.tensor
        def _(pe):
            def passes(t, s, product, piece=None):
                pe.wait_ge(hi_ready, t + 1)
                pieces = [range(KC)] if piece is None else [(2 * g, 2 * g + 1) for g in range(KC // 2)]
                for g, ks in enumerate(pieces):
                    if piece is not None:
                        piece(g)
                    product(w_hi[:, s % HI, :], 0, ks, g == 0, False)
                    product(w_hi[:, s % HI, :], 1, ks, False, False)
                    if g == 0:
                        pe.wait_ge(lo_ready, t + 1)
                    ins = product(w_lo[:, s % LO, :], 0, ks, False, g == len(pieces) - 1)
                ins.then_inc(tile_done, 1)

            def col_feat(t, s, bank, op, piece=None):
                parts = (op_hi[op], op_lo[op])

                def product(w, a, ks, first, last):
                    w = w.rearrange("p (k n) -> p k n", k=KC)
                    for c in range(2):
                        for k in ks:
                            ins = nc.tensor.matmul(psum[:, bank, c * S:(c + 1) * S], w[:, k, c * P:(c + 1) * P],
                                                   parts[a][:, k, :], start=(first and c == 0 and k == 0),
                                                   stop=(last and k == KC - 1), skip_group_check=True)
                    return ins
                passes(t, s, product, piece)

            def col_tok(t, s, bank, op, piece=None):
                parts = (op_hi[op], op_lo[op])

                def product(w, a, ks, first, last):
                    w = w.rearrange("p (k n) -> p k n", k=KC)
                    for b in range(TB):
                        for k in ks:
                            ins = nc.tensor.matmul(psum[:, bank, b * 256:(b + 1) * 256], parts[a][:, k, b * P:(b + 1) * P],
                                                   w[:, k, :], start=(first and b == 0 and k == 0),
                                                   stop=(last and k == KC - 1), skip_group_check=True)
                    return ins
                passes(t, s, product, piece)

            def row_tok(t, s, slot, first_tile):
                parts = (op_hi[1], op_lo[1])

                def product(w, a, ks, first, last):
                    w = w.rearrange("p (k n) -> p k n", k=2)
                    for b in range(TB):
                        for n in range(2):
                            for k in range(2):
                                ins = nc.tensor.matmul(psum[:, 4 + 2 * b + n, :], parts[a][:, 2 * slot + k, b * P:(b + 1) * P],
                                                       w[:, k, n * 512:(n + 1) * 512], start=(first_tile and first and k == 0),
                                                       stop=False, skip_group_check=True)
                    return ins
                passes(t, s, product)

            def turn(src, signal, half_ready):
                for b in range(TB):
                    pe.wait_ge(norm_x if signal is turned else b_x, half_ready + b)
                    for c in range(KC):
                        ins = nc.tensor.matmul(psum[:, 4 + c // 2, (c % 2) * S + b * P:(c % 2) * S + (b + 1) * P],
                                               src[:, b, c * P:(c + 1) * P], diag[:, b, :], start=True, stop=True)
                        if b and c % 2:
                            ins.then_inc(signal, 1)

            def out_tile(t, s, op):
                pe.wait_ge(hi_ready, t + 1)
                pe.wait_ge(lo_ready, t + 1)
                for b in range(TB):
                    for i, (w, part) in enumerate(((w_hi[:, s % HI, :], op_hi), (w_hi[:, s % HI, :], op_lo), (w_lo[:, s % LO, :], op_hi))):
                        w = w.rearrange("p (k n) -> p k n", k=KC)
                        for k in range(KC):
                            ins = nc.tensor.matmul(psum[:, OUT_BANKS[b], 0:256], part[op][:, k, b * P:(b + 1) * P], w[:, k, :],
                                                   start=(i == 0 and k == 0), stop=(i == 2 and k == KC - 1))
                    ins.then_inc(tile_done if b else half_done, 1)

            def row_tok_end(t, s, slot):
                pe.wait_ge(hi_ready, t + 1)
                pe.wait_ge(lo_ready, t + 1)
                for b in range(TB):
                    for w, part in ((w_hi[:, s % HI, :], op_hi), (w_hi[:, s % HI, :], op_lo), (w_lo[:, s % LO, :], op_hi)):
                        w = w.rearrange("p (k n) -> p k n", k=2)
                        for n in range(2):
                            for k in range(2):
                                ins = nc.tensor.matmul(psum[:, 4 + 2 * b + n, :], part[1][:, 2 * slot + k, b * P:(b + 1) * P],
                                                       w[:, k, n * 512:(n + 1) * 512], start=False, stop=(k == 1),
                                                       skip_group_check=True)
                    ins.then_inc(tile_done if b else half_done, 1)

            pe.wait_ge(t5_loaded, 16)
            nc.tensor.matmul(psum[0:8, 0, :], B[1][0:33, 512:520], B[1][0:33, 0:512], start=True, stop=True).then_inc(t5_rows_ready, 1)
            turn(tok(B[6]), turned, 1)
            pe.wait_ge(t5_evac, 1)
            pe.wait_ge(masks_ready, 4)
            with pe.Fori(0, DEPTH) as l:
                T = l * A_TILES

                def ready(op, g=3):
                    pe.wait_ge(op_ready, l * (4 * N_OPS) + (4 * op + g + 1))

                def tile(t, product, op, piece=None):
                    if t >= 4:
                        if t - 4 in ACT_EVAC:
                            pe.wait_ge(act_evac, l * N_ACT_EVAC + ACT_EVAC[t - 4])
                        else:
                            pe.wait_ge(dve_evac, l * N_DVE_EVAC + DVE_EVAC[t - 4])
                    product(T + t, t, t % 4, op, piece)

                for t in range(T_K, T_V):
                    tile(t, col_feat, 0, (lambda g: ready(MEM_OP, g)) if t == T_K else None)
                pe.wait_ge(mem_copied, 1)
                turn(x, turned, l * NORM_COUNT + (NORM_AT[MIX] + 1))
                for t in range(T_V, T_XQ):
                    tile(t, col_tok, 0)
                ready(MIX_OP)
                for t in range(T_XQ, T_QK):
                    tile(t, col_feat, 1)

                def rope_turn(i):
                    pe.wait_ge(rope_ready, l * 8 + i + 1)
                    if i:
                        pe.wait_ge(rope_evac, l * 8 + i)
                    for c in range(2):
                        for b in range(TB):
                            ins = nc.tensor.transpose(psum[:, 5, c * S + b * P:c * S + (b + 1) * P],
                                                      rot[:, i % 2, b * 256 + c * P:b * 256 + (c + 1) * P], ident[:])
                    ins.then_inc(rope_turned, 1)

                def x_score(h):
                    pe.wait_ge(act_evac, l * N_ACT_EVAC + ACT_EVAC[T_XQ + 3])
                    for b in range(TB):
                        for k in range(2):
                            ins = nc.tensor.matmul(psum[:, 4, b * 256:(b + 1) * 256], q_mem[:, 2 * h + k, b * P:(b + 1) * P],
                                                   k_mem[:, 2 * h + k, :], start=(k == 0), stop=(k == 1))
                    ins.then_inc(x_scores, 1)

                def x_turn(h):
                    pe.wait_ge(x_probs, l * X_HEADS + h + 1)
                    for k in range(TB):
                        for b in range(TB):
                            ins = nc.tensor.transpose(psum[:, 6, k * 256 + b * P:k * 256 + (b + 1) * P],
                                                      expd[:, b, k * P:(k + 1) * P], ident[:])
                    ins.then_inc(x_turned, 1)

                def x_values(h):
                    pe.wait_ge(x_pt, l * X_HEADS + h + 1)
                    if h:
                        ready(X_OP, h - 1)
                    for c in range(2):
                        for k in range(TB):
                            ins = nc.tensor.matmul(psum[:, 7, c * S:(c + 1) * S], v_mem[:, k, h * X_HD + c * P:h * X_HD + (c + 1) * P],
                                                   probs_t[:, k * 256:(k + 1) * 256], start=(k == 0), stop=(k == 1))
                    ins.then_inc(x_out, 1)

                for i in range(8):
                    tile(T_QK + i, col_tok, 1)
                    if i:
                        rope_turn(i - 1)
                    if i % 2 == 0:
                        if i:
                            x_values(i // 2 - 1)
                        x_score(i // 2)
                    else:
                        x_turn(i // 2)
                tile(T_AV, col_tok, 1)
                rope_turn(7)
                x_values(3)
                for t in range(T_AV + 1, T_ZX):
                    tile(t, col_tok, 1)

                def d_score(h):
                    if h == 0:
                        pe.wait_ge(rope_evac, l * 8 + 8)
                    for m in range(2):
                        q = slice(64 * m, 64 * m + 64)
                        for b in range(TB):
                            n = (b + 1) * P
                            nc.tensor.matmul(psum[:, 4 + m, b * 256:b * 256 + n], q_t[q, h, b * P:(b + 1) * P], k_t[q, h, 0:n],
                                             start=True, stop=False, skip_group_check=True)
                            ins = nc.tensor.matmul(psum[:, 4 + m, b * 256 + n - 64:b * 256 + n], rowmask[64 * m:64 * m + 1, :],
                                                   colmask[64 * m:64 * m + 1, :], start=False, stop=True, skip_group_check=True)
                    ins.then_inc(d_scores, 1)

                def d_turn(h):
                    pe.wait_ge(d_probs, l * A_HEADS + h + 1)
                    for b in range(TB):
                        nc.tensor.transpose(psum[:, 6, b * P:(b + 1) * P], expd[:, b, 0:P], ident[:])
                    nc.tensor.transpose(psum[:, 6, 256:384], expd[:, 1, P:2 * P], ident[:]).then_inc(d_turned, 1)

                def d_values(h):
                    pe.wait_ge(d_pt, l * A_HEADS + h + 1)
                    pe.wait_ge(act_evac, l * N_ACT_EVAC + ACT_EVAC[T_AV + 3])
                    if h:
                        pe.wait_ge(d_kept, l * A_HEADS + h)
                    v = slice(h * P, (h + 1) * P)
                    nc.tensor.matmul(psum[:, 7, 0:P], probs_t[:, 0:P], v_a[:, 0, v], start=True, stop=True)
                    nc.tensor.matmul(psum[:, 7, P:2 * P], probs_t[:, P:2 * P], v_a[:, 0, v], start=True, stop=False)
                    nc.tensor.matmul(psum[:, 7, P:2 * P], probs_t[:, 256:384], v_a[:, 1, v], start=False, stop=True).then_inc(d_out, 1)

                for h in range(A_HEADS):
                    t = T_ZX + 2 * h
                    d_score(h)
                    if t == T_PM:
                        ready(X_OP)
                    tile(t, col_feat, 0 if t >= T_PM else 1)
                    d_turn(h)
                    tile(t + 1, col_feat, 0 if t >= T_PM else 1)
                    d_values(h)

                def rg(c):
                    if c == 0:
                        pe.wait_ge(rgw_in, l * 16 + 16)
                    if c == 3:
                        pe.wait_ge(d_kept, l * A_HEADS + A_HEADS)
                    if c >= 4:
                        pe.wait_ge(rg_evac, l * KC + c - 3)
                    for g in range(2):
                        ins = nc.tensor.matmul(psum[:, 4 + c % 4, g * S:(g + 1) * S], rgw[:, g, c, :], xc[:, c, :], start=True, stop=True)
                    ins.then_inc(rg_done, 1)

                for n in range(2):
                    tile(T_GA + n, col_feat, 1)
                    for c in range(4):
                        rg(4 * n + c)
                tile(T_GA + 2, col_feat, 1)
                pe.wait_ge(norm_x, l * NORM_COUNT + (NORM_AT[SUB] + 1))
                pe.wait_ge(rg_evac, l * KC + KC)
                for c in range(KC):
                    for b in range(TB):
                        ins = nc.tensor.transpose(psum[:, 4 + c // 2, (c % 2) * S + b * P:(c % 2) * S + (b + 1) * P],
                                                  o_a[:, b, c * P:(c + 1) * P], ident[:])
                    if c % 2:
                        ins.then_inc(turned, 1)
                tile(T_GA + 3, col_feat, 1)
                ready(SUB_OP)
                for t in range(T_PA, T_GL):
                    tile(t, col_feat, 0)
                for t in range(T_GL, T_PL):
                    tile(t, col_feat, 1)
                ready(LRU_OP)
                for t in range(T_PL, T_OUT):
                    tile(t, col_feat, 0)
                for t in range(T_OUT, T_UP - 1):
                    tile(t, col_tok, 1, (lambda g: ready(OUT_OP, g)) if t == T_OUT else None)
                pe.wait_ge(dve_evac, l * N_DVE_EVAC + DVE_EVAC[T_OUT])
                out_tile(T + (T_UP - 1), T_UP - 1, 1)

                turn(x, turned, l * NORM_COUNT + (NORM_AT[MLP] + 1))

                def up(j, t, s, slot, first=False):
                    if not first:
                        pe.wait_ge(relu_done, l * A_UP + j - 1)
                    col_feat(T + t, s, slot, 0, (lambda g: ready(MLP_OP, g)) if first == "operand" else None)

                def down(j, t, s, slot, first=False):
                    pe.wait_ge(ffn_ready, l * A_UP + j + 1)
                    row_tok(T + t, s, slot, first)

                up(0, T_UP, T_UP, 0, "operand")
                up(1, T_UP + 1, T_UP + 1, 1, True)
                down(0, T_UP + 2, T_UP + 2, 0, True)
                with pe.Fori(0, A_UP // 2 - 1) as i:
                    t0 = T_UP + 3
                    up(i * 2 + 2, i * 4 + t0, t0, 0)
                    down(i * 2 + 1, i * 4 + t0 + 1, t0 + 1, 1)
                    up(i * 2 + 3, i * 4 + t0 + 2, t0 + 2, 1)
                    down(i * 2 + 2, i * 4 + t0 + 3, t0 + 3, 0)
                pe.wait_ge(ffn_ready, l * A_UP + A_UP)
                row_tok_end(T + (A_TILES - 1), A_TILES - 1, 1)

            T0 = DEPTH * A_TILES

            def row_feat(t, s):
                parts = (op_hi[1], op_lo[1])
                pe.wait_ge(hi_ready, t + 1)
                pe.wait_ge(lo_ready, t + 1)
                for n in range(4):
                    for i, (w, a) in enumerate(((w_hi[:, s % HI, :], 0), (w_hi[:, s % HI, :], 1), (w_lo[:, s % LO, :], 0))):
                        w = w.rearrange("p (k n) -> p k n", k=2)
                        for c in (2 * n, 2 * n + 1):
                            for k in range(2):
                                ins = nc.tensor.matmul(psum[:, n, (c % 2) * S:(c % 2 + 1) * S], w[:, k, c * P:(c + 1) * P],
                                                       parts[a][:, k, :], start=(i == 0 and c % 2 == 0 and k == 0),
                                                       stop=(i == 2 and k == 1), skip_group_check=True)
                    ins.then_inc(tile_done if n == 3 else b_bank, 1)

            def b_piece(op):
                return lambda g: pe.wait_ge(b_ready, op + g + 1)

            turn(x, b_turned, 1)
            for t in range(N_FEAT + N_TOK):
                if t >= 4:
                    pe.wait_ge(b_evac_a, t - 3)
                (col_feat if t < N_FEAT else col_tok)(T0 + t, t, t % 4, 0, b_piece(B_MIX) if t == 0 else None)

            def gate_tile(b, n):
                t = T2_GATE + 5 * b + n
                if b == 0:
                    pe.wait_ge(b_evac_a, N_FEAT + N_TOK)
                else:
                    pe.wait_ge(b_evac_d, 4 * (b - 1) + n + 1)
                col_feat(T0 + t, t, n, 0)

            def index_scores(h):
                if h >= 4:
                    pe.wait_ge(ix_relu, h - 3)
                r = slice(32 * (h % 4), 32 * (h % 4) + 32)
                for b in range(TB):
                    ins = nc.tensor.matmul(psum[:, 4 + h % 4, b * 256:b * 256 + (b + 1) * P], f_b[IX_Q + h // 4][r, b * P:(b + 1) * P],
                                           f_b[IX_K][r, 0:(b + 1) * P], start=True, stop=True)
                ins.then_inc(ix_scores, 1)

            pe.wait_ge(b_evac_a, N_FEAT + N_TOK)
            pe.wait_ge(b_masks_in, 16)
            for h in range(4):
                index_scores(h)
            gate_tile(0, 0)
            for h in range(4, IDX_HEADS):
                index_scores(h)
            pe.wait_ge(ix_relu, IDX_HEADS)

            def c_rows():
                pe.wait_ge(f_wide, 1)
                for h in range(4):
                    row = psum[:, 4 + 2 * (h // 2), (h % 2) * S:(h % 2 + 1) * S]
                    nc.tensor.matmul(row, log_f_wide[:, h, :], B[6][:, 0:2 * P], start=True, stop=False)
                    ins = nc.tensor.matmul(row[:, P:2 * P], log_f_wide[:, 4 + h, :], up_to, start=False, stop=True)
                ins.then_inc(c_sums, 1)

            def c_columns():
                nc.tensor.matmul(psum[:, 5, 0:4], up_to, log_f[:, 0:4], start=True, stop=True)
                nc.tensor.matmul(psum[:, 5, 4:8], ones_p, log_f[:, 0:4], start=True, stop=False)
                nc.tensor.matmul(psum[:, 5, 4:8], up_to, log_f[:, 4:8], start=False, stop=True).then_inc(c_sums, 1)

            def rows_of(h):
                return slice(64 * (h % 2), 64 * (h % 2) + 64)

            def values(b, h):
                if h == 0 and b:
                    pe.wait_ge(b_ready, B_BRANCH + b)
                col = V_COL[b] + (64 * h if b < 3 else 0)
                o = psum[rows_of(h), 7, (h // 2) * S:(h // 2 + 1) * S]
                nc.tensor.matmul(o, v_b[:, 0, col:col + 64], probs_t[:, 0:256], start=True, stop=False, skip_group_check=True)
                nc.tensor.matmul(o[:, P:2 * P], v_b[:, 1, col:col + 64], probs_t[:, 256:384], start=False, stop=True,
                                 skip_group_check=True).then_inc(b_out, 1)

            def sb_logits(h):
                r = rows_of(h)
                k, q = f_b[SB_K + h // 2], f_b[SB_Q + h // 2]
                nc.tensor.matmul(psum[:, 4 + h % 2, 0:256], k[r, 0:P], q[r, :], start=True, stop=False, skip_group_check=True)
                nc.tensor.matmul(psum[:, 4 + h % 2, 256:384], k[r, P:2 * P], q[r, P:2 * P], start=False, stop=False,
                                 skip_group_check=True).then_inc(sb_z, 1)

            def sb_sums(h):
                pe.wait_ge(sb_masked, h + 1)
                m = expd[:, 2 * (h % 2):2 * (h % 2) + 2, :].rearrange("p a n -> p (a n)")
                z = psum[:, 4 + h % 2, :]
                for dst, w, src in ((z[:, 0:P], ident[:], before_neg), (z[:, 256:384], ident[:], before_neg),
                                    (z[:, 0:256], neg_from, m[:, 0:256]), (z[:, P:256], neg_all, m[:, 256:384]),
                                    (z[:, 256:384], neg_from, m[:, 256:384])):
                    ins = nc.tensor.matmul(dst, w, src, start=False, stop=True, skip_group_check=True)
                ins.then_inc(sb_summed, 1)

            sb_logits(0)
            for h in range(4):
                if h < 3:
                    gate_tile(0, h + 1)
                else:
                    c_rows()
                sb_sums(h)
                if h < 3:
                    sb_logits(h + 1)
                pe.wait_ge(sb_w, h + 1)
                values(0, h)
            c_columns()

            def s_score(b, h):
                g = 4 * (b - 1) + h
                if g >= 2:
                    pe.wait_ge(s_probs, g - 1)
                r = rows_of(h)
                q = f_b[(None, MB_Q, FX_Q, DS_Q)[b] + h // 2]
                k = f_b[DS_K] if b == 3 else f_b[(None, MB_K, FX_K)[b] + h // 2]
                for u in range(TB):
                    ins = nc.tensor.matmul(psum[:, 4 + h % 2, u * 256:u * 256 + (u + 1) * P], q[r, u * P:(u + 1) * P],
                                           k[r, 0:(u + 1) * P], start=True, stop=True)
                ins.then_inc(s_scores, 1)

            def s_turn(b, h):
                g = 4 * (b - 1) + h
                pe.wait_ge(s_probs, g + 1)
                e = 2 * (h % 2)
                for u in range(TB):
                    nc.tensor.transpose(psum[:, 6, u * P:(u + 1) * P], expd[:, e + u, 0:P], ident[:])
                nc.tensor.transpose(psum[:, 6, 256:384], expd[:, e + 1, P:2 * P], ident[:]).then_inc(s_turned, 1)

            def branch_product(b):
                pe.wait_ge(b_evac_a, N_FEAT + N_TOK + 4 * (b + 1))
                if b:
                    pe.wait_ge(b_evac_d, 4 * b)
                pe.wait_ge(b_ready, B_BRANCH + b + 1)
                t = T2_GATE + 5 * b + 4
                row_feat(T0 + t, t)

            for b in range(1, 4):
                if b == 1:
                    branch_product(0)
                    pe.wait_ge(c_kept, 2)
                    s_score(1, 0)
                else:
                    s_score(b, 0)
                    branch_product(b - 1)
                for h in range(4):
                    gate_tile(b, h)
                    s_turn(b, h)
                    if h < 3:
                        s_score(b, h + 1)
                    pe.wait_ge(s_pt, 4 * (b - 1) + h + 1)
                    values(b, h)
            branch_product(3)

            for n in range(4):
                pe.wait_ge(b_evac_d, 12 + n + 1)
                t = T2_OUT + n
                if n < 3:
                    col_tok(T0 + t, t, n, 0, b_piece(B_OUT) if n == 0 else None)
                else:
                    pe.wait_ge(x_part, 1)
                    out_tile(T0 + t, t, 0)

            turn(x, b_turned, 3)

            def f_up(j):
                t = T2_FFN + (0 if j == 0 else 2 + 3 * (j - 1))
                for n in range(2):
                    if j >= 2:
                        pe.wait_ge(f_evac, 2 * (j - 2) + n + 1)
                    col_feat(T0 + t + n, t + n, 2 * (j % 2) + n, 0, b_piece(B_FFN) if j == n == 0 else None)

            def f_down(j):
                t = T2_FFN + 3 * (j + 1) + 1 if j < B_UP - 1 else B_TILES - 1
                pe.wait_ge(f_ready, j + 1)
                if j < B_UP - 1:
                    row_tok(T0 + t, t, j % 2, j == 0)
                else:
                    row_tok_end(T0 + t, t, j % 2)

            f_up(0)
            for j in range(1, B_UP):
                f_up(j)
                f_down(j - 1)
            f_down(B_UP - 1)

        @block.scalar
        def _(act):
            act.dma_start(ident[:], ident_in).then_inc(ident_loaded, 16)
            act.dma_start(par[:], params[0]).then_inc(par_in, 16)
            act.dma_start(B[1][0:33, 0:520], t5_in).then_inc(t5_loaded, 16)
            act.preload_act_table_set("sqrt_and_others")
            step = Steps(act, act_step, ACT_STEPS)

            def squares(b, src, col, signal):
                nc.scalar.activation(tok(gate)[:, b, :], src, ACT.Square, accum_out=sm(SS + col + b)).then_inc(signal, 1)

            def norm_root(b, src, col, ss, sd):
                squares(b, src, col, ss[0])
                act.wait_ge(*ss)
                root(sm(SD + col + b), sm(SS + col + b), D, sd)

            def root(dst, src, n, signal):
                nc.scalar.activation(dst, src, ACT.Sqrt, scale=1.0 / n, bias=eps[:]).then_inc(signal, 1)

            def operand_hi(which, turns, signal, ready, gain):
                for c in range(KC):
                    if c % 2 == 0:
                        act.wait_ge(signal, turns + c // 2 + 1)
                    nc.scalar.activation(op_hi[which][:, c, :], psum[:, 4 + c // 2, (c % 2) * S:(c % 2 + 1) * S],
                                         ACT.Identity, scale=gain(c)).then_inc(ready, 1)

            act.wait_ge(masks_ready, 1)
            for b in range(TB):
                act.wait_ge(mem_half_in[b], 16)
                norm_root(b, tok(B[6])[:, b, :], 0, (norm_ss, b + 1), norm_sd)
            act.dma_start(x[:], x_in).then_inc(x_loaded, 16)
            act.dma_start(cos[:], cos_in).then_inc(rope_in, 16)
            act.dma_start(sin[:], sin_in).then_inc(rope_in, 16)
            act.wait_ge(par_in, 16)
            operand_hi(0, 0, turned, op_hi_done, lambda c: par[:, PA["mem"] + c:PA["mem"] + c + 1])
            act.wait_ge(op_ready, 4)
            nc.scalar.activation(B[6][:], psum[:, 4:8, :].rearrange("p a n -> p (a n)"), ACT.Identity).then_inc(mem_copied, 1)
            act.wait_ge(mem_copied, 1)
            act.dma_start(mem_normed, B[6][:]).then_inc(mem_stored, 16)

            with act.Fori(0, DEPTH) as l:
                T = l * A_TILES
                step.base, step.n = l * ACT_STEPS, 0

                def empty(t, dst, scale=1.0):
                    act.wait_ge(tile_done, T + t + 1)
                    src = psum[:, t % 4, :].rearrange("p (a n) -> p a n", a=2)
                    nc.scalar.activation(dst, src, ACT.Identity, scale=scale).then_inc(act_evac, 1)

                def empty_gate(t, func, branch, n):
                    act.wait_ge(tile_done, T + t + 1)
                    for c in range(2):
                        col = PA["b_gate"] + branch * KC + 2 * n + c
                        ins = nc.scalar.activation(feat(gate)[:, 2 * n + c, :], psum[:, t % 4, c * S:(c + 1) * S], func,
                                                   bias=par[:, col:col + 1])
                    ins.then_inc(act_evac, 1)

                def turns(norm):
                    return l * (4 * N_NORMS) + 4 * norm

                for b in range(TB):
                    act.wait_ge(x_ready, l * 4 + b + 1)
                    norm_root(b, x[:, b, :], 2, (norm_ss, l * 4 + (b + 3)), norm_sd)
                act.wait_ge(par_d, l + 1)
                step(nc.scalar.activation(prep[:, 0:8], prep[:, 0:8], ACT.Exp))
                nc.scalar.activation(prep[:, 16:18], prep[:, 8:10], ACT.Exp).then_inc(par_a, 1)
                nc.scalar.activation(prep[:, 0:8], prep[:, 0:8], ACT.Ln, bias=1.0).then_inc(par_a, 1)

                for n in range(4):
                    empty(T_K + n, k_mem[:, 2 * n:2 * n + 2, :])
                operand_hi(1, turns(MIX), turned, op_hi_done, lambda c: par[:, PA["mix_pre"] + c:PA["mix_pre"] + c + 1])
                act.wait_ge(t5_stored, 16)
                for n in range(4):
                    empty(T_V + n, v_mem[:, :, n * 256:(n + 1) * 256])
                for n in range(4):
                    empty(T_XQ + n, q_mem[:, 2 * n:2 * n + 2, :], X_HD ** -0.5)

                def empty_rope(i):
                    act.wait_ge(rope_turned, l * 8 + i + 1)
                    dst, scale = (q_t, A_HD ** -0.5) if i < 4 else (k_t, 1.0)
                    nc.scalar.activation(dst[:, 2 * (i % 4):2 * (i % 4) + 2, :], psum[:, 5, :].rearrange("p (a n) -> p a n", a=2),
                                         ACT.Identity, scale=scale).then_inc(rope_evac, 1)

                def x_exps(h):
                    act.wait_ge(x_max, l * X_HEADS + h + 1)
                    for b in range(TB):
                        ins = nc.scalar.activation(expd[:, b, :], psum[:, 4, b * 256:(b + 1) * 256], ACT.Exp,
                                                   bias=sm(NMAX + b), accum_out=sm(ZSUM + b))
                    ins.then_inc(x_exp, 1)

                def x_empty_turned(h):
                    act.wait_ge(x_turned, l * X_HEADS + h + 1)
                    nc.scalar.activation(probs_t[:], psum[:, 6, :], ACT.Identity).then_inc(x_pt, 1)

                def x_hi(h):
                    act.wait_ge(x_out, l * X_HEADS + h + 1)
                    nc.scalar.activation(op_hi[0][:, 2 * h:2 * h + 2, :], psum[:, 7, :].rearrange("p (a n) -> p a n", a=2),
                                         ACT.Identity).then_inc(op_hi_done, 1)

                for i in range(8):
                    if i:
                        empty_rope(i - 1)
                    if i % 2 == 0:
                        if i:
                            x_hi(i // 2 - 1)
                        x_exps(i // 2)
                    else:
                        x_empty_turned(i // 2)
                empty(T_AV, v_a[:, :, 0:256])
                empty_rope(7)
                x_hi(3)
                for n in range(1, 4):
                    empty(T_AV + n, v_a[:, :, n * 256:(n + 1) * 256])

                def empty_during_heads(t):
                    if t < T_ZY:
                        n = t - T_ZX
                        empty(t, zx[:, 2 * n:2 * n + 2, 4:260])
                    elif t < T_GM:
                        n = t - T_ZY
                        empty(t, gz[:, 2 * n:2 * n + 2, :])
                    elif t < T_PM:
                        empty_gate(t, ACT.Identity, 2, t - T_GM)

                act.wait_ge(mem_stored, 16)
                for h in range(A_HEADS):
                    t = T_ZX + 2 * h
                    act.wait_ge(d_max, l * A_HEADS + h + 1)
                    for m in range(2):
                        for b in range(TB):
                            n = (b + 1) * P
                            ins = nc.scalar.activation(expd[:, 2 * m + b, 0:n], psum[:, 4 + m, b * 256:b * 256 + n], ACT.Exp,
                                                       bias=sm(NMAX + 2 * m + b), accum_out=sm(ZSUM + 2 * m + b))
                    ins.then_inc(d_exp, 1)
                    empty_during_heads(t)
                    act.wait_ge(d_turned, l * A_HEADS + h + 1)
                    nc.scalar.activation(probs_t[:, 0:384], psum[:, 6, 0:384], ACT.Identity).then_inc(d_pt, 1)
                    empty_during_heads(t + 1)
                    if t + 2 == T_PM:
                        act.wait_ge(act_evac, l * N_ACT_EVAC + ACT_EVAC[T_PM - 1])
                        nc.scalar.activation(gate[:], gate[:], ACT.Sigmoid).then_inc(mem_gate, 1)
                    if h == 6:
                        act.wait_ge(conv_done, l * 4 + 4)
                        act.dma_start(B[0][:, 0:2048], rg_w[l]).then_inc(rgw_in, 16)
                    act.wait_ge(d_out, l * A_HEADS + h + 1)
                    nc.scalar.activation(o_a[:, :, h * P:(h + 1) * P], psum[:, 7, 0:256].rearrange("p (b n) -> p b n", b=TB),
                                         ACT.Identity).then_inc(d_kept, 1)

                act.wait_ge(sub_ss, l + 1)
                root(prep[:, 48:64], prep[:, 32:48], P, norm_sd)
                act.wait_ge(dve_evac, l * N_DVE_EVAC + DVE_EVAC[T_PM + 3])

                def rg_sigmoids(c):
                    act.wait_ge(rg_done, l * KC + c + 1)
                    nc.scalar.activation(r_g[:, c, :], psum[:, 4 + c % 4, 0:S], ACT.Sigmoid,
                                         bias=par[:, PA["rg_ba"] + c:PA["rg_ba"] + c + 1])
                    nc.scalar.activation(i_g[:, c, :], psum[:, 4 + c % 4, S:2 * S], ACT.Sigmoid,
                                         bias=par[:, PA["rg_bi"] + c:PA["rg_bi"] + c + 1]).then_inc(rg_evac, 1)

                for n in range(2):
                    empty_gate(T_GA + n, ACT.Sigmoid, 0, n)
                    for c in range(4):
                        rg_sigmoids(4 * n + c)
                empty_gate(T_GA + 2, ACT.Sigmoid, 0, 2)
                operand_hi(0, turns(SUB), turned, op_hi_done, lambda c: sm(GSUB))
                empty_gate(T_GA + 3, ACT.Sigmoid, 0, 3)
                for c in range(KC):
                    nc.scalar.activation(t_g[:, c, :], r_g[:, c, :], ACT.Tanh, scale=sm(SP_POS + c))
                    ins = nc.scalar.activation(r_g[:, c, :], r_g[:, c, :], ACT.Exp, scale=sm(SP_NEG + c))
                ins.then_inc(lru_ta, 1)
                nc.scalar.activation(B[5][:], B[5][:], ACT.Gelu_apprx_tanh).then_inc(gelu_done, 1)
                act.wait_ge(lru_v, l + 1)
                nc.scalar.activation(B[4][:], B[4][:], ACT.Sqrt).then_inc(lru_s, 1)
                act.wait_ge(lru_u, l + 1)
                act.dma_start(B[4][:], post_gain[l]).then_inc(gain_in, 16)
                act.wait_ge(dve_evac, l * N_DVE_EVAC + DVE_EVAC[T_PA + 3])
                act.wait_ge(lru_y, l + 1)
                nc.scalar.activation(op_hi[0][:].rearrange("p c t -> p (c t)"), B[6][:], ACT.Identity).then_inc(op_hi_done, 1)
                for n in range(4):
                    empty_gate(T_GL + n, ACT.Sigmoid, 1, n)
                act.preload_act_table_set("sqrt_and_others")
                for n in range(4):
                    act.wait_ge(merged_part, l * 4 + n + 1)
                    nc.scalar.activation(op_hi[1][:, 2 * n:2 * n + 2, :], feat(merged)[:, 2 * n:2 * n + 2, :],
                                         ACT.Identity).then_inc(op_hi_done, 1)
                for n in range(3):
                    act.wait_ge(tile_done, T + (T_OUT + n + 1))
                    for b in range(TB):
                        ins = nc.scalar.activation(B[5][:, (2 * n + b) * 256:(2 * n + b + 1) * 256], psum[:, n, b * 256:(b + 1) * 256],
                                                   ACT.Square, accum_out=sm(SS + 8 + 4 * b + n))
                    ins.then_inc(out_ss, 1)
                for b in range(TB):
                    if b == 0:
                        act.wait_ge(half_done, l * 2 + 1)
                    else:
                        act.wait_ge(tile_done, T + T_UP)
                    nc.scalar.activation(B[5][:, (6 + b) * 256:(7 + b) * 256], psum[:, OUT_BANKS[b], 0:256],
                                         ACT.Square, accum_out=sm(SS + 11 + 4 * b)).then_inc(out_ss, 1)
                    act.wait_ge(post_var, l * 2 + b + 1)
                    root(sm(SD + 4 + b), sm(VAR + b), D, post_sd)
                for b in range(TB):
                    act.wait_ge(x_ready, l * 4 + (b + 3))
                    norm_root(b, x[:, b, :], 6, (norm_ss, l * 4 + (b + 5)), norm_sd)
                operand_hi(0, turns(MLP), turned, op_hi_done, lambda c: par[:, PA["mlp_pre"] + c:PA["mlp_pre"] + c + 1])
                act.wait_ge(op_ready, l * (4 * N_OPS) + 4 * (MLP_OP + 1))
                act.dma_start(par[:], params[l + 1]).then_inc(par_in, 16)
                act.dma_start(B[6][:], mem_normed).then_inc(mem_loaded, 16)

                def relu(j, t, slot, first=False):
                    act.wait_ge(tile_done, T + (t + 1))
                    if not first:
                        act.wait_ge(squared_done, l * A_UP + (j - 1))
                    nc.scalar.activation(relu_u[:, slot, :], psum[:, slot, :], ACT.Relu).then_inc(relu_done, 1)

                relu(0, T_UP, 0, True)
                relu(1, T_UP + 1, 1, True)
                with act.Fori(0, A_UP // 2 - 1) as i:
                    relu(i * 2 + 2, i * 4 + (T_UP + 3), 0)
                    relu(i * 2 + 3, i * 4 + (T_UP + 5), 1)
                act.wait_ge(par_in, l * 16 + 32)
                act.wait_ge(mem_loaded, l * 16 + 16)
                for c in range(KC):
                    nc.scalar.activation(op_hi[0][:, c, :], feat(B[6])[:, c, :], ACT.Identity,
                                         scale=par[:, PA["mem"] + c:PA["mem"] + c + 1]).then_inc(op_hi_done, 1)
                for b in range(TB):
                    if b == 0:
                        act.wait_ge(half_done, l * 2 + 2)
                    else:
                        act.wait_ge(tile_done, T + A_TILES)
                    squares(b, psum[:, 4 + 2 * b:6 + 2 * b, :].rearrange("p a n -> p (a n)"), 8, post_ss)
                    act.wait_ge(post_ss, l * 2 + b + 1)
                    root(sm(SD + 8 + b), sm(SS + 8 + b), D, post_sd)
                assert step.n == ACT_STEPS, step.n

            T0 = DEPTH * A_TILES
            act.wait_ge(par_in, 16 * (DEPTH + 1))
            act.wait_ge(t5_skewed_in, 8 * 16)
            for b in range(TB):
                act.wait_ge(x_ready, 4 * DEPTH + b + 1)
                norm_root(b, x[:, b, :], 0, (b_ss, b + 1), b_sd)
            operand_hi(0, 0, b_turned, b_hi, lambda c: par[:, PB["mix"] + c:PB["mix"] + c + 1])
            act.preload_act_table_set("natural_log_exp_and_others")
            act.wait_ge(op_ready, DEPTH * 4 * N_OPS + 4)
            act.wait_ge(t5_skewed_in, 8 * 16)
            act.dma_start(B[6][:, 0:7 * P], masks_in).then_inc(b_masks_in, 16)
            for h in range(8):
                for u in range(TB):
                    src = bass.AP(tensor=t5_skewed.tensor, offset=t5_skewed.offset + h * P * (SKEW + 1) + 255 - u * P,
                                  ap=[[SKEW, P], [1, (u + 1) * P]])
                    act.dma_start(bias_b[h][:, u, 0:(u + 1) * P], src).then_inc(bias_in, 16)
            for t in range(N_FEAT):
                act.wait_ge(tile_done, T0 + t + 1)
                dst = B[t // 4][:, (t % 4) * 512:(t % 4 + 1) * 512]
                is_query = 2 * t in (SB_Q, MB_Q, FX_Q, DS_Q)
                nc.scalar.activation(dst, psum[:, t % 4, :], ACT.Identity, scale=B_HD ** -0.5 if is_query else 1.0).then_inc(b_evac_a, 1)
            for n in range(N_TOK):
                act.wait_ge(tile_done, T0 + N_FEAT + n + 1)
                nc.scalar.activation(v_b[:, :, n * 256:(n + 1) * 256], psum[:, (N_FEAT + n) % 4, :].rearrange("p (b n) -> p b n", b=TB),
                                     ACT.Identity).then_inc(b_evac_a, 1)

            def empty_gate_b(b, n):
                act.wait_ge(tile_done, T0 + T2_GATE + 5 * b + n + 1)
                if b:
                    act.wait_ge(b_mixed, b)
                nc.scalar.activation(gate[:, n * 512:(n + 1) * 512], psum[:, n, :], ACT.Identity).then_inc(b_evac_a, 1)

            def open_gate_b(b):
                act.wait_ge(b_evac_a, N_FEAT + N_TOK + 4 * (b + 1))
                nc.scalar.activation(gate[:], gate[:], ACT.Sigmoid).then_inc(gate_open, 1)

            def index_relu(h):
                act.wait_ge(ix_scores, h + 1)
                if h >= 2:
                    act.wait_ge(ix_added, h - 1)
                nc.scalar.activation(expd[:, 2 * (h % 2), 0:P], psum[:, 4 + h % 4, 0:P], ACT.Relu)
                nc.scalar.activation(expd[:, 2 * (h % 2) + 1, :], psum[:, 4 + h % 4, 256:512], ACT.Relu).then_inc(ix_relu, 1)

            for h in range(4):
                index_relu(h)
            empty_gate_b(0, 0)
            for h in range(4, IDX_HEADS):
                index_relu(h)
            act.wait_ge(f_in, 1)
            nc.scalar.activation(prep[:, 8:16], prep[:, 8:16], ACT.Exp).then_inc(f_ln, 1)
            act.wait_ge(f_ln, 1)
            nc.scalar.activation(prep[:, 8:16], prep[:, 8:16], ACT.Ln, bias=1.0).then_inc(f_ln, 1)
            def sb_softplus_tail(h):
                act.wait_ge(sb_z, h + 1)
                a = expd[:, 2 * (h % 2):2 * (h % 2) + 2, :].rearrange("p a n -> p (a n)")[:, 0:384]
                if h == 0:
                    act.wait_ge(ix_added, IDX_HEADS)
                for k, (src, func, bias) in enumerate(((psum[:, 4 + h % 2, 0:384], ACT.Abs, 0.0), (a, ACT.Exp, 0.0), (a, ACT.Ln, 1.0))):
                    nc.scalar.activation(a, src, func, bias=bias, scale=-1.0 if k == 1 else 1.0).then_inc(sb_ln, 1)
                    if k < 2:
                        act.wait_ge(sb_ln, 3 * h + k + 1)

            def sb_weights(h):
                act.wait_ge(sb_summed, h + 1)
                if h:
                    act.wait_ge(b_out, h)
                nc.scalar.activation(probs_t[:, 0:384], psum[:, 4 + h % 2, 0:384], ACT.Exp).then_inc(sb_w, 1)

            def branch_hi(b):
                act.wait_ge(b_out, 4 * (b + 1))
                if b:
                    act.wait_ge(tile_done, T0 + T2_GATE + 5 * b)
                nc.scalar.activation(op_hi[1][:, 0:2, :], psum[:, 7, :].rearrange("p (a t) -> p a t", a=2), ACT.Identity).then_inc(b_hi, 1)

            sb_softplus_tail(0)
            for h in range(4):
                if h < 3:
                    empty_gate_b(0, h + 1)
                sb_weights(h)
                if h < 3:
                    sb_softplus_tail(h + 1)
            branch_hi(0)
            act.wait_ge(c_sums, 1)
            for a in range(2):
                ins = nc.scalar.activation(minus_c_row[:, 2 * a:2 * a + 2, :].rearrange("p h n -> p (h n)"), psum[:, 4 + 2 * a, :],
                                           ACT.Identity, scale=-1.0)
            ins.then_inc(c_kept, 1)
            act.wait_ge(c_sums, 2)
            nc.scalar.activation(c_col, psum[:, 5, 0:8], ACT.Identity).then_inc(c_kept, 1)
            open_gate_b(0)

            def s_exps(b, h):
                g = 4 * (b - 1) + h
                act.wait_ge(s_max, g + 1)
                e = 2 * (h % 2)
                for u in range(TB):
                    ins = nc.scalar.activation(expd[:, e + u, 0:(u + 1) * P], expd[:, e + u, 0:(u + 1) * P], ACT.Exp,
                                               bias=sm(NMAX + e + u), accum_out=sm(ZSUM + e + u))
                ins.then_inc(s_exp, 1)

            def s_empty_turned(b, h):
                g = 4 * (b - 1) + h
                act.wait_ge(s_turned, g + 1)
                if h:
                    act.wait_ge(b_out, 4 * b + h)
                nc.scalar.activation(probs_t[:, 0:384], psum[:, 6, 0:384], ACT.Identity).then_inc(s_pt, 1)

            for b in range(1, 4):
                s_exps(b, 0)
                if b > 1:
                    open_gate_b(b - 1)
                    act.preload_act_table_set("exp_and_others")
                for h in range(4):
                    empty_gate_b(b, h)
                    s_empty_turned(b, h)
                    if h < 3:
                        s_exps(b, h + 1)
                branch_hi(b)
            open_gate_b(3)
            act.preload_act_table_set("sqrt_and_others")

            for n in range(4):
                act.wait_ge(out_part, n + 1)
                nc.scalar.activation(op_hi[0][:, 2 * n:2 * n + 2, :], feat(merged)[:, 2 * n:2 * n + 2, :], ACT.Identity).then_inc(b_hi, 1)
            for n in range(3):
                act.wait_ge(x_part, n + 1)
                for b in range(TB):
                    ins = nc.scalar.activation(gate[:, (2 * n + b) * 256:(2 * n + b + 1) * 256], x[:, b, n * 256:(n + 1) * 256],
                                               ACT.Square, accum_out=sm(SS + 8 + 4 * b + n))
                ins.then_inc(xb_ss, 1)
            act.dma_start(merged[:, 0:D], final_gain).then_inc(final_in, 16)
            for b in range(TB):
                act.wait_ge(x_part, 4 + b)
                nc.scalar.activation(gate[:, (6 + b) * 256:(7 + b) * 256], x[:, b, 768:1024],
                                     ACT.Square, accum_out=sm(SS + 11 + 4 * b)).then_inc(xb_ss, 1)
                act.wait_ge(xb_sum, b + 1)
                root(sm(SD + 2 + b), sm(VAR + b), D, b_sd)
            operand_hi(0, 4, b_turned, b_hi, lambda c: par[:, PB["ffn"] + c:PB["ffn"] + c + 1])
            act.wait_ge(pads_zero, 1)
            for j in range(B_UP):
                t = T2_FFN + (0 if j == 0 else 2 + 3 * (j - 1))
                for n in range(2):
                    act.wait_ge(tile_done, T0 + t + n + 1)
                    if j >= 2 and n == 0:
                        act.wait_ge(f_conv, j - 1)
                    nc.scalar.activation(padded[:, j % 2, 2 * n:2 * n + 2, 2:2 + S],
                                         psum[:, 2 * (j % 2) + n, :].rearrange("p (a t) -> p a t", a=2), ACT.Identity).then_inc(f_evac, 1)
                act.wait_ge(f_conv, j + 1)
                if j >= 2:
                    act.wait_ge(f_gated, j - 1)
                nc.scalar.activation(gelu_g[:, j % 2, :], conved[:, j % 2, 0:2, :].rearrange("p a t -> p (a t)"), ACT.Gelu).then_inc(f_gelu, 1)
            act.preload_act_table_set("sqrt_and_others")
            for b in range(TB):
                act.wait_ge(x_b, b + 1)
                norm_root(b, x[:, b, :], 4, (b_ss, b + 3), b_sd)
                act.wait_ge(y_done, b + 1)
                act.dma_start(out[:, b, :], y_tok[:, b, :]).then_inc(out_done, 16)

        @block.vector
        def _(dve):
            step = Steps(dve, dve_step, DVE_STEPS)

            def split(t, s, round_of_slot):
                dve.wait_ge(raw_loaded[s], round_of_slot * 16 + 16)
                nc.vector.tensor_copy(w_hi[:, s, :], w_raw[:, s, :]).then_inc(hi_ready, 1)

            nc.vector.memset(eps[:], EPS).then_inc(masks_ready, 1)
            nc.vector.memset(rowmask[:], 0.0).then_inc(masks_ready, 1)
            nc.vector.memset(colmask[:], NEG).then_inc(masks_ready, 1)
            dve.wait_ge(masks_ready, 3)
            nc.vector.memset(rowmask[:, 0:64], 1.0).then_inc(masks_ready, 1)

            def diagonal(b, col, sd, own, signal):
                dve.wait_ge(*sd)
                own(nc.vector.reciprocal(sm(RS + col + b), sm(SD + col + b)))
                nc.vector.tensor_scalar(diag[:, b, :], ident[:], sm(RS + col + b), None, ALU.mult).then_inc(signal, 1)

            def operand_lo(which, hi_part, ready, gain):
                for c in range(KC):
                    if c % 2 == 0:
                        hi_part(2)
                    ins = nc.vector.scalar_tensor_tensor(
                        op_lo[which][:, c, :], psum[:, 4 + c // 2, (c % 2) * S:(c % 2 + 1) * S], gain(c),
                        op_hi[which][:, c, :].bitcast(F32), ALU.mult, ALU.subtract)
                    if c % 2:
                        ins.then_inc(ready, 1)

            dve.wait_ge(ident_loaded, 16)
            for b in range(TB):
                def own(ins):
                    ins.then_inc(rs_ready, 1)
                    dve.wait_ge(rs_ready, b + 1)

                diagonal(b, 0, (norm_sd, b + 1), own, norm_x)
            dve.wait_ge(t5_rows_ready, 1)
            nc.vector.tensor_copy(B[1][0:8, 1024:1536], psum[0:8, 0, :]).then_inc(t5_evac, 1)
            split(0, 0, 0)
            his = [0]

            def first_hi_part(n):
                his[0] += n
                dve.wait_ge(op_hi_done, his[0])

            operand_lo(0, first_hi_part, op_ready, lambda c: par[:, PA["mem"] + c:PA["mem"] + c + 1])
            for s in range(1, HI):
                split(s, s, 0)
            dve.wait_ge(x_loaded, 16)
            nc.vector.sem_inc(x_ready, TB)

            with dve.Fori(0, DEPTH) as l:
                T = l * A_TILES
                step.base, step.n = l * DVE_STEPS, 0
                his[0] = 0

                def hi_part(n=1):
                    his[0] += n
                    dve.wait_ge(op_hi_done, l * 41 + (KC + his[0]))

                def after(t, evac=None):
                    dve.wait_ge(tile_done, T + t + 1)
                    if evac:
                        evac()
                    split(T + t + 4, (t + 4) % 4, l * (A_TILES // 4) + (t + 4) // 4)

                for b in range(TB):
                    diagonal(b, 2, (norm_sd, l * NORM_COUNT + (NORM_AT[MIX] + b + 1)), step, norm_x)

                lam = par[:, PA["rg_lambda"]:PA["rg_lambda"] + 8]
                nc.vector.scalar_tensor_tensor(prep[:, 0:8], lam, -1.0, lam, ALU.mult, ALU.min)
                nc.vector.tensor_scalar(prep[:, 24:32], lam, 0.0, -1.0, ALU.min, ALU.mult)
                step(nc.vector.tensor_tensor(prep[:, 32:160], par[:, PA["lambda_q"]:PA["lambda_q"] + 128],
                                             par[:, PA["lambda_k"]:PA["lambda_k"] + 128], ALU.mult))
                nc.vector.tensor_reduce(prep[:, 8:10], prep[:, 32:160].rearrange("p (a n) -> p a n", a=2), AX.X,
                                        ALU.add).then_inc(par_d, 1)
                nc.vector.tensor_tensor(sm(GSUB), par[:, PA["subln"]:PA["subln"] + 1],
                                        par[:, PA["one_minus_init"]:PA["one_minus_init"] + 1], ALU.mult)
                dve.wait_ge(par_a, l * 2 + 2)
                step(nc.vector.tensor_tensor(sm(NLAM), prep[:, 17:18], prep[:, 16:17], ALU.subtract))
                nc.vector.tensor_tensor(sm(NLAM), sm(NLAM), par[:, PA["init"]:PA["init"] + 1], ALU.subtract)
                step(nc.vector.tensor_tensor(prep[:, 0:8], prep[:, 0:8], prep[:, 24:32], ALU.add))
                nc.vector.tensor_scalar(sm(SP_POS, 8), prep[:, 0:8], 8.0, None, ALU.mult)
                step(nc.vector.tensor_scalar(sm(SP_NEG, 8), prep[:, 0:8], -8.0, None, ALU.mult))

                for t in range(T_K, T_V):
                    after(t)
                operand_lo(1, hi_part, op_ready, lambda c: par[:, PA["mix_pre"] + c:PA["mix_pre"] + c + 1])
                for t in range(T_V, T_QK):
                    after(t)
                dve.wait_ge(rope_in, 2 * 16)

                def rope(i):
                    def evac():
                        bank = (T_QK + i) % 4
                        if i >= 2:
                            dve.wait_ge(rope_turned, l * 8 + i - 1)
                        if i:
                            dve.wait_ge(rope_ready, l * 8 + i)
                        for b in range(TB):
                            z = psum[:, bank, b * 256:(b + 1) * 256]
                            zg = z.rearrange("p (g h n) -> p g h n", g=4, h=2)
                            za = rope_a[:, b * 256:(b + 1) * 256]
                            zb = rope_b[:, b * 256:(b + 1) * 256].rearrange("p (g h n) -> p g h n", g=4, h=2)
                            nc.vector.tensor_tensor(za.rearrange("p (g n) -> p g n", n=32), z.rearrange("p (g n) -> p g n", n=32),
                                                    cos[:, b:b + 1, :].to_broadcast([P, 8, 32]), ALU.mult)
                            s4 = sin[:, b:b + 1, :].to_broadcast([P, 4, 32])
                            nc.vector.scalar_tensor_tensor(zb[:, :, 0, :], zg[:, :, 1, :], -1.0, s4, ALU.mult, ALU.mult)
                            ins = nc.vector.tensor_tensor(zb[:, :, 1, :], zg[:, :, 0, :], s4, ALU.mult)
                        ins.then_inc(dve_evac, 1)
                        dve.wait_ge(dve_evac, l * N_DVE_EVAC + i + 1)
                        nc.vector.tensor_tensor(rot[:, i % 2, :], rope_a, rope_b, ALU.add).then_inc(rope_ready, 1)
                    return evac

                def x_softmax(h):
                    dve.wait_ge(x_scores, l * X_HEADS + h + 1)
                    nc.vector.tensor_reduce(sm(NMAX, 2), psum[:, 4, :].rearrange("p (b n) -> p b n", b=TB), AX.X, ALU.max,
                                            negate=True).then_inc(x_max, 1)
                    dve.wait_ge(x_exp, l * X_HEADS + h + 1)
                    step(nc.vector.reciprocal(sm(RZ, 2), sm(ZSUM, 2)))
                    for b in range(TB):
                        ins = nc.vector.tensor_scalar(expd[:, b, :], expd[:, b, :], sm(RZ + b), None, ALU.mult)
                    ins.then_inc(x_probs, 1)

                def x_lo(h):
                    hi_part()
                    nc.vector.tensor_tensor(op_lo[0][:, 2 * h:2 * h + 2, :], psum[:, 7, :].rearrange("p (a n) -> p a n", a=2),
                                            op_hi[0][:, 2 * h:2 * h + 2, :].bitcast(F32), ALU.subtract).then_inc(op_ready, 1)

                for i in range(8):
                    after(T_QK + i, rope(i))
                    if i % 2 == 0:
                        x_softmax(i // 2)
                        if i:
                            x_lo(i // 2 - 1)
                after(T_AV)
                x_lo(3)
                nc.vector.memset(zx[:, :, 0:4], 0.0).then_inc(zx_padded, 1)
                for t in range(T_AV + 1, T_ZX):
                    after(t)

                def add_branch(t0, n, first, last=False):
                    def evac():
                        cols = slice(n * 512, (n + 1) * 512)
                        if first:
                            nc.vector.tensor_tensor(merged[:, cols], psum[:, (t0 + n) % 4, :], gate[:, cols], ALU.mult).then_inc(dve_evac, 1)
                            return
                        prod = expd[:, 0:2, :].rearrange("p a n -> p (a n)")
                        if last and n:
                            dve.wait_ge(merged_part, l * 4 + n)
                        nc.vector.tensor_tensor(prod, psum[:, (t0 + n) % 4, :], gate[:, cols], ALU.mult).then_inc(dve_evac, 1)
                        dve.wait_ge(dve_evac, l * N_DVE_EVAC + DVE_EVAC[t0 + n])
                        ins = nc.vector.tensor_tensor(merged[:, cols], merged[:, cols], prod, ALU.add)
                        if last:
                            ins.then_inc(merged_part, 1)
                        else:
                            step(ins)
                    return evac

                def conv(c0):
                    for k in range(4):
                        for c in (c0, c0 + 1):
                            w = par[:, PA["conv_w"] + k * KC + c:PA["conv_w"] + k * KC + c + 1]
                            src = zx[:, c, 1 + k:1 + k + S]
                            if k == 0:
                                ins = nc.vector.tensor_scalar(xc[:, c, :], src, w, par[:, PA["conv_b"] + c:PA["conv_b"] + c + 1],
                                                              ALU.mult, ALU.add)
                            else:
                                ins = nc.vector.scalar_tensor_tensor(xc[:, c, :], src, w, xc[:, c, :], ALU.mult, ALU.add)
                        if k < 3:
                            step(ins)
                    ins.then_inc(conv_done, 1)

                for h in range(A_HEADS):
                    t = T_ZX + 2 * h
                    dve.wait_ge(d_scores, l * A_HEADS + h + 1)
                    for b in range(TB):
                        n = (b + 1) * P
                        ins = nc.vector.tensor_reduce(small[:, NMAX + b:NMAX + b + 3:2], psum[:, 4:6, b * 256:b * 256 + n], AX.X,
                                                      ALU.max, negate=True)
                    ins.then_inc(d_max, 1)
                    dve.wait_ge(d_exp, l * A_HEADS + h + 1)
                    step(nc.vector.reciprocal(sm(RZ, 4), sm(ZSUM, 4)))
                    nc.vector.tensor_scalar(sm(R2, 2), sm(RZ + 2, 2), sm(NLAM), None, ALU.mult)
                    for b in range(TB):
                        ins = nc.vector.tensor_scalar(expd[:, b, 0:(b + 1) * P], expd[:, b, 0:(b + 1) * P], sm(RZ + b), None, ALU.mult)
                    step(ins)
                    for b in range(TB):
                        n = (b + 1) * P
                        ins = nc.vector.scalar_tensor_tensor(expd[:, b, 0:n], expd[:, 2 + b, 0:n], sm(R2 + b), expd[:, b, 0:n],
                                                             ALU.mult, ALU.add)
                    ins.then_inc(d_probs, 1)
                    for u in (t, t + 1):
                        if u >= T_PM:
                            if u == T_PM:
                                dve.wait_ge(mem_gate, l + 1)
                            after(u, add_branch(T_PM, u - T_PM, True))
                        else:
                            after(u)
                        if u == t and 2 <= h < 6:
                            dve.wait_ge(act_evac, l * N_ACT_EVAC + ACT_EVAC[T_ZX + h - 2])
                            if h == 2:
                                dve.wait_ge(zx_padded, l + 1)
                            conv(2 * (h - 2))

                dve.wait_ge(d_kept, l * A_HEADS + A_HEADS)
                step(nc.vector.tensor_tensor(B[4][:], B[6][:], B[6][:], ALU.mult))
                ins = nc.vector.tensor_reduce(prep[:, 32:48], B[4][:].rearrange("p (a n) -> p a n", n=P), AX.X, ALU.add)
                ins.then_inc(sub_ss, 1)
                dve.wait_ge(norm_sd, l * NORM_COUNT + (NORM_AT[SUB] + 1))
                step(nc.vector.reciprocal(prep[:, 48:64], prep[:, 48:64]))
                heads = B[6][:].rearrange("p (a n) -> p a n", n=P)
                nc.vector.tensor_tensor(heads, heads, prep[:, 48:64].unsqueeze(2).to_broadcast([P, 16, P]), ALU.mult).then_inc(norm_x, 1)
                after(T_GA)
                after(T_GA + 1)
                after(T_GA + 2)
                operand_lo(0, hi_part, op_ready, lambda c: sm(GSUB))
                after(T_GA + 3)

                dve.wait_ge(lru_ta, l + 1)
                step(nc.vector.tensor_tensor(B[6][:], B[2][:], B[2][:], ALU.mult))
                nc.vector.scalar_tensor_tensor(B[4][:], B[6][:], 1.0, B[4][:], ALU.add, ALU.mult).then_inc(lru_v, 1)
                after(T_PA, add_branch(T_PA, 0, False))
                step(nc.vector.tensor_tensor(B[3][:], B[3][:], B[1][:], ALU.mult))
                dve.wait_ge(lru_s, l + 1)
                nc.vector.tensor_tensor(B[3][:], B[3][:], B[4][:], ALU.mult).then_inc(lru_u, 1)
                after(T_PA + 1, add_branch(T_PA, 1, False))
                dve.wait_ge(lru_u, l + 1)
                for c in range(KC):
                    ins = nc.vector.tensor_tensor_scan(lru[:, c, :], r_g[:, c, :], i_g[:, c, :], 0.0, ALU.mult, ALU.add)
                step(ins)
                after(T_PA + 2, add_branch(T_PA, 2, False))
                dve.wait_ge(gelu_done, l + 1)
                nc.vector.tensor_tensor(B[6][:], B[6][:], B[5][:], ALU.mult).then_inc(lru_y, 1)
                after(T_PA + 3, add_branch(T_PA, 3, False))
                hi_part()
                for c in range(0, KC, 2):
                    nc.vector.tensor_tensor(op_lo[0][:, c:c + 2, :], feat(B[6])[:, c:c + 2, :], op_hi[0][:, c:c + 2, :].bitcast(F32),
                                            ALU.subtract).then_inc(op_ready, 1)
                for t in range(T_GL, T_PL):
                    after(t)
                for n in range(4):
                    if n < 3:
                        after(T_PL + n, add_branch(T_PL, n, False, True))
                    else:
                        dve.wait_ge(tile_done, T + (T_PL + n + 1))
                        add_branch(T_PL, n, False, True)()
                    hi_part()
                    nc.vector.tensor_tensor(op_lo[1][:, 2 * n:2 * n + 2, :], feat(merged)[:, 2 * n:2 * n + 2, :],
                                            op_hi[1][:, 2 * n:2 * n + 2, :].bitcast(F32), ALU.subtract).then_inc(op_ready, 1)
                after(T_PL + 3)

                def gained(n):
                    def evac():
                        cols = slice(n * 256, (n + 1) * 256)
                        dve.wait_ge(out_ss, l * 5 + n + 1)
                        if n == 0:
                            dve.wait_ge(gain_in, l * 16 + 16)
                        nc.vector.tensor_tensor(y_tok[:, :, cols], psum[:, n, :].rearrange("p (b n) -> p b n", b=TB),
                                                gains[:, 0:1, cols].to_broadcast([P, TB, 256]), ALU.mult).then_inc(dve_evac, 1)
                    return evac

                def add_normed(k, b):
                    col = 4 + 4 * k + b
                    dve.wait_ge(post_sd, l * 4 + (2 * k + b + 1))
                    step(nc.vector.reciprocal(sm(RS + col), sm(SD + col)))
                    dve.wait_ge(post_gained, l * 4 + (2 * k + b + 1))
                    nc.vector.scalar_tensor_tensor(x[:, b, :], y_tok[:, b, :], sm(RS + col), x[:, b, :],
                                                   ALU.mult, ALU.add).then_inc(x_ready, 1)

                for n in range(3):
                    after(T_OUT + n, gained(n))
                dve.wait_ge(dve_evac, l * N_DVE_EVAC + N_DVE_EVAC)
                for b in range(TB):
                    dve.wait_ge(out_ss, l * 5 + (4 + b))
                    nc.vector.tensor_reduce(sm(VAR + b), sm(SS + 8 + 4 * b, 4), AX.X, ALU.add).then_inc(post_var, 1)
                    nc.vector.tensor_tensor(y_tok[:, b, 768:1024], psum[:, OUT_BANKS[b], 0:256], gains[:, 0, 768:1024],
                                            ALU.mult).then_inc(post_gained, 1)
                    add_normed(0, b)
                for b in range(TB):
                    diagonal(b, 6, (norm_sd, l * NORM_COUNT + (NORM_AT[MLP] + b + 1)), step, norm_x)
                after(T_OUT + 3)
                operand_lo(0, hi_part, op_ready, lambda c: par[:, PA["mlp_pre"] + c:PA["mlp_pre"] + c + 1])

                def after_mlp(t, i=None):
                    if i is None:
                        dve.wait_ge(tile_done, T + (t + 1))
                        split(None, (t + 4) % 4, l * (A_TILES // 4) + (t + 4) // 4)
                    else:
                        dve.wait_ge(tile_done, T + i * 4 + (t + 1))
                        split(None, (t + 4) % 4, l * (A_TILES // 4) + i + (t + 4) // 4)

                def hidden(j, slot):
                    dve.wait_ge(relu_done, l * A_UP + (j + 1))
                    nc.vector.tensor_tensor(squared[:, slot, :], relu_u[:, slot, :], relu_u[:, slot, :], ALU.mult).then_inc(squared_done, 1)
                    dve.wait_ge(squared_done, l * A_UP + (j + 1))
                    hi = op_hi[1][:, 2 * slot:2 * slot + 2, :].rearrange("p a t -> p (a t)")
                    lo = op_lo[1][:, 2 * slot:2 * slot + 2, :].rearrange("p a t -> p (a t)")
                    nc.vector.tensor_copy(hi, squared[:, slot, :]).then_inc(ffn_hi, 1)
                    dve.wait_ge(ffn_hi, l * A_UP + (j + 1))
                    nc.vector.tensor_tensor(lo, squared[:, slot, :], hi.bitcast(F32), ALU.subtract).then_inc(ffn_ready, 1)

                after_mlp(T_UP)
                hidden(0, 0)
                after_mlp(T_UP + 1)
                hidden(1, 1)
                after_mlp(T_UP + 2)
                with dve.Fori(0, A_UP // 2 - 1) as i:
                    after_mlp(T_UP + 3, i)
                    hidden(i * 2 + 2, 0)
                    after_mlp(T_UP + 4, i)
                    after_mlp(T_UP + 5, i)
                    hidden(i * 2 + 3, 1)
                    after_mlp(T_UP + 6, i)
                dve.wait_ge(par_in, l * 16 + 32)
                dve.wait_ge(mem_loaded, l * 16 + 16)
                for c in range(KC):
                    hi_part()
                    ins = nc.vector.scalar_tensor_tensor(
                        op_lo[0][:, c, :], feat(B[6])[:, c, :], par[:, PA["mem"] + c:PA["mem"] + c + 1],
                        op_hi[0][:, c, :].bitcast(F32), ALU.mult, ALU.subtract)
                    if c % 2:
                        ins.then_inc(op_ready, 1)
                for b in range(TB):
                    dve.wait_ge(post_ss, l * 2 + b + 1)
                    nc.vector.tensor_tensor(y_tok[:, b, :], psum[:, 4 + 2 * b:6 + 2 * b, :].rearrange("p a n -> p (a n)"),
                                            gains[:, 1, :], ALU.mult).then_inc(post_gained, 1)
                    add_normed(1, b)
                after_mlp(A_TILES - 1)
                assert step.n == DVE_STEPS, step.n

            T0 = DEPTH * A_TILES
            bstep = Steps(dve, b_step, 0)
            bhis = [0]

            def hi_b(n=1):
                bhis[0] += n
                dve.wait_ge(b_hi, bhis[0])

            def after_b(t, evac=None):
                dve.wait_ge(tile_done, T0 + t + 1)
                if evac:
                    evac()
                if T0 + t + 4 < N_TILES:
                    split(T0 + t + 4, (t + 4) % 4, (T0 + t + 4) // 4)

            dve.wait_ge(op_ready, DEPTH * 4 * N_OPS + 4)
            for b in range(TB):
                diagonal(b, 0, (b_sd, b + 1), bstep, b_x)
            operand_lo(0, hi_b, b_ready, lambda c: par[:, PB["mix"] + c:PB["mix"] + c + 1])
            for t in range(N_FEAT + N_TOK):
                after_b(t)

            dve.wait_ge(b_evac_a, N_FEAT + N_TOK)
            dve.wait_ge(b_masks_in, 16)
            f = prep[:, 0:8].rearrange("p (b h) -> p b h", b=TB)
            bstep(nc.vector.tensor_tensor(f, v_b[:, :, F_COL:F_COL + 4],
                                          par[:, PB["fox_b"]:PB["fox_b"] + 4].unsqueeze(1).to_broadcast([P, TB, 4]), ALU.add))
            nc.vector.scalar_tensor_tensor(prep[:, 8:16], prep[:, 0:8], -1.0, prep[:, 0:8], ALU.mult, ALU.min).then_inc(f_in, 1)

            def index_add(h):
                dve.wait_ge(ix_relu, h + 1)
                for u in range(TB):
                    n = (u + 1) * P
                    w = v_b[:, u, W_COL + h:W_COL + h + 1]
                    r = expd[:, 2 * (h % 2) + u, 0:n]
                    if h == 0:
                        ins = nc.vector.tensor_scalar(index[:, u, 0:n], r, w, None, ALU.mult)
                    else:
                        ins = nc.vector.scalar_tensor_tensor(index[:, u, 0:n], r, w, index[:, u, 0:n], ALU.mult, ALU.add)
                ins.then_inc(ix_added, 1)
                dve.wait_ge(ix_added, h + 1)

            for h in range(4):
                index_add(h)
            after_b(T2_GATE)
            for h in range(4, IDX_HEADS):
                index_add(h)
            dve.wait_ge(f_ln, 2)
            bstep(nc.vector.scalar_tensor_tensor(log_f, prep[:, 0:8], 0.0, prep[:, 8:16], ALU.min, ALU.subtract))
            nc.vector.tensor_copy(log_f_wide, log_f.unsqueeze(2).to_broadcast([P, 8, P])).then_inc(f_wide, 1)
            for u in range(TB):
                own = index[:, u, u * P:(u + 1) * P]
                ins = nc.vector.scalar_tensor_tensor(own, causal, OUTSIDE / NEG, own, ALU.mult, ALU.add)
            bstep(ins)

            def take_eight():
                for u in range(TB):
                    ins = nc.vector.max(sm(SS + 8 * u, 8), index[:, u, 0:(u + 1) * P])
                bstep(ins)
                for u in range(TB):
                    s = index[:, u, 0:(u + 1) * P]
                    ins = nc.vector.match_replace(s, sm(SS + 8 * u, 8), s, REPLACED)
                bstep(ins)

            def sb_mask(h):
                dve.wait_ge(sb_ln, 3 * h + 3)
                m = expd[:, 2 * (h % 2):2 * (h % 2) + 2, :].rearrange("p a n -> p (a n)")
                bstep(nc.vector.scalar_tensor_tensor(m[:, 0:384], psum[:, 4 + h % 2, 0:384], 0.0, m[:, 0:384], ALU.max, ALU.add))
                nc.vector.tensor_tensor(m[:, 0:P], m[:, 0:P], before01, ALU.mult)
                nc.vector.tensor_tensor(m[:, 256:384], m[:, 256:384], before01, ALU.mult).then_inc(sb_masked, 1)

            def branch_lo(b):
                hi_b()
                nc.vector.tensor_tensor(op_lo[1][:, 0:2, :], psum[:, 7, :].rearrange("p (a t) -> p a t", a=2),
                                        op_hi[1][:, 0:2, :].bitcast(F32), ALU.subtract).then_inc(b_ready, 1)

            def mix_branch(b, part_done=None):
                dve.wait_ge(gate_open, b + 1)
                for n in range(5):
                    if n < 4:
                        if n < 3:
                            dve.wait_ge(b_bank, 3 * b + n + 1)
                        else:
                            dve.wait_ge(tile_done, T0 + T2_GATE + 5 * (b + 1))
                        cols = slice(n * 512, (n + 1) * 512)
                        dst = gate if b else merged
                        ins = nc.vector.tensor_tensor(dst[:, cols], psum[:, n, :], gate[:, cols], ALU.mult).then_inc(b_evac_d, 1)
                    if n and b:
                        dve.wait_ge(b_evac_d, 4 * b + n)
                        cols = slice((n - 1) * 512, n * 512)
                        ins = nc.vector.tensor_tensor(merged[:, cols], merged[:, cols], gate[:, cols], ALU.add)
                        if b == 3:
                            ins.then_inc(out_part, 1)
                    if part_done and n >= 2:
                        part_done(n - 2)
                if b == 3:
                    part_done(3)
                    return
                if b == 0:
                    dve.wait_ge(b_evac_d, 4)
                    nc.vector.sem_inc(b_mixed, 1)
                else:
                    ins.then_inc(b_mixed, 1)
                    dve.wait_ge(b_mixed, b + 1)

            sb_mask(0)
            for h in range(4):
                if h < 3:
                    after_b(T2_GATE + 1 + h)
                take_eight()
                if h < 3:
                    sb_mask(h + 1)
            branch_lo(0)

            def s_softmax(b, h):
                g = 4 * (b - 1) + h
                dve.wait_ge(s_scores, g + 1)
                e = 2 * (h % 2)
                if b == 1 and h == 0:
                    dve.wait_ge(bias_in, 16 * 16)
                for u in range(TB):
                    n = (u + 1) * P
                    sc, dst = psum[:, 4 + h % 2, u * 256:u * 256 + n], expd[:, e + u, 0:n]
                    if b == 2:
                        ins = nc.vector.scalar_tensor_tensor(dst, sc, c_col[:, 4 * u + h:4 * u + h + 1], minus_c_row[:, h, 0:n], ALU.add, ALU.add)
                    else:
                        ins = nc.vector.tensor_tensor(dst, sc, bias_b[h + (4 if b == 3 else 0)][:, u, 0:n], ALU.add)
                bstep(ins)
                if b == 2:
                    for u in range(TB):
                        own = expd[:, e + u, u * P:(u + 1) * P]
                        ins = nc.vector.tensor_tensor(own, own, causal, ALU.add)
                    bstep(ins)
                for u in range(TB):
                    ins = nc.vector.tensor_reduce(sm(NMAX + e + u), expd[:, e + u, 0:(u + 1) * P], AX.X, ALU.max, negate=True)
                ins.then_inc(s_max, 1)
                dve.wait_ge(s_exp, g + 1)
                bstep(nc.vector.reciprocal(sm(RZ + e, 2), sm(ZSUM + e, 2)))
                for u in range(TB):
                    p = expd[:, e + u, 0:(u + 1) * P]
                    ins = nc.vector.tensor_scalar(p, p, sm(RZ + e + u), None, ALU.mult)
                ins.then_inc(s_probs, 1)

            def keep_taken(h):
                for u in range(TB):
                    n = (u + 1) * P
                    ins = nc.vector.scalar_tensor_tensor(bias_b[4 + h][:, u, 0:n], index[:, u, 0:n], -NEG, bias_b[4 + h][:, u, 0:n],
                                                         ALU.mult, ALU.add)
                return ins

            for b in range(1, 4):
                if b == 1:
                    mix_branch(0)
                    s_softmax(1, 0)
                else:
                    s_softmax(b, 0)
                    mix_branch(b - 1)
                after_b(T2_GATE + 5 * b - 1)
                for h in range(4):
                    after_b(T2_GATE + 5 * b + h)
                    if b == 1:
                        take_eight()
                    if b == 2:
                        if h == 0:
                            for u in range(TB):
                                s = index[:, u, 0:(u + 1) * P]
                                ins = nc.vector.tensor_scalar(s, s, REPLACED, 1.0, ALU.is_equal, ALU.subtract)
                            bstep(ins)
                        bstep(keep_taken(h))
                    if h < 3:
                        s_softmax(b, h + 1)
                branch_lo(b)

            def out_lo(n):
                hi_b()
                nc.vector.tensor_tensor(op_lo[0][:, 2 * n:2 * n + 2, :], feat(merged)[:, 2 * n:2 * n + 2, :],
                                        op_hi[0][:, 2 * n:2 * n + 2, :].bitcast(F32), ALU.subtract).then_inc(b_ready, 1)

            mix_branch(3, out_lo)
            after_b(T2_GATE + 19)

            def add_out(n):
                def evac():
                    dst = x[:, :, n * 256:(n + 1) * 256]
                    nc.vector.tensor_tensor(dst, dst, psum[:, n, :].rearrange("p (b n) -> p b n", b=TB), ALU.add).then_inc(x_part, 1)
                return evac

            for n in range(3):
                after_b(T2_OUT + n, add_out(n))
            for b in range(TB):
                if b == 0:
                    dve.wait_ge(half_done, 2 * DEPTH + 1)
                else:
                    dve.wait_ge(tile_done, T0 + T2_OUT + 4)
                dst = x[:, b, 768:1024]
                nc.vector.tensor_tensor(dst, dst, psum[:, OUT_BANKS[b], 0:256], ALU.add).then_inc(x_part, 1)
                dve.wait_ge(xb_ss, 4 + b)
                nc.vector.tensor_reduce(sm(VAR + b), sm(SS + 8 + 4 * b, 4), AX.X, ALU.add).then_inc(xb_sum, 1)
                diagonal(b, 2, (b_sd, 3 + b), bstep, b_x)
            nc.vector.memset(padded[:, :, :, 0:2], 0.0).then_inc(pads_zero, 1)
            after_b(T2_OUT + 3)
            operand_lo(0, hi_b, b_ready, lambda c: par[:, PB["ffn"] + c:PB["ffn"] + c + 1])

            def f_convolve(j):
                dve.wait_ge(f_evac, 2 * j + 2)
                if j >= 2:
                    dve.wait_ge(f_gated, j - 1)
                for k in range(3):
                    for i in range(4):
                        w = PB["conv_w"] + (k * B_UP + j) * 4 + i
                        src, acc = padded[:, j % 2, i, k:k + S], conved[:, j % 2, i, :]
                        if k == 0:
                            cb = PB["conv_b"] + 4 * j + i
                            ins = nc.vector.tensor_scalar(acc, src, par[:, w:w + 1], par[:, cb:cb + 1], ALU.mult, ALU.add)
                        else:
                            ins = nc.vector.scalar_tensor_tensor(acc, src, par[:, w:w + 1], acc, ALU.mult, ALU.add)
                    if k < 2:
                        bstep(ins)
                ins.then_inc(f_conv, 1)

            def f_operand(j):
                dve.wait_ge(f_gelu, j + 1)
                s = j % 2
                u = conved[:, s, 2:4, :].rearrange("p a t -> p (a t)")
                dve.wait_ge(f_conv, j + 1)
                if j >= 2:
                    dve.wait_ge(f_ready, j - 1)
                nc.vector.tensor_tensor(gated[:, s, :], gelu_g[:, s, :], u, ALU.mult).then_inc(f_gated, 1)
                dve.wait_ge(f_gated, j + 1)
                hi = op_hi[1][:, 2 * s:2 * s + 2, :].rearrange("p a t -> p (a t)")
                lo = op_lo[1][:, 2 * s:2 * s + 2, :].rearrange("p a t -> p (a t)")
                nc.vector.tensor_copy(hi, gated[:, s, :]).then_inc(f_hi, 1)
                dve.wait_ge(f_hi, j + 1)
                nc.vector.tensor_tensor(lo, gated[:, s, :], hi.bitcast(F32), ALU.subtract).then_inc(f_ready, 1)

            for j in range(B_UP):
                t = T2_FFN + (0 if j == 0 else 2 + 3 * (j - 1))
                after_b(t)
                after_b(t + 1)
                f_convolve(j)
                if j:
                    after_b(t + 2)
                f_operand(j)
            dve.wait_ge(final_in, 16)
            for b in range(TB):
                if b == 0:
                    dve.wait_ge(half_done, 2 * DEPTH + 2)
                else:
                    dve.wait_ge(tile_done, T0 + B_TILES)
                nc.vector.tensor_tensor(x[:, b, :], x[:, b, :], psum[:, 4 + 2 * b:6 + 2 * b, :].rearrange("p a n -> p (a n)"),
                                        ALU.add).then_inc(x_b, 1)
                dve.wait_ge(b_sd, 5 + b)
                bstep(nc.vector.reciprocal(sm(RS + 4 + b), sm(SD + 4 + b)))
                nc.vector.scalar_tensor_tensor(y_tok[:, b, :], x[:, b, :], sm(RS + 4 + b), merged[:, 0:D], ALU.mult,
                                               ALU.mult).then_inc(y_done, 1)


def _col_tiles(w):
    n = w.shape[1] // 256
    return w.reshape(KC, P, n, 256).transpose(2, 1, 0, 3).reshape(n, P, TILE)


def _row_tiles(w):
    n = w.shape[0] // 256
    return w.reshape(n, 2, P, D).transpose(0, 2, 1, 3).reshape(n, P, TILE)


def _feat_vector(v):
    return np.ascontiguousarray(v.reshape(-1, P).T)


def _weight_stream(a):
    stream = np.empty((N_TILES, P, TILE), np.float32)
    at = 0

    def put(tiles):
        nonlocal at
        stream[at:at + len(tiles)] = tiles
        at += len(tiles)

    for l in range(DEPTH):
        q, k, v, zx, zy, xq, g = np.split(a["w_in"][l], np.cumsum([D] * 6), axis=1)
        put(_col_tiles(a["w_kv_mem"][l]))
        for w in (xq, q, k, v, zx, zy):
            put(_col_tiles(w))
        for branch, w in ((2, "w_proj_mem"), (0, "w_proj_attn"), (1, "w_proj_lru")):
            put(_col_tiles(g[:, branch * D:(branch + 1) * D]))
            put(_col_tiles(a[w][l]))
        put(_col_tiles(a["w_out"][l]))
        ups, downs = _col_tiles(a["w_mlp_up"][l]), _row_tiles(a["w_mlp_down"][l])
        put(ups[0:1])
        for j in range(A_UP):
            if j + 1 < A_UP:
                put(ups[j + 1:j + 2])
            put(downs[j:j + 1])
    assert at == DEPTH * A_TILES
    _block_b_tiles(a, put)
    assert at == N_TILES
    return stream


def _rope_tables():
    half = A_HD // 2
    inv = (np.float32(1.0) / (np.float32(10000.0) ** (np.arange(half, dtype=np.float32) / np.float32(half)))).astype(np.float32)
    ang = np.arange(S, dtype=np.float32)[:, None] * inv[None, :]
    both = [f(ang).astype(np.float32).reshape(TB, P, half).transpose(1, 0, 2) for f in (np.cos, np.sin)]
    return [np.ascontiguousarray(t) for t in both]


def _params(a):
    par = np.zeros((DEPTH + 1, P, N_PAR), np.float32)

    def put(l, table, name, v):
        par[l, :, table[name]:table[name] + v.shape[1]] = v

    for l in range(DEPTH):
        init = 0.8 - 0.6 * math.exp(-0.3 * l)
        for name, v in (("mix_pre", a["norm_mix_pre"]), ("mlp_pre", a["norm_mlp_pre"]), ("mem", a["norm_mem"]),
                        ("b_gate", a["b_gate"]), ("conv_w", a["conv_w"]), ("conv_b", a["conv_b"]), ("rg_ba", a["rg_ba"]),
                        ("rg_bi", a["rg_bi"]), ("rg_lambda", a["rg_lambda"]), ("subln", a["diff_subln"])):
            put(l, PA, name, _feat_vector(v[l]))
        put(l, PA, "one_minus_init", np.full((P, 1), 1.0 - init, np.float32))
        put(l, PA, "init", np.full((P, 1), init, np.float32))
        for name, pair in (("lambda_q", ("lambda_q1", "lambda_q2")), ("lambda_k", ("lambda_k1", "lambda_k2"))):
            row = np.concatenate([a[n][l] for n in pair])
            put(l, PA, name, np.broadcast_to(row, (P, 128)))
    _block_b_params(a, lambda name, v: put(DEPTH, PB, name, v))
    return par


B_SIZES = [256] * 9 + [4, 256, 64, 64, 256, 32, 8]


def _block_b_tiles(a, put):
    (sq, sk, sv, mq, mk, mv, fq, fk, fv, ff, dq, dk, dv, iq, ik, iw) = np.split(a["w_in_2"][0], np.cumsum(B_SIZES)[:-1], axis=1)
    pad = lambda w, n: np.concatenate([w, np.zeros((D, n - w.shape[1]), np.float32)], axis=1)
    put(_col_tiles(pad(np.concatenate([sq, sk, mq, mk, fq, fk, dq, dk, dk, ik, ik, ik, ik, iq], axis=1), N_FEAT * 256)))
    put(_col_tiles(pad(np.concatenate([sv, mv, fv, dv, iw, ff], axis=1), N_TOK * 256)))
    for b in range(4):
        put(_col_tiles(a["w_gate_2"][0, b]))
        put(_row_tiles(a["w_branch_2"][0, b]))
    put(_col_tiles(a["w_out_2"][0]))
    gs, us = _col_tiles(a["w_up_2"][0][:, :B_FF]), _col_tiles(a["w_up_2"][0][:, B_FF:])
    downs = _row_tiles(a["w_down_2"][0])
    put(gs[0:1])
    put(us[0:1])
    for j in range(B_UP):
        if j + 1 < B_UP:
            put(gs[j + 1:j + 2])
            put(us[j + 1:j + 2])
        put(downs[j:j + 1])


def _block_b_params(a, put):
    put("mix", _feat_vector(a["norm_mix_g_2"][0]))
    put("ffn", _feat_vector(a["norm_ffn_g_2"][0]))
    put("fox_b", np.broadcast_to(a["fox_b_f_2"][0], (P, 4)))
    for name, v in (("conv_w", a["conv_w_2"][0]), ("conv_b", a["conv_b_2"][0])):
        v = v.reshape(-1, 2, B_UP, 2, P).transpose(0, 2, 1, 3, 4)
        put(name, _feat_vector(v))


def _masks():
    p, j = np.arange(P)[:, None], np.arange(P)[None, :]
    one = np.ones((P, P))
    m = [p <= j, one, -(p >= j).astype(float), -one, p < j, np.where(p < j, 0.0, NEG), np.where(j <= p, 0.0, NEG)]
    return np.ascontiguousarray(np.stack(m, axis=1).astype(np.float32).reshape(P, 7 * P))


def _t5_constants():
    n = 255 - np.arange(512)
    near = np.maximum(n, 1).astype(np.float32)
    large = 16 + (np.log(near / np.float32(16)) / np.float32(math.log(128 / 16)) * np.float32(16)).astype(np.int32)
    bucket = np.where(np.maximum(n, 0) < 16, np.maximum(n, 0), np.minimum(large, 31))
    rows = np.zeros((33, 512), np.float32)
    rows[bucket, np.arange(512)] = 1.0
    rows[32] = np.where(n < 0, NEG, 0.0)
    return rows


def kernel(**a):
    import concourse.bacc as bacc
    from concourse.bass_utils import run_bass_kernel_spmd

    a = {k: np.asarray(v) for k, v in a.items()}

    def tok(v):
        return np.ascontiguousarray(v.reshape(TB, P, -1).transpose(1, 0, 2))

    cos, sin = _rope_tables()
    arrays = {
        "stream": _weight_stream(a), "x_in": tok(a["x"][0]), "mem_in": tok(a["mem"][0]).reshape(P, TB * D), "params": _params(a),
        "post_gain": np.ascontiguousarray(np.broadcast_to(
            np.stack([a["norm_mix_post"], a["norm_mlp_post"]], 1).reshape(DEPTH, 1, 2 * D), (DEPTH, P, 2 * D))),
        "rg_w": np.ascontiguousarray(np.stack([a["rg_wa"], a["rg_wi"]], 1).transpose(0, 3, 1, 2, 4).reshape(DEPTH, P, 2048)),
        "cos_in": cos, "sin_in": sin, "ident_in": np.eye(P, dtype=np.float32), "masks_in": _masks(),
        "t5_in": np.concatenate([_t5_constants(), np.concatenate([a["t5_bias_2"], np.ones((1, 8), np.float32)])], axis=1),
        "final_gain": np.ascontiguousarray(np.broadcast_to(a["norm_final_g_2"], (P, D))),
    }
    nc = bacc.Bacc("TRN2", target_bir_lowering=False, num_devices=1)
    args = {k: nc.dram_tensor(k, v.shape, mybir.dt.from_np(v.dtype), kind="ExternalInput").ap() for k, v in arrays.items()}
    args["out"] = nc.dram_tensor("out", (P, TB, D), F32, kind="ExternalOutput").ap()
    build(nc, **args)
    got = run_bass_kernel_spmd(nc, [arrays], core_ids=[0]).results[0]["out"]
    return got.transpose(1, 0, 2).reshape(1, S, D)
```

```python
import math
from contextlib import ExitStack

import numpy as np

import concourse.bass as bass
from concourse import mybir
from concourse.alu_op_type import AluOpType as ALU

ACT = mybir.ActivationFunctionType
AX = mybir.AxisListType
F32 = mybir.dt.float32
F32R = mybir.dt.float32r
BF16 = mybir.dt.bfloat16

P = 128
D = 1024
S = 256
DEPTH = 2
KC = D // P
TB = S // P
EPS = 1e-6
NEG = -1e30
TILE = 2048
RAW, HI, LO = 4, 4, 2

A_HEADS, A_HD = 8, 64
X_HEADS, X_HD = 4, 256
A_FF = 4 * D
A_UP = A_FF // 256
B_FF = 2816
B_UP = B_FF // 256
B_HD = 64
B_TOPK = min(256, S // 4)
IDX_HEADS, IDX_HD = 8, 32
REPLACED = -3e38
OUTSIDE = -1e38

T_K, T_V, T_XQ, T_QK, T_AV, T_ZX, T_ZY = 0, 4, 8, 12, 20, 24, 28
T_GM, T_PM, T_GA, T_PA, T_GL, T_PL, T_OUT = 32, 36, 40, 44, 48, 52, 56
T_UP = 60
A_TILES = T_UP + 2 * A_UP
N_FEAT, N_TOK = 9, 4
T2_TOK = N_FEAT
T2_GATE = T2_TOK + N_TOK
T2_OUT = T2_GATE + 4 * 5
T2_FFN = T2_OUT + 4
B_TILES = T2_FFN + 3 * B_UP
FFN_ORDER = [("up", 0)] + [step for j in range(1, B_UP - 1) for step in (("up", j), ("down", j - 1))]
FFN_ORDER = FFN_ORDER[:-1] + [("up", B_UP - 1)] + [("down", j) for j in range(B_UP - 3, B_UP)]
FFN_AT, _at = {}, T2_FFN
for _step in FFN_ORDER:
    FFN_AT[_step] = _at
    _at += 2 if _step[0] == "up" else 1
assert _at == B_TILES
N_TILES = DEPTH * A_TILES + B_TILES
SKEW = 3 * P
assert A_TILES % RAW == 0 and N_TILES % 2 == 0

_ACT_TILES = [t for t in range(T_UP) if not (T_QK <= t < T_AV or T_PM <= t < T_GA or T_PA <= t < T_GL or T_PL <= t)]
_DVE_TILES = [t for t in range(T_UP - 1) if t not in _ACT_TILES]
ACT_EVAC = {t: n + 1 for n, t in enumerate(_ACT_TILES)}
DVE_EVAC = {t: n + 1 for n, t in enumerate(_DVE_TILES)}
N_ACT_EVAC, N_DVE_EVAC = len(_ACT_TILES), len(_DVE_TILES)

def _columns(*sizes):
    at, out = 0, {}
    for name, n in sizes:
        out[name] = at
        at += n
    return out, at


PA, _na = _columns(("mix_pre", 8), ("mlp_pre", 8), ("mem", 8), ("b_gate", 24), ("conv_w", 32), ("conv_b", 8),
                   ("rg_ba", 8), ("rg_bi", 8), ("rg_lambda", 8), ("subln", 1), ("one_minus_init", 1), ("init", 1),
                   ("lambda_q", 128), ("lambda_k", 128))
PB, _nb = _columns(("mix", 8), ("ffn", 8), ("fox_b", 4), ("conv_w", 3 * 4 * B_UP), ("conv_b", 4 * B_UP))
N_PAR = max(_na, _nb)

DVE_STEPS, ACT_STEPS = 53, 1


def build(nc, stream, x_in, mem_in, params, post_gain, rg_w, cos_in, sin_in, ident_in, masks_in, t5_in,
          final_gain, out):
    mem_normed = nc.dram_tensor("mem_normed", (P, KC * S), F32, kind="Internal").ap()
    t5_rows = nc.dram_tensor("t5_rows", (8, 512), F32, kind="Internal").ap()
    t5_skewed = nc.dram_tensor("t5_skewed", (8, P, SKEW + 1), F32, kind="Internal").ap()
    with ExitStack() as ctx:
        def sb(name, shape, dt=F32):
            return ctx.enter_context(nc.sbuf_tensor(name, shape, dt))

        def sem(name):
            return ctx.enter_context(nc.semaphore(name))

        w_raw = sb("w_raw", [P, RAW, TILE])
        w_hi = sb("w_hi", [P, HI, TILE], F32R)
        w_lo = sb("w_lo", [P, LO, TILE], F32R)
        raw_loaded = [sem(f"raw_loaded{s}") for s in range(RAW)]
        hi_ready = sem("hi_ready")
        lo_ready = [sem("lo_even_ready"), sem("lo_odd_ready")]
        half_done = sem("half_done")
        tile_done = sem("tile_done")

        x = sb("x", [P, TB, D])
        op_hi = [sb("opA_hi", [P, KC, S], F32R), sb("opB_hi", [P, KC, S], F32R)]
        op_lo = [sb("opA_lo", [P, KC, S], F32R), sb("opB_lo", [P, KC, S], F32R)]
        B = [sb(f"B{n}", [P, 2080 if n == 0 else 2048]) for n in range(7)]
        merged = sb("merged", [P, 2048])
        gate = sb("gate", [P, 2048])
        expd = sb("expd", [P, 4, 256])
        probs_t = sb("probs_t", [P, 512])
        par = sb("par", [P, N_PAR])
        cos = sb("cos", [P, TB, 32])
        sin = sb("sin", [P, TB, 32])
        ident = sb("ident", [P, P])
        small = sb("small", [P, 96])
        rowmask = sb("rowmask", [P, P], BF16)
        colmask = sb("colmask", [P, 64], BF16)
        diag = sb("diag", [P, TB, P])
        eps = sb("eps", [P, 1])
        psum = ctx.enter_context(nc.psum_tensor("psum", [P, 8, 512], F32))

        def tok(buf):
            return buf[:, 0:2048].rearrange("p (b f) -> p b f", b=TB)

        def feat(buf):
            return buf[:, 0:2048].rearrange("p (c t) -> p c t", c=KC)

        k_mem, v_mem, q_t, k_t, v_a, q_mem, o_a = feat(B[0]), tok(B[1]), feat(B[2]), feat(B[3]), tok(B[4]), feat(B[5]), tok(B[6])
        zx = B[0][:, :].rearrange("p (c t) -> p c t", c=KC)
        xc, gz = feat(B[1]), feat(B[5])
        r_g, i_g, t_g, lru = feat(B[2]), feat(B[3]), feat(B[4]), feat(B[6])
        rgw = B[0][:, 0:2048].rearrange("p (g c d) -> p g c d", g=2, c=KC)
        y_tok = tok(B[1])
        gains = tok(B[4])
        relu_u, squared = B[2][:, 0:1024].rearrange("p (b n) -> p b n", b=2), B[3][:, 0:1024].rearrange("p (b n) -> p b n", b=2)
        rot = merged[:, 0:1024].rearrange("p (b n) -> p b n", b=2)
        rope_a, rope_b = gate[:, 0:512], gate[:, 512:1024]

        def sm(a, n=1):
            return small[:, a:a + n]
        SS, VAR, SD, RS, NMAX, ZSUM, RZ, R2 = 0, 16, 32, 48, 64, 68, 72, 76
        NLAM, GSUB, SP_POS, SP_NEG = 78, 79, 80, 88
        prep = sb("prep", [P, 160])

        ident_loaded, rope_in, x_loaded, par_in, mem_loaded, rgw_in, gain_in, out_done = (sem(n) for n in (
            "ident_loaded", "rope_in", "x_loaded", "par_in", "mem_loaded", "rgw_in", "gain_in", "out_done"))
        mem_half_in = [sem(f"mem_half_in{b}") for b in range(TB)]
        mem_copied, mem_stored = sem("mem_copied"), sem("mem_stored")
        norm_ss, sub_ss, norm_sd, norm_x = (sem(n) for n in ("norm_ss", "sub_ss", "norm_sd", "norm_x"))
        turned = sem("turned")
        op_hi_done = sem("op_hi_done")
        op_ready = sem("op_ready")
        act_evac, dve_evac = sem("act_evac"), sem("dve_evac")
        par_d, par_a = sem("par_d"), sem("par_a")
        rope_turned, rope_evac, rope_ready = sem("rope_turned"), sem("rope_evac"), sem("rope_ready")
        x_scores, x_max, x_exp, x_probs, x_turned, x_pt, x_out = (sem("x_" + n) for n in (
            "scores", "max", "exp", "probs", "turned", "pt", "out"))
        d_scores, d_max, d_exp, d_probs, d_turned, d_pt, d_out, d_kept = (sem("d_" + n) for n in (
            "scores", "max", "exp", "probs", "turned", "pt", "out", "kept"))
        conv_done, rg_done, rg_evac, lru_ta, lru_v, lru_s, lru_y, gelu_done = (sem(n) for n in (
            "conv_done", "rg_done", "rg_evac", "lru_ta", "lru_v", "lru_s", "lru_y", "gelu_done"))
        lru_u = sem("lru_u")
        masks_ready = sem("masks_ready")
        out_ss, post_ss, post_var, post_sd, post_gained = (sem(n) for n in ("out_ss", "post_ss", "post_var", "post_sd", "post_gained"))
        x_ready = sem("x_ready")
        squared_done, ffn_hi = sem("squared_done"), sem("ffn_hi")
        zx_padded = sem("zx_padded")
        mem_gate, merged_part = sem("mem_gate"), sem("merged_part")
        relu_done, ffn_ready = sem("relu_done"), sem("ffn_ready")
        dve_step, act_step, rs_ready = sem("dve_step"), sem("act_step"), sem("rs_ready")

        MEM_OP, MIX_OP, X_OP, SUB_OP, LRU_OP, OUT_OP, MLP_OP, N_OPS = 0, 1, 2, 3, 4, 5, 6, 7
        HI_PARTS = 4 * KC + 4 + 1 + 4
        B_MIX, B_BRANCH, B_OUT, B_FFN = 0, 4, 12, 16
        MIX, SUB, MLP, N_NORMS = 1, 2, 3, 3
        OUT_BANKS = (3, 0)
        NORM_AT, NORM_COUNT = {MIX: 2, SUB: 4, MLP: 5}, 5

        f_b = [feat(B[0])[:, c, :] for c in range(8)] + [feat(B[1])[:, c, :] for c in range(8)] \
            + [B[2][:, c * S:(c + 1) * S] for c in range(2)]
        SB_Q, SB_K, MB_Q, MB_K, FX_Q, FX_K, DS_Q, DS_K, IX_K, IX_Q = 0, 2, 4, 6, 8, 10, 12, 14, 15, 16
        v_b = tok(B[3])
        V_COL, W_COL, F_COL = (0, 256, 512, 768), 832, 840
        bias_b = [B[4 + h // 4][:, (h % 4) * 512:(h % 4 + 1) * 512].rearrange("p (b n) -> p b n", b=TB) for h in range(8)]
        index = B[2][:, 512:1024].rearrange("p (b n) -> p b n", b=TB)
        minus_c_row = B[2][:, 1024:2048].rearrange("p (h n) -> p h n", h=4)
        log_f_wide = merged[:, 0:1024].rearrange("p (a n) -> p a n", n=P)
        up_to, ones_p, neg_from, neg_all, before01, before_neg, causal = (
            B[6][:, n * P:(n + 1) * P] for n in range(7))
        log_f, c_col = prep[:, 16:24], prep[:, 24:32]
        padded = B[0][:, 0:2064].rearrange("p (s c t) -> p s c t", s=2, c=4)
        conved = B[1][:, 0:2048].rearrange("p (s c t) -> p s c t", s=2, c=4)
        gelu_g = B[2][:, 0:1024].rearrange("p (s n) -> p s n", s=2)
        gated = B[3][:, 0:1024].rearrange("p (s n) -> p s n", s=2)

        def gate_bank(b, n):
            return (n + T2_GATE) % 4 if b == 0 else n

        (t5_loaded, t5_rows_ready, t5_evac, t5_stored, t5_skewed_in, bias_in, b_masks_in, final_in) = (sem(n) for n in (
            "t5_loaded", "t5_rows_ready", "t5_evac", "t5_stored", "t5_skewed_in", "bias_in", "b_masks_in", "final_in"))
        b_ss, b_sd, b_x, b_turned, b_hi, b_ready = (sem("b_" + n) for n in (
            "ss", "sd", "x", "turned", "hi", "ready"))
        b_bank = sem("b_bank")
        gate_open = sem("gate_open")
        x_part, xb_ss, xb_sum, y_done = sem("x_part"), sem("xb_ss"), sem("xb_sum"), sem("y_done")
        b_evac_a, b_evac_d = sem("b_evac_a"), sem("b_evac_d")
        ix_scores, ix_relu, ix_added = sem("ix_scores"), sem("ix_relu"), sem("ix_added")
        f_in, f_ln, f_wide, c_sums, c_kept = (sem(n) for n in ("f_in", "f_ln", "f_wide", "c_sums", "c_kept"))
        sb_z, sb_ln, sb_masked, sb_summed, sb_w = (sem("sb_" + n) for n in ("z", "ln", "masked", "summed", "w"))
        s_scores, s_max, s_exp, s_probs, s_turned, s_pt = (sem("s_" + n) for n in (
            "scores", "max", "exp", "probs", "turned", "pt"))
        b_out = sem("b_out")
        b_mixed = sem("b_mixed")
        out_part, x_b = sem("out_part"), sem("x_b")
        pads_zero = sem("pads_zero")
        f_evac, f_conv, f_gelu, f_gated, f_hi, f_ready = (sem("f_" + n) for n in ("evac", "conv", "gelu", "gated", "hi", "ready"))
        b_step = sem("b_step")

        class Steps:
            def __init__(self, eng, s, per_layer):
                self.eng, self.s, self.per_layer, self.base, self.n = eng, s, per_layer, 0, 0

            def __call__(self, ins):
                ins.then_inc(self.s, 1)
                self.n += 1
                self.eng.wait_ge(self.s, self.base + self.n)

        block = ctx.enter_context(nc.Block())

        @block.sync
        def _(sp):
            for b in range(TB):
                sp.dma_start(tok(B[6])[:, b, :], mem_in[:, b * D:(b + 1) * D]).then_inc(mem_half_in[b], 16)
            for s in range(RAW):
                sp.dma_start(w_raw[:, s, :], stream[s]).then_inc(raw_loaded[s], 16)
            sp.wait_ge(t5_evac, 1)
            sp.dma_start(t5_rows, B[1][0:8, 1024:1536]).then_inc(t5_stored, 16)
            sp.wait_ge(t5_stored, 16)
            for h in range(8):
                row = bass.AP(tensor=t5_rows.tensor, offset=t5_rows.offset + h * 512, ap=[[0, P], [1, SKEW]])
                sp.dma_start(t5_skewed[h, :, 0:SKEW], row).then_inc(t5_skewed_in, 16)
            groups = N_TILES // RAW
            with sp.Fori(1, groups) as g:
                for s in range(RAW):
                    sp.wait_ge(lo_ready[s % 2], g * RAW + (s - RAW + 2 - s % 2))
                    sp.dma_start(w_raw[:, s, :], stream[g * RAW + s]).then_inc(raw_loaded[s], 16)
            for t in range(groups * RAW, N_TILES):
                sp.wait_ge(lo_ready[t % 2], t - RAW + 2 - t % 2)
                sp.dma_start(w_raw[:, t % RAW, :], stream[t]).then_inc(raw_loaded[t % RAW], 16)
            sp.wait_ge(out_done, TB * 2 * 16)

        @block.gpsimd
        def _(pool):
            def rest(t, s, first=False):
                pool.wait_ge(hi_ready, t + 1)
                if not first:
                    pool.wait_ge(tile_done, t - (LO - 1))
                nc.gpsimd.tensor_tensor(w_lo[:, s % LO, :], w_raw[:, s % RAW, :], w_hi[:, s % HI, :].bitcast(F32),
                                        ALU.subtract).then_inc(lo_ready[1], 2)

            for t in (1, 3):
                rest(t, t, t < LO)
            with pool.Fori(1, N_TILES // 4) as g:
                for s in (1, 3):
                    rest(g * 4 + s, s)
            for t in range(N_TILES // 4 * 4, N_TILES):
                if t % 2:
                    rest(t, t)

        @block.tensor
        def _(pe):
            def passes(t, s, product, piece=None):
                pe.wait_ge(hi_ready, t + 1)
                pieces = [range(KC)] if piece is None else [(2 * g, 2 * g + 1) for g in range(KC // 2)]
                for g, ks in enumerate(pieces):
                    if piece is not None:
                        piece(g)[0]()
                    product(w_hi[:, s % HI, :], 0, ks, g == 0, False)
                    if piece is not None:
                        piece(g)[1]()
                    product(w_hi[:, s % HI, :], 1, ks, False, False)
                    if g == 0:
                        pe.wait_ge(lo_ready[s % 2], t + (2 - s % 2))
                    ins = product(w_lo[:, s % LO, :], 0, ks, False, g == len(pieces) - 1)
                ins.then_inc(tile_done, 1)

            def col_feat(t, s, bank, op, piece=None):
                parts = (op_hi[op], op_lo[op])

                def product(w, a, ks, first, last):
                    w = w.rearrange("p (k n) -> p k n", k=KC)
                    for c in range(2):
                        for k in ks:
                            ins = nc.tensor.matmul(psum[:, bank, c * S:(c + 1) * S], w[:, k, c * P:(c + 1) * P],
                                                   parts[a][:, k, :], start=(first and c == 0 and k == 0),
                                                   stop=(last and k == KC - 1), skip_group_check=True)
                    return ins
                passes(t, s, product, piece)

            def col_tok(t, s, bank, op, piece=None):
                parts = (op_hi[op], op_lo[op])

                def product(w, a, ks, first, last):
                    w = w.rearrange("p (k n) -> p k n", k=KC)
                    for b in range(TB):
                        for k in ks:
                            ins = nc.tensor.matmul(psum[:, bank, b * 256:(b + 1) * 256], parts[a][:, k, b * P:(b + 1) * P],
                                                   w[:, k, :], start=(first and b == 0 and k == 0),
                                                   stop=(last and k == KC - 1), skip_group_check=True)
                    return ins
                passes(t, s, product, piece)

            def row_tok(t, s, slot, first_tile):
                parts = (op_hi[1], op_lo[1])

                def product(w, a, ks, first, last):
                    w = w.rearrange("p (k n) -> p k n", k=2)
                    for b in range(TB):
                        for n in range(2):
                            for k in range(2):
                                ins = nc.tensor.matmul(psum[:, 4 + 2 * b + n, :], parts[a][:, 2 * slot + k, b * P:(b + 1) * P],
                                                       w[:, k, n * 512:(n + 1) * 512], start=(first_tile and first and k == 0),
                                                       stop=False, skip_group_check=True)
                    return ins
                passes(t, s, product)

            def turn(src, signal, half_ready):
                for b in range(TB):
                    pe.wait_ge(norm_x if signal is turned else b_x, half_ready + b)
                    for c in range(KC):
                        ins = nc.tensor.matmul(psum[:, 4 + c // 2, (c % 2) * S + b * P:(c % 2) * S + (b + 1) * P],
                                               src[:, b, c * P:(c + 1) * P], diag[:, b, :], start=True, stop=True)
                        if b and c % 2:
                            ins.then_inc(signal, 1)

            def transpose(src, normed):
                pe.wait_ge(norm_x, normed)
                for c in range(KC):
                    for b in range(TB):
                        ins = nc.tensor.transpose(psum[:, 4 + c // 2, (c % 2) * S + b * P:(c % 2) * S + (b + 1) * P],
                                                  src[:, b, c * P:(c + 1) * P], ident[:])
                    if c % 2:
                        ins.then_inc(turned, 1)

            def out_tile(t, s, op):
                pe.wait_ge(hi_ready, t + 1)
                pe.wait_ge(lo_ready[s % 2], t + (2 - s % 2))
                for b in range(TB):
                    for i, (w, part) in enumerate(((w_hi[:, s % HI, :], op_hi), (w_hi[:, s % HI, :], op_lo), (w_lo[:, s % LO, :], op_hi))):
                        w = w.rearrange("p (k n) -> p k n", k=KC)
                        for k in range(KC):
                            ins = nc.tensor.matmul(psum[:, OUT_BANKS[b], 0:256], part[op][:, k, b * P:(b + 1) * P], w[:, k, :],
                                                   start=(i == 0 and k == 0), stop=(i == 2 and k == KC - 1))
                    ins.then_inc(tile_done if b else half_done, 1)

            def row_tok_end(t, s, slot):
                pe.wait_ge(hi_ready, t + 1)
                pe.wait_ge(lo_ready[s % 2], t + (2 - s % 2))
                for b in range(TB):
                    for w, part in ((w_hi[:, s % HI, :], op_hi), (w_hi[:, s % HI, :], op_lo), (w_lo[:, s % LO, :], op_hi)):
                        w = w.rearrange("p (k n) -> p k n", k=2)
                        for n in range(2):
                            for k in range(2):
                                ins = nc.tensor.matmul(psum[:, 4 + 2 * b + n, :], part[1][:, 2 * slot + k, b * P:(b + 1) * P],
                                                       w[:, k, n * 512:(n + 1) * 512], start=False, stop=(k == 1),
                                                       skip_group_check=True)
                    ins.then_inc(tile_done if b else half_done, 1)

            turn(tok(B[6]), turned, 1)
            pe.wait_ge(t5_loaded, 16)
            nc.tensor.matmul(psum[0:8, 3, :], B[1][0:33, 512:520], B[1][0:33, 0:512], start=True, stop=True).then_inc(t5_rows_ready, 1)
            pe.wait_ge(masks_ready, 4)
            with pe.Fori(0, DEPTH) as l:
                T = l * A_TILES

                def ready(op, g=3):
                    pe.wait_ge(op_ready, l * (4 * N_OPS) + (4 * op + g + 1))

                def operand_pieces(op, his, his_a_piece):
                    return lambda g: (lambda: pe.wait_ge(op_hi_done, l * HI_PARTS + his + his_a_piece * (g + 1)),
                                      lambda: ready(op, g))

                def tile(t, product, op, piece=None):
                    if t >= 4:
                        if t - 4 in ACT_EVAC:
                            pe.wait_ge(act_evac, l * N_ACT_EVAC + ACT_EVAC[t - 4])
                        else:
                            pe.wait_ge(dve_evac, l * N_DVE_EVAC + DVE_EVAC[t - 4])
                    product(T + t, t, t % 4, op, piece)

                for t in range(T_K, T_V):
                    if t == 3:
                        pe.wait_ge(t5_evac, 1)
                    tile(t, col_feat, 0, operand_pieces(MEM_OP, 0, 2) if t == T_K else None)
                pe.wait_ge(mem_copied, 1)
                transpose(tok(gate), l * NORM_COUNT + (NORM_AT[MIX] + 2))
                for t in range(T_V, T_XQ):
                    tile(t, col_tok, 0)
                ready(MIX_OP)
                for t in range(T_XQ, T_QK):
                    tile(t, col_feat, 1)

                def rope_turn(i):
                    pe.wait_ge(rope_ready, l * 8 + i + 1)
                    if i:
                        pe.wait_ge(rope_evac, l * 8 + i)
                    for c in range(2):
                        for b in range(TB):
                            ins = nc.tensor.transpose(psum[:, 5, c * S + b * P:c * S + (b + 1) * P],
                                                      rot[:, i % 2, b * 256 + c * P:b * 256 + (c + 1) * P], ident[:])
                    ins.then_inc(rope_turned, 1)

                def x_score(h):
                    pe.wait_ge(act_evac, l * N_ACT_EVAC + ACT_EVAC[T_XQ + 3])
                    for b in range(TB):
                        for k in range(2):
                            ins = nc.tensor.matmul(psum[:, 4, b * 256:(b + 1) * 256], q_mem[:, 2 * h + k, b * P:(b + 1) * P],
                                                   k_mem[:, 2 * h + k, :], start=(k == 0), stop=(k == 1))
                    ins.then_inc(x_scores, 1)

                def x_turn(h):
                    pe.wait_ge(x_probs, l * X_HEADS + h + 1)
                    for k in range(TB):
                        for b in range(TB):
                            ins = nc.tensor.transpose(psum[:, 6, k * 256 + b * P:k * 256 + (b + 1) * P],
                                                      expd[:, b, k * P:(k + 1) * P], ident[:])
                    ins.then_inc(x_turned, 1)

                def x_values(h):
                    pe.wait_ge(x_pt, l * X_HEADS + h + 1)
                    if h:
                        ready(X_OP, h - 1)
                    for c in range(2):
                        for k in range(TB):
                            ins = nc.tensor.matmul(psum[:, 7, c * S:(c + 1) * S], v_mem[:, k, h * X_HD + c * P:h * X_HD + (c + 1) * P],
                                                   probs_t[:, k * 256:(k + 1) * 256], start=(k == 0), stop=(k == 1))
                    ins.then_inc(x_out, 1)

                for i in range(8):
                    tile(T_QK + i, col_tok, 1)
                    if i:
                        rope_turn(i - 1)
                    if i % 2 == 0:
                        if i:
                            x_values(i // 2 - 1)
                        x_score(i // 2)
                    else:
                        x_turn(i // 2)
                tile(T_AV, col_tok, 1)
                rope_turn(7)
                x_values(3)
                for t in range(T_AV + 1, T_ZX):
                    tile(t, col_tok, 1)

                def d_score(h):
                    if h == 0:
                        pe.wait_ge(rope_evac, l * 8 + 8)
                    for m in range(2):
                        q = slice(64 * m, 64 * m + 64)
                        for b in range(TB):
                            n = (b + 1) * P
                            nc.tensor.matmul(psum[:, 4 + m, b * 256:b * 256 + n], q_t[q, h, b * P:(b + 1) * P], k_t[q, h, 0:n],
                                             start=True, stop=False, skip_group_check=True)
                            ins = nc.tensor.matmul(psum[:, 4 + m, b * 256 + n - 64:b * 256 + n], rowmask[64 * m:64 * m + 1, :],
                                                   colmask[64 * m:64 * m + 1, :], start=False, stop=True, skip_group_check=True)
                    ins.then_inc(d_scores, 1)

                def d_turn(h):
                    pe.wait_ge(d_probs, l * A_HEADS + h + 1)
                    for b in range(TB):
                        nc.tensor.transpose(psum[:, 6, b * P:(b + 1) * P], expd[:, b, 0:P], ident[:])
                    nc.tensor.transpose(psum[:, 6, 256:384], expd[:, 1, P:2 * P], ident[:]).then_inc(d_turned, 1)

                def d_values(h):
                    pe.wait_ge(d_pt, l * A_HEADS + h + 1)
                    pe.wait_ge(act_evac, l * N_ACT_EVAC + ACT_EVAC[T_AV + 3])
                    if h:
                        pe.wait_ge(d_kept, l * A_HEADS + h)
                    v = slice(h * P, (h + 1) * P)
                    nc.tensor.matmul(psum[:, 7, 0:P], probs_t[:, 0:P], v_a[:, 0, v], start=True, stop=True)
                    nc.tensor.matmul(psum[:, 7, P:2 * P], probs_t[:, P:2 * P], v_a[:, 0, v], start=True, stop=False)
                    nc.tensor.matmul(psum[:, 7, P:2 * P], probs_t[:, 256:384], v_a[:, 1, v], start=False, stop=True).then_inc(d_out, 1)

                for h in range(A_HEADS):
                    t = T_ZX + 2 * h
                    d_score(h)
                    if t == T_PM:
                        ready(X_OP)
                    tile(t, col_feat, 0 if t >= T_PM else 1)
                    d_turn(h)
                    tile(t + 1, col_feat, 0 if t >= T_PM else 1)
                    d_values(h)

                def rg(c):
                    if c == 0:
                        pe.wait_ge(rgw_in, l * 16 + 16)
                    if c == 3:
                        pe.wait_ge(d_kept, l * A_HEADS + A_HEADS)
                    if c >= 4:
                        pe.wait_ge(rg_evac, l * KC + c - 3)
                    for g in range(2):
                        ins = nc.tensor.matmul(psum[:, 4 + c % 4, g * S:(g + 1) * S], rgw[:, g, c, :], xc[:, c, :], start=True, stop=True)
                    ins.then_inc(rg_done, 1)

                for n in range(2):
                    tile(T_GA + n, col_feat, 1)
                    for c in range(4):
                        rg(4 * n + c)
                tile(T_GA + 2, col_feat, 1)
                pe.wait_ge(rg_evac, l * KC + KC)
                transpose(o_a, l * NORM_COUNT + (NORM_AT[SUB] + 1))
                tile(T_GA + 3, col_feat, 1)
                ready(SUB_OP)
                for t in range(T_PA, T_GL):
                    tile(t, col_feat, 0)
                for t in range(T_GL, T_PL):
                    tile(t, col_feat, 1)
                ready(LRU_OP)
                for t in range(T_PL, T_OUT):
                    tile(t, col_feat, 0)
                for t in range(T_OUT, T_UP - 1):
                    tile(t, col_tok, 1, operand_pieces(OUT_OP, HI_PARTS - KC - 4, 1) if t == T_OUT else None)
                pe.wait_ge(dve_evac, l * N_DVE_EVAC + DVE_EVAC[T_OUT])
                out_tile(T + (T_UP - 1), T_UP - 1, 1)

                turn(x, turned, l * NORM_COUNT + (NORM_AT[MLP] + 1))

                def up(j, t, s, slot, first=False):
                    if not first:
                        pe.wait_ge(relu_done, l * A_UP + j - 1)
                    col_feat(T + t, s, slot, 0, operand_pieces(MLP_OP, HI_PARTS - KC, 2) if first == "operand" else None)

                def down(j, t, s, slot, first=False):
                    pe.wait_ge(ffn_ready, l * A_UP + j + 1)
                    row_tok(T + t, s, slot, first)

                up(0, T_UP, T_UP, 0, "operand")
                up(1, T_UP + 1, T_UP + 1, 1, True)
                down(0, T_UP + 2, T_UP + 2, 0, True)
                with pe.Fori(0, A_UP // 2 - 1) as i:
                    t0 = T_UP + 3
                    up(i * 2 + 2, i * 4 + t0, t0, 0)
                    down(i * 2 + 1, i * 4 + t0 + 1, t0 + 1, 1)
                    up(i * 2 + 3, i * 4 + t0 + 2, t0 + 2, 1)
                    down(i * 2 + 2, i * 4 + t0 + 3, t0 + 3, 0)
                pe.wait_ge(ffn_ready, l * A_UP + A_UP)
                row_tok_end(T + (A_TILES - 1), A_TILES - 1, 1)

            T0 = DEPTH * A_TILES

            def row_feat(t, s, lo_wait):
                parts = (op_hi[1], op_lo[1])
                pe.wait_ge(hi_ready, t + 1)
                pe.wait_ge(lo_ready[s % 2], t + (2 - s % 2))
                for n in range(4):
                    for i, (w, a) in enumerate(((w_hi[:, s % HI, :], 0), (w_hi[:, s % HI, :], 1), (w_lo[:, s % LO, :], 0))):
                        w = w.rearrange("p (k n) -> p k n", k=2)
                        if n == 0 and a == 1:
                            lo_wait()
                        for c in (2 * n, 2 * n + 1):
                            for k in range(2):
                                ins = nc.tensor.matmul(psum[:, n, (c % 2) * S:(c % 2 + 1) * S], w[:, k, c * P:(c + 1) * P],
                                                       parts[a][:, k, :], start=(i == 0 and c % 2 == 0 and k == 0),
                                                       stop=(i == 2 and k == 1), skip_group_check=True)
                    ins.then_inc(tile_done if n == 3 else b_bank, 1)

            def b_piece(op, his, his_a_piece):
                return lambda g: (lambda: pe.wait_ge(b_hi, his + his_a_piece * (g + 1)), lambda: pe.wait_ge(b_ready, op + g + 1))

            turn(x, b_turned, 1)
            for t in range(N_FEAT + N_TOK):
                if t >= 4:
                    pe.wait_ge(b_evac_a, t - 3)
                (col_feat if t < N_FEAT else col_tok)(T0 + t, t, t % 4, 0, b_piece(B_MIX, 0, 2) if t == 0 else None)

            def gate_tile(b, n):
                t = T2_GATE + 5 * b + n
                if b == 0:
                    pe.wait_ge(b_evac_a, N_FEAT + n + 1)
                else:
                    pe.wait_ge(b_evac_d, 4 * (b - 1) + n + 1)
                col_feat(T0 + t, t, gate_bank(b, n), 0)

            def index_scores(h):
                if h >= 4:
                    pe.wait_ge(ix_relu, h - 3)
                r = slice(32 * (h % 4), 32 * (h % 4) + 32)
                for b in range(TB):
                    ins = nc.tensor.matmul(psum[:, 4 + h % 4, b * 256:b * 256 + (b + 1) * P], f_b[IX_Q + h // 4][r, b * P:(b + 1) * P],
                                           f_b[IX_K][r, 0:(b + 1) * P], start=True, stop=True)
                ins.then_inc(ix_scores, 1)

            gate_tile(0, 0)
            pe.wait_ge(b_evac_a, N_FEAT + N_TOK)
            pe.wait_ge(b_masks_in, 16)
            for h in range(4):
                index_scores(h)
            gate_tile(0, 1)
            for h in range(4, IDX_HEADS):
                index_scores(h)

            def c_rows(h0):
                pe.wait_ge(f_wide, 1)
                for h in (h0, h0 + 1):
                    row = psum[:, 4 + 2 * (h // 2), (h % 2) * S:(h % 2 + 1) * S]
                    nc.tensor.matmul(row, log_f_wide[:, h, :], B[6][:, 0:2 * P], start=True, stop=False)
                    ins = nc.tensor.matmul(row[:, P:2 * P], log_f_wide[:, 4 + h, :], up_to, start=False, stop=True)
                ins.then_inc(c_sums, 1)

            def c_columns():
                nc.tensor.matmul(psum[:, 5, 0:4], up_to, log_f[:, 0:4], start=True, stop=True)
                nc.tensor.matmul(psum[:, 5, 4:8], ones_p, log_f[:, 0:4], start=True, stop=False)
                nc.tensor.matmul(psum[:, 5, 4:8], up_to, log_f[:, 4:8], start=False, stop=True).then_inc(c_sums, 1)

            def rows_of(h):
                return slice(64 * (h % 2), 64 * (h % 2) + 64)

            def values(b, h):
                if h % 2 == 0 and (b or h):
                    pe.wait_ge(b_ready, B_BRANCH + 2 * b + h // 2)
                col = V_COL[b] + (64 * h if b < 3 else 0)
                o = psum[rows_of(h), 7, (h // 2) * S:(h // 2 + 1) * S]
                nc.tensor.matmul(o, v_b[:, 0, col:col + 64], probs_t[:, 0:256], start=True, stop=False, skip_group_check=True)
                nc.tensor.matmul(o[:, P:2 * P], v_b[:, 1, col:col + 64], probs_t[:, 256:384], start=False, stop=True,
                                 skip_group_check=True).then_inc(b_out, 1)

            def sb_logits(h):
                if h < 2:
                    pe.wait_ge(ix_relu, 5 + h)
                r = rows_of(h)
                k, q = f_b[SB_K + h // 2], f_b[SB_Q + h // 2]
                nc.tensor.matmul(psum[:, 4 + h % 2, 0:256], k[r, 0:P], q[r, :], start=True, stop=False, skip_group_check=True)
                nc.tensor.matmul(psum[:, 4 + h % 2, 256:384], k[r, P:2 * P], q[r, P:2 * P], start=False, stop=False,
                                 skip_group_check=True).then_inc(sb_z, 1)

            def sb_sums(h):
                pe.wait_ge(sb_masked, h + 1)
                m = expd[:, 2 * (h % 2):2 * (h % 2) + 2, :].rearrange("p a n -> p (a n)")
                z = psum[:, 4 + h % 2, :]
                for dst, w, src in ((z[:, 0:P], ident[:], before_neg), (z[:, 256:384], ident[:], before_neg),
                                    (z[:, 0:256], neg_from, m[:, 0:256]), (z[:, P:256], neg_all, m[:, 256:384]),
                                    (z[:, 256:384], neg_from, m[:, 256:384])):
                    ins = nc.tensor.matmul(dst, w, src, start=False, stop=True, skip_group_check=True)
                ins.then_inc(sb_summed, 1)

            sb_logits(0)
            for h in range(4):
                if h % 2 == 0:
                    gate_tile(0, 2 + h // 2)
                else:
                    c_rows(2 if h == 1 else 0)
                sb_sums(h)
                if h < 3:
                    sb_logits(h + 1)
                pe.wait_ge(sb_w, h + 1)
                values(0, h)
            c_columns()

            def s_score(b, h):
                g = 4 * (b - 1) + h
                if g >= 2:
                    pe.wait_ge(s_probs, g - 1)
                r = rows_of(h)
                q = f_b[(None, MB_Q, FX_Q, DS_Q)[b] + h // 2]
                k = f_b[DS_K] if b == 3 else f_b[(None, MB_K, FX_K)[b] + h // 2]
                for u in range(TB):
                    ins = nc.tensor.matmul(psum[:, 4 + h % 2, u * 256:u * 256 + (u + 1) * P], q[r, u * P:(u + 1) * P],
                                           k[r, 0:(u + 1) * P], start=True, stop=True)
                ins.then_inc(s_scores, 1)

            def s_turn(b, h):
                g = 4 * (b - 1) + h
                pe.wait_ge(s_probs, g + 1)
                e = 2 * (h % 2)
                for u in range(TB):
                    nc.tensor.transpose(psum[:, 6, u * P:(u + 1) * P], expd[:, e + u, 0:P], ident[:])
                nc.tensor.transpose(psum[:, 6, 256:384], expd[:, e + 1, P:2 * P], ident[:]).then_inc(s_turned, 1)

            def branch_product(b):
                pe.wait_ge(b_evac_a, N_FEAT + N_TOK + 4 * (b + 1))
                if b:
                    pe.wait_ge(b_evac_d, 4 * b)
                pe.wait_ge(b_hi, KC + 2 * (b + 1))
                t = T2_GATE + 5 * b + 4
                row_feat(T0 + t, t, lambda: pe.wait_ge(b_ready, B_BRANCH + 2 * b + 2))

            for b in range(1, 4):
                branch_product(b - 1)
                if b == 1:
                    pe.wait_ge(c_kept, 2)
                    s_score(1, 0)
                for h in range(4):
                    gate_tile(b, h)
                    s_turn(b, h)
                    if h < 3:
                        s_score(b, h + 1)
                    elif b < 3:
                        s_score(b + 1, 0)
                    pe.wait_ge(s_pt, 4 * (b - 1) + h + 1)
                    values(b, h)
            branch_product(3)

            for n in range(4):
                pe.wait_ge(b_evac_d, 12 + n + 1)
                t = T2_OUT + n
                if n < 3:
                    col_tok(T0 + t, t, n, 0, b_piece(B_OUT, 2 * KC, 1) if n == 0 else None)
                else:
                    pe.wait_ge(x_part, 1)
                    out_tile(T0 + t, t, 0)

            turn(x, b_turned, 3)

            def f_up(j):
                t = FFN_AT["up", j]
                for n in range(2):
                    if j >= 2:
                        pe.wait_ge(f_evac, 2 * (j - 2) + n + 1)
                    col_feat(T0 + t + n, t + n, 2 * (j % 2) + n, 0, b_piece(B_FFN, 2 * KC + 4, 2) if j == n == 0 else None)

            def f_down(j):
                t = FFN_AT["down", j]
                pe.wait_ge(f_ready, j + 1)
                if j < B_UP - 1:
                    row_tok(T0 + t, t, j % 4, j == 0)
                else:
                    row_tok_end(T0 + t, t, j % 4)

            for kind, j in FFN_ORDER:
                (f_up if kind == "up" else f_down)(j)

        @block.scalar
        def _(act):
            act.preload_act_table_set("sqrt_and_others")
            act.dma_start(ident[:], ident_in).then_inc(ident_loaded, 16)
            act.dma_start(par[:], params[0]).then_inc(par_in, 16)
            act.dma_start(B[1][0:33, 0:520], t5_in).then_inc(t5_loaded, 16)
            step = Steps(act, act_step, ACT_STEPS)

            def round_tile(s, round_of_slot):
                act.wait_ge(raw_loaded[s], round_of_slot * 16 + 16)
                nc.scalar.activation(w_hi[:, s, :], w_raw[:, s, :], ACT.Identity).then_inc(hi_ready, 1)

            def squares(b, src, col, signal):
                nc.scalar.activation(tok(gate)[:, b, :], src, ACT.Square, accum_out=sm(SS + col + b)).then_inc(signal, 1)

            def norm_root(b, src, col, ss, sd):
                squares(b, src, col, ss[0])
                act.wait_ge(*ss)
                root(sm(SD + col + b), sm(SS + col + b), D, sd)

            def root(dst, src, n, signal):
                nc.scalar.activation(dst, src, ACT.Sqrt, scale=1.0 / n, bias=eps[:]).then_inc(signal, 1)

            def operand_hi(which, turns, signal, ready, gain):
                for c in range(KC):
                    if c % 2 == 0:
                        act.wait_ge(signal, turns + c // 2 + 1)
                    nc.scalar.activation(op_hi[which][:, c, :], psum[:, 4 + c // 2, (c % 2) * S:(c % 2 + 1) * S],
                                         ACT.Identity, scale=gain(c)).then_inc(ready, 1)

            act.wait_ge(masks_ready, 1)
            for b in range(TB):
                act.wait_ge(mem_half_in[b], 16)
                norm_root(b, tok(B[6])[:, b, :], 0, (norm_ss, b + 1), norm_sd)
            act.dma_start(x[:], x_in).then_inc(x_loaded, 16)
            act.dma_start(cos[:], cos_in).then_inc(rope_in, 16)
            act.dma_start(sin[:], sin_in).then_inc(rope_in, 16)
            act.wait_ge(par_in, 16)
            operand_hi(0, 0, turned, op_hi_done, lambda c: par[:, PA["mem"] + c:PA["mem"] + c + 1])
            act.wait_ge(hi_ready, 1)
            round_tile(1, 0)
            act.wait_ge(op_ready, 4)
            nc.scalar.activation(B[6][:], psum[:, 4:8, :].rearrange("p a n -> p (a n)"), ACT.Identity).then_inc(mem_copied, 1)
            act.wait_ge(mem_copied, 1)
            act.dma_start(mem_normed, B[6][:]).then_inc(mem_stored, 16)
            round_tile(2, 0)

            with act.Fori(0, DEPTH) as l:
                T = l * A_TILES
                step.base, step.n = l * ACT_STEPS, 0

                def round_after(t, i=None):
                    s, r = t % 4, l * (A_TILES // 4) + (t // 4 + 1)
                    act.wait_ge(tile_done, T + (t + 1) if i is None else T + i * 4 + (t + 1))
                    round_tile(s, r if i is None else r + i)

                def empty(t, dst, scale=1.0):
                    act.wait_ge(tile_done, T + t + 1)
                    src = psum[:, t % 4, :].rearrange("p (a n) -> p a n", a=2)
                    nc.scalar.activation(dst, src, ACT.Identity, scale=scale).then_inc(act_evac, 1)

                def empty_gate(t, func, branch, n):
                    act.wait_ge(tile_done, T + t + 1)
                    for c in range(2):
                        col = PA["b_gate"] + branch * KC + 2 * n + c
                        ins = nc.scalar.activation(feat(gate)[:, 2 * n + c, :], psum[:, t % 4, c * S:(c + 1) * S], func,
                                                   bias=par[:, col:col + 1])
                    ins.then_inc(act_evac, 1)

                def turns(norm):
                    return l * (4 * N_NORMS) + 4 * norm

                for b in range(TB):
                    act.wait_ge(x_ready, l * 4 + b + 1)
                    norm_root(b, x[:, b, :], 2, (norm_ss, l * 4 + (b + 3)), norm_sd)
                round_tile(3, l * (A_TILES // 4))
                act.wait_ge(par_d, l + 1)
                step(nc.scalar.activation(prep[:, 0:8], prep[:, 0:8], ACT.Exp))
                nc.scalar.activation(prep[:, 16:18], prep[:, 8:10], ACT.Exp).then_inc(par_a, 1)
                nc.scalar.activation(prep[:, 0:8], prep[:, 0:8], ACT.Ln, bias=1.0).then_inc(par_a, 1)

                for n in range(4):
                    empty(T_K + n, k_mem[:, 2 * n:2 * n + 2, :])
                    round_after(T_K + n)
                operand_hi(1, turns(MIX), turned, op_hi_done, lambda c: par[:, PA["mix_pre"] + c:PA["mix_pre"] + c + 1])
                act.wait_ge(t5_stored, 16)
                for n in range(4):
                    empty(T_V + n, v_mem[:, :, n * 256:(n + 1) * 256])
                    round_after(T_V + n)
                for n in range(4):
                    empty(T_XQ + n, q_mem[:, 2 * n:2 * n + 2, :], X_HD ** -0.5)
                    round_after(T_XQ + n)

                def empty_rope(i):
                    act.wait_ge(rope_turned, l * 8 + i + 1)
                    dst, scale = (q_t, A_HD ** -0.5) if i < 4 else (k_t, 1.0)
                    nc.scalar.activation(dst[:, 2 * (i % 4):2 * (i % 4) + 2, :], psum[:, 5, :].rearrange("p (a n) -> p a n", a=2),
                                         ACT.Identity, scale=scale).then_inc(rope_evac, 1)

                def x_exps(h):
                    act.wait_ge(x_max, l * X_HEADS + h + 1)
                    for b in range(TB):
                        ins = nc.scalar.activation(expd[:, b, :], psum[:, 4, b * 256:(b + 1) * 256], ACT.Exp,
                                                   bias=sm(NMAX + b), accum_out=sm(ZSUM + b))
                    ins.then_inc(x_exp, 1)

                def x_empty_turned(h):
                    act.wait_ge(x_turned, l * X_HEADS + h + 1)
                    nc.scalar.activation(probs_t[:], psum[:, 6, :], ACT.Identity).then_inc(x_pt, 1)

                def x_hi(h):
                    act.wait_ge(x_out, l * X_HEADS + h + 1)
                    nc.scalar.activation(op_hi[0][:, 2 * h:2 * h + 2, :], psum[:, 7, :].rearrange("p (a n) -> p a n", a=2),
                                         ACT.Identity).then_inc(op_hi_done, 1)

                for i in range(8):
                    if i:
                        round_after(T_QK + i - 1)
                        empty_rope(i - 1)
                    if i % 2 == 0:
                        if i:
                            x_hi(i // 2 - 1)
                        x_exps(i // 2)
                    else:
                        x_empty_turned(i // 2)
                round_after(T_QK + 7)
                empty(T_AV, v_a[:, :, 0:256])
                empty_rope(7)
                x_hi(3)
                for n in range(1, 4):
                    round_after(T_AV + n - 1)
                    empty(T_AV + n, v_a[:, :, n * 256:(n + 1) * 256])

                def empty_during_heads(t):
                    if t < T_ZY:
                        n = t - T_ZX
                        empty(t, zx[:, 2 * n:2 * n + 2, 4:260])
                    elif t < T_GM:
                        n = t - T_ZY
                        empty(t, gz[:, 2 * n:2 * n + 2, :])
                    elif t < T_PM:
                        empty_gate(t, ACT.Identity, 2, t - T_GM)

                act.wait_ge(mem_stored, 16)
                for h in range(A_HEADS):
                    t = T_ZX + 2 * h
                    act.wait_ge(d_max, l * A_HEADS + h + 1)
                    for m in range(2):
                        for b in range(TB):
                            n = (b + 1) * P
                            ins = nc.scalar.activation(expd[:, 2 * m + b, 0:n], psum[:, 4 + m, b * 256:b * 256 + n], ACT.Exp,
                                                       bias=sm(NMAX + 2 * m + b), accum_out=sm(ZSUM + 2 * m + b))
                    ins.then_inc(d_exp, 1)
                    round_after(t - 1)
                    if t == T_PM:
                        act.wait_ge(act_evac, l * N_ACT_EVAC + ACT_EVAC[T_PM - 1])
                        nc.scalar.activation(gate[:], gate[:], ACT.Sigmoid).then_inc(mem_gate, 1)
                    empty_during_heads(t)
                    act.wait_ge(d_turned, l * A_HEADS + h + 1)
                    nc.scalar.activation(probs_t[:, 0:384], psum[:, 6, 0:384], ACT.Identity).then_inc(d_pt, 1)
                    round_after(t)
                    empty_during_heads(t + 1)
                    if h == 6:
                        act.wait_ge(conv_done, l * 4 + 4)
                        act.dma_start(B[0][:, 0:2048], rg_w[l]).then_inc(rgw_in, 16)
                    act.wait_ge(d_out, l * A_HEADS + h + 1)
                    nc.scalar.activation(o_a[:, :, h * P:(h + 1) * P], psum[:, 7, 0:256].rearrange("p (b n) -> p b n", b=TB),
                                         ACT.Identity).then_inc(d_kept, 1)

                act.wait_ge(sub_ss, l + 1)
                root(prep[:, 48:64], prep[:, 32:48], P, norm_sd)
                round_after(T_GA - 1)
                act.wait_ge(dve_evac, l * N_DVE_EVAC + DVE_EVAC[T_PM + 3])

                def rg_sigmoids(c):
                    act.wait_ge(rg_done, l * KC + c + 1)
                    nc.scalar.activation(r_g[:, c, :], psum[:, 4 + c % 4, 0:S], ACT.Sigmoid,
                                         bias=par[:, PA["rg_ba"] + c:PA["rg_ba"] + c + 1])
                    nc.scalar.activation(i_g[:, c, :], psum[:, 4 + c % 4, S:2 * S], ACT.Sigmoid,
                                         bias=par[:, PA["rg_bi"] + c:PA["rg_bi"] + c + 1]).then_inc(rg_evac, 1)

                for n in range(2):
                    empty_gate(T_GA + n, ACT.Sigmoid, 0, n)
                    for c in range(4):
                        rg_sigmoids(4 * n + c)
                    round_after(T_GA + n)
                empty_gate(T_GA + 2, ACT.Sigmoid, 0, 2)
                operand_hi(0, turns(SUB), turned, op_hi_done, lambda c: sm(GSUB))
                round_after(T_GA + 2)
                empty_gate(T_GA + 3, ACT.Sigmoid, 0, 3)
                for c in range(KC):
                    nc.scalar.activation(t_g[:, c, :], r_g[:, c, :], ACT.Tanh, scale=sm(SP_POS + c))
                    ins = nc.scalar.activation(r_g[:, c, :], r_g[:, c, :], ACT.Exp, scale=sm(SP_NEG + c))
                ins.then_inc(lru_ta, 1)
                round_after(T_GA + 3)
                nc.scalar.activation(B[5][:], B[5][:], ACT.Gelu_apprx_tanh).then_inc(gelu_done, 1)
                act.wait_ge(lru_v, l + 1)
                nc.scalar.activation(B[4][:], B[4][:], ACT.Sqrt).then_inc(lru_s, 1)
                round_after(T_PA)
                act.wait_ge(lru_u, l + 1)
                act.dma_start(B[4][:], post_gain[l]).then_inc(gain_in, 16)
                round_after(T_PA + 1)
                round_after(T_PA + 2)
                act.wait_ge(dve_evac, l * N_DVE_EVAC + DVE_EVAC[T_PA + 3])
                act.wait_ge(lru_y, l + 1)
                nc.scalar.activation(op_hi[0][:].rearrange("p c t -> p (c t)"), B[6][:], ACT.Identity).then_inc(op_hi_done, 1)
                round_after(T_PA + 3)
                for n in range(4):
                    empty_gate(T_GL + n, ACT.Sigmoid, 1, n)
                    round_after(T_GL + n)
                act.preload_act_table_set("sqrt_and_others")
                for n in range(4):
                    act.wait_ge(merged_part, l * 4 + n + 1)
                    nc.scalar.activation(op_hi[1][:, 2 * n:2 * n + 2, :], feat(merged)[:, 2 * n:2 * n + 2, :],
                                         ACT.Identity).then_inc(op_hi_done, 1)
                    round_after(T_PL + n)
                for n in range(3):
                    act.wait_ge(tile_done, T + (T_OUT + n + 1))
                    for b in range(TB):
                        ins = nc.scalar.activation(B[5][:, (2 * n + b) * 256:(2 * n + b + 1) * 256], psum[:, n, b * 256:(b + 1) * 256],
                                                   ACT.Square, accum_out=sm(SS + 8 + 4 * b + n))
                    ins.then_inc(out_ss, 1)
                    round_after(T_OUT + n)
                for b in range(TB):
                    if b == 0:
                        act.wait_ge(half_done, l * 2 + 1)
                    else:
                        act.wait_ge(tile_done, T + T_UP)
                    nc.scalar.activation(B[5][:, (6 + b) * 256:(7 + b) * 256], psum[:, OUT_BANKS[b], 0:256],
                                         ACT.Square, accum_out=sm(SS + 11 + 4 * b)).then_inc(out_ss, 1)
                    act.wait_ge(post_var, l * 2 + b + 1)
                    root(sm(SD + 4 + b), sm(VAR + b), D, post_sd)
                for b in range(TB):
                    act.wait_ge(x_ready, l * 4 + (b + 3))
                    norm_root(b, x[:, b, :], 6, (norm_ss, l * 4 + (b + 5)), norm_sd)
                operand_hi(0, turns(MLP), turned, op_hi_done, lambda c: par[:, PA["mlp_pre"] + c:PA["mlp_pre"] + c + 1])
                act.wait_ge(op_ready, l * (4 * N_OPS) + 4 * (MLP_OP + 1))
                act.dma_start(par[:], params[l + 1]).then_inc(par_in, 16)
                act.dma_start(B[6][:], mem_normed).then_inc(mem_loaded, 16)
                round_after(T_OUT + 3)

                def relu(j, t, slot, first=False):
                    act.wait_ge(tile_done, T + (t + 1))
                    if not first:
                        act.wait_ge(squared_done, l * A_UP + (j - 1))
                    nc.scalar.activation(relu_u[:, slot, :], psum[:, slot, :], ACT.Relu).then_inc(relu_done, 1)

                relu(0, T_UP, 0, True)
                round_after(T_UP)
                relu(1, T_UP + 1, 1, True)
                round_after(T_UP + 1)
                with act.Fori(0, A_UP // 2 - 1) as i:
                    round_after(T_UP + 2, i)
                    relu(i * 2 + 2, i * 4 + (T_UP + 3), 0)
                    round_after(T_UP + 3, i)
                    round_after(T_UP + 4, i)
                    relu(i * 2 + 3, i * 4 + (T_UP + 5), 1)
                    round_after(T_UP + 5, i)
                act.wait_ge(par_in, l * 16 + 32)
                act.wait_ge(mem_loaded, l * 16 + 16)
                for c in range(KC):
                    nc.scalar.activation(op_hi[0][:, c, :], feat(B[6])[:, c, :], ACT.Identity,
                                         scale=par[:, PA["mem"] + c:PA["mem"] + c + 1]).then_inc(op_hi_done, 1)
                round_after(A_TILES - 2)
                for b in range(TB):
                    if b == 0:
                        act.wait_ge(half_done, l * 2 + 2)
                    else:
                        act.wait_ge(tile_done, T + A_TILES)
                    squares(b, psum[:, 4 + 2 * b:6 + 2 * b, :].rearrange("p a n -> p (a n)"), 8, post_ss)
                    act.wait_ge(post_ss, l * 2 + b + 1)
                    root(sm(SD + 8 + b), sm(SS + 8 + b), D, post_sd)
                assert step.n == ACT_STEPS, step.n

            T0 = DEPTH * A_TILES
            act.wait_ge(par_in, 16 * (DEPTH + 1))

            def round_after_b(t):
                if T0 + t + 4 < N_TILES:
                    act.wait_ge(tile_done, T0 + t + 1)
                    round_tile(t % 4, (T0 + t) // 4 + 1)

            for b in range(TB):
                act.wait_ge(x_ready, 4 * DEPTH + b + 1)
                norm_root(b, x[:, b, :], 0, (b_ss, b + 1), b_sd)
            round_after_b(-1)
            operand_hi(0, 0, b_turned, b_hi, lambda c: par[:, PB["mix"] + c:PB["mix"] + c + 1])
            act.preload_act_table_set("natural_log_exp_and_others")
            act.wait_ge(op_ready, DEPTH * 4 * N_OPS + 4)
            act.wait_ge(t5_skewed_in, 8 * 16)
            act.dma_start(B[6][:, 0:7 * P], masks_in).then_inc(b_masks_in, 16)
            for h in range(8):
                for u in range(TB):
                    src = bass.AP(tensor=t5_skewed.tensor, offset=t5_skewed.offset + h * P * (SKEW + 1) + 255 - u * P,
                                  ap=[[SKEW, P], [1, (u + 1) * P]])
                    act.dma_start(bias_b[h][:, u, 0:(u + 1) * P], src).then_inc(bias_in, 16)
            for t in range(N_FEAT):
                act.wait_ge(tile_done, T0 + t + 1)
                dst = B[t // 4][:, (t % 4) * 512:(t % 4 + 1) * 512]
                is_query = 2 * t in (SB_Q, MB_Q, FX_Q, DS_Q)
                nc.scalar.activation(dst, psum[:, t % 4, :], ACT.Identity, scale=B_HD ** -0.5 if is_query else 1.0).then_inc(b_evac_a, 1)
                round_after_b(t)
            for n in range(N_TOK):
                act.wait_ge(tile_done, T0 + N_FEAT + n + 1)
                nc.scalar.activation(v_b[:, :, n * 256:(n + 1) * 256], psum[:, (N_FEAT + n) % 4, :].rearrange("p (b n) -> p b n", b=TB),
                                     ACT.Identity).then_inc(b_evac_a, 1)
                if n < N_TOK - 1:
                    round_after_b(N_FEAT + n)

            def empty_gate_b(b, n):
                act.wait_ge(tile_done, T0 + T2_GATE + 5 * b + n + 1)
                if b:
                    act.wait_ge(b_mixed, b)
                nc.scalar.activation(gate[:, n * 512:(n + 1) * 512], psum[:, gate_bank(b, n), :], ACT.Identity).then_inc(b_evac_a, 1)

            def open_gate_b(b):
                act.wait_ge(b_evac_a, N_FEAT + N_TOK + 4 * (b + 1))
                for n in range(4):
                    cols = slice(n * 512, (n + 1) * 512)
                    nc.scalar.activation(gate[:, cols], gate[:, cols], ACT.Sigmoid).then_inc(gate_open, 1)

            def index_relu(h):
                act.wait_ge(ix_scores, h + 1)
                if h >= 2:
                    act.wait_ge(ix_added, h - 1)
                nc.scalar.activation(expd[:, 2 * (h % 2), 0:P], psum[:, 4 + h % 4, 0:P], ACT.Relu)
                nc.scalar.activation(expd[:, 2 * (h % 2) + 1, :], psum[:, 4 + h % 4, 256:512], ACT.Relu).then_inc(ix_relu, 1)

            round_after_b(N_FEAT + N_TOK - 1)
            empty_gate_b(0, 0)
            for h in range(4):
                index_relu(h)
            round_after_b(T2_GATE)
            empty_gate_b(0, 1)
            for h in range(4, IDX_HEADS):
                index_relu(h)
            round_after_b(T2_GATE + 1)
            act.wait_ge(f_in, 1)
            nc.scalar.activation(prep[:, 8:16], prep[:, 8:16], ACT.Exp).then_inc(f_ln, 1)
            act.wait_ge(f_ln, 1)
            nc.scalar.activation(prep[:, 8:16], prep[:, 8:16], ACT.Ln, bias=1.0).then_inc(f_ln, 1)

            def sb_softplus_tail(h):
                act.wait_ge(sb_z, h + 1)
                a = expd[:, 2 * (h % 2):2 * (h % 2) + 2, :].rearrange("p a n -> p (a n)")[:, 0:384]
                if h == 0:
                    act.wait_ge(ix_added, IDX_HEADS)
                for k, (src, func, bias) in enumerate(((psum[:, 4 + h % 2, 0:384], ACT.Abs, 0.0), (a, ACT.Exp, 0.0), (a, ACT.Ln, 1.0))):
                    nc.scalar.activation(a, src, func, bias=bias, scale=-1.0 if k == 1 else 1.0).then_inc(sb_ln, 1)
                    if k < 2:
                        act.wait_ge(sb_ln, 3 * h + k + 1)

            def sb_weights(h):
                act.wait_ge(sb_summed, h + 1)
                if h:
                    act.wait_ge(b_out, h)
                nc.scalar.activation(probs_t[:, 0:384], psum[:, 4 + h % 2, 0:384], ACT.Exp).then_inc(sb_w, 1)

            def branch_hi(b, k):
                act.wait_ge(b_out, 4 * b + 2 * k + 2)
                if b:
                    act.wait_ge(tile_done, T0 + T2_GATE + 5 * b)
                nc.scalar.activation(op_hi[1][:, k, :], psum[:, 7, k * S:(k + 1) * S], ACT.Identity).then_inc(b_hi, 1)

            sb_softplus_tail(0)
            for h in range(4):
                if h % 2 == 0:
                    empty_gate_b(0, 2 + h // 2)
                sb_weights(h)
                if h < 3:
                    sb_softplus_tail(h + 1)
                if h % 2:
                    branch_hi(0, h // 2)
                if h % 2 == 0:
                    round_after_b(T2_GATE + 2 + h // 2)
            act.wait_ge(c_sums, 2)
            for a in range(2):
                ins = nc.scalar.activation(minus_c_row[:, 2 * a:2 * a + 2, :].rearrange("p h n -> p (h n)"), psum[:, 4 + 2 * a, :],
                                           ACT.Identity, scale=-1.0)
            ins.then_inc(c_kept, 1)
            act.wait_ge(c_sums, 3)
            nc.scalar.activation(c_col, psum[:, 5, 0:8], ACT.Identity).then_inc(c_kept, 1)

            def s_exps(b, h):
                g = 4 * (b - 1) + h
                act.wait_ge(s_max, g + 1)
                e = 2 * (h % 2)
                for u in range(TB):
                    ins = nc.scalar.activation(expd[:, e + u, 0:(u + 1) * P], expd[:, e + u, 0:(u + 1) * P], ACT.Exp,
                                               bias=sm(NMAX + e + u), accum_out=sm(ZSUM + e + u))
                ins.then_inc(s_exp, 1)

            def s_empty_turned(b, h):
                g = 4 * (b - 1) + h
                act.wait_ge(s_turned, g + 1)
                if h:
                    act.wait_ge(b_out, 4 * b + h)
                nc.scalar.activation(probs_t[:, 0:384], psum[:, 6, 0:384], ACT.Identity).then_inc(s_pt, 1)

            for b in range(1, 4):
                open_gate_b(b - 1)
                if b > 1:
                    round_after_b(T2_GATE + 5 * b - 2)
                act.preload_act_table_set("exp_and_others")
                s_exps(b, 0)
                for h in range(4):
                    empty_gate_b(b, h)
                    s_empty_turned(b, h)
                    if h == 0:
                        round_after_b(T2_GATE + 5 * b - 1)
                    if h < 3:
                        s_exps(b, h + 1)
                    if h % 2:
                        branch_hi(b, h // 2)
                    if h < 3:
                        round_after_b(T2_GATE + 5 * b + h)
            open_gate_b(3)
            act.preload_act_table_set("sqrt_and_others")

            for n in range(4):
                act.wait_ge(out_part, n + 1)
                nc.scalar.activation(op_hi[0][:, 2 * n:2 * n + 2, :], feat(merged)[:, 2 * n:2 * n + 2, :], ACT.Identity).then_inc(b_hi, 1)
            round_after_b(T2_GATE + 18)
            round_after_b(T2_GATE + 19)
            for n in range(3):
                act.wait_ge(x_part, n + 1)
                for b in range(TB):
                    ins = nc.scalar.activation(gate[:, (2 * n + b) * 256:(2 * n + b + 1) * 256], x[:, b, n * 256:(n + 1) * 256],
                                               ACT.Square, accum_out=sm(SS + 8 + 4 * b + n))
                ins.then_inc(xb_ss, 1)
                round_after_b(T2_OUT + n)
            act.dma_start(merged[:, 0:D], final_gain).then_inc(final_in, 16)
            for b in range(TB):
                act.wait_ge(x_part, 4 + b)
                nc.scalar.activation(gate[:, (6 + b) * 256:(7 + b) * 256], x[:, b, 768:1024],
                                     ACT.Square, accum_out=sm(SS + 11 + 4 * b)).then_inc(xb_ss, 1)
                act.wait_ge(xb_sum, b + 1)
                root(sm(SD + 2 + b), sm(VAR + b), D, b_sd)
            operand_hi(0, 4, b_turned, b_hi, lambda c: par[:, PB["ffn"] + c:PB["ffn"] + c + 1])
            round_after_b(T2_OUT + 3)
            act.wait_ge(pads_zero, 1)
            for kind, j in FFN_ORDER:
                t = FFN_AT[kind, j]
                if kind == "down":
                    round_after_b(t)
                    continue
                for n in range(2):
                    act.wait_ge(tile_done, T0 + t + n + 1)
                    if j >= 2 and n == 0:
                        act.wait_ge(f_conv, j - 1)
                    nc.scalar.activation(padded[:, j % 2, 2 * n:2 * n + 2, 2:2 + S],
                                         psum[:, 2 * (j % 2) + n, :].rearrange("p (a t) -> p a t", a=2), ACT.Identity).then_inc(f_evac, 1)
                round_after_b(t)
                round_after_b(t + 1)
                act.wait_ge(f_conv, j + 1)
                if j >= 2:
                    act.wait_ge(f_gated, j - 1)
                nc.scalar.activation(gelu_g[:, j % 2, :], conved[:, j % 2, 0:2, :].rearrange("p a t -> p (a t)"), ACT.Gelu).then_inc(f_gelu, 1)
            act.preload_act_table_set("sqrt_and_others")
            for b in range(TB):
                act.wait_ge(x_b, b + 1)
                norm_root(b, x[:, b, :], 4, (b_ss, b + 3), b_sd)
            for b in range(TB):
                for n in range(2):
                    act.wait_ge(y_done, 2 * b + n + 1)
                    cols = slice(n * 512, (n + 1) * 512)
                    act.dma_start(out[:, b, cols], y_tok[:, b, cols]).then_inc(out_done, 16)

        @block.vector
        def _(dve):
            step = Steps(dve, dve_step, DVE_STEPS)

            def rest(t, s):
                dve.wait_ge(hi_ready, t + 1)
                nc.vector.tensor_tensor(w_lo[:, s % LO, :], w_raw[:, s, :], w_hi[:, s, :].bitcast(F32), ALU.subtract)\
                    .then_inc(lo_ready[0], 2)

            nc.vector.memset(eps[:], EPS).then_inc(masks_ready, 1)
            nc.vector.memset(rowmask[:], 0.0).then_inc(masks_ready, 1)
            nc.vector.memset(colmask[:], NEG).then_inc(masks_ready, 1)
            dve.wait_ge(masks_ready, 3)
            nc.vector.memset(rowmask[:, 0:64], 1.0).then_inc(masks_ready, 1)

            def diagonal(b, col, sd, own, signal):
                dve.wait_ge(*sd)
                own(nc.vector.reciprocal(sm(RS + col + b), sm(SD + col + b)))
                nc.vector.tensor_scalar(diag[:, b, :], ident[:], sm(RS + col + b), None, ALU.mult).then_inc(signal, 1)

            def operand_lo(which, hi_part, ready, gain):
                for c in range(KC):
                    if c % 2 == 0:
                        hi_part(2)
                    ins = nc.vector.scalar_tensor_tensor(
                        op_lo[which][:, c, :], psum[:, 4 + c // 2, (c % 2) * S:(c % 2 + 1) * S], gain(c),
                        op_hi[which][:, c, :].bitcast(F32), ALU.mult, ALU.subtract)
                    if c % 2:
                        ins.then_inc(ready, 1)

            dve.wait_ge(ident_loaded, 16)
            for b in range(TB):
                def own(ins):
                    ins.then_inc(rs_ready, 1)
                    dve.wait_ge(rs_ready, b + 1)

                diagonal(b, 0, (norm_sd, b + 1), own, norm_x)
            dve.wait_ge(raw_loaded[0], 16)
            nc.vector.tensor_copy(w_hi[:, 0, :], w_raw[:, 0, :]).then_inc(hi_ready, 1)
            rest(0, 0)
            his = [0]

            def first_hi_part(n):
                his[0] += n
                dve.wait_ge(op_hi_done, his[0])

            operand_lo(0, first_hi_part, op_ready, lambda c: par[:, PA["mem"] + c:PA["mem"] + c + 1])
            dve.wait_ge(t5_rows_ready, 1)
            nc.vector.tensor_copy(B[1][0:8, 1024:1536], psum[0:8, 3, :]).then_inc(t5_evac, 1)
            dve.wait_ge(x_loaded, 16)
            nc.vector.sem_inc(x_ready, TB)

            with dve.Fori(0, DEPTH) as l:
                T = l * A_TILES
                step.base, step.n = l * DVE_STEPS, 0
                his[0] = 0

                def hi_part(n=1):
                    his[0] += n
                    dve.wait_ge(op_hi_done, l * HI_PARTS + (KC + his[0]))

                def after(t, evac=None):
                    dve.wait_ge(tile_done, T + t + 1)
                    if evac:
                        evac()
                    if t % 2 == 0:
                        rest(T + (t + 2), (t + 2) % 4)

                after(T_K)
                for b in range(TB):
                    dve.wait_ge(norm_sd, l * NORM_COUNT + (NORM_AT[MIX] + b + 1))
                    step(nc.vector.reciprocal(sm(RS + 2 + b), sm(SD + 2 + b)))
                    nc.vector.tensor_scalar(tok(gate)[:, b, :], x[:, b, :], sm(RS + 2 + b), None, ALU.mult).then_inc(norm_x, 1)

                lam = par[:, PA["rg_lambda"]:PA["rg_lambda"] + 8]
                nc.vector.scalar_tensor_tensor(prep[:, 0:8], lam, -1.0, lam, ALU.mult, ALU.min)
                nc.vector.tensor_scalar(prep[:, 24:32], lam, 0.0, -1.0, ALU.min, ALU.mult)
                step(nc.vector.tensor_tensor(prep[:, 32:160], par[:, PA["lambda_q"]:PA["lambda_q"] + 128],
                                             par[:, PA["lambda_k"]:PA["lambda_k"] + 128], ALU.mult))
                nc.vector.tensor_reduce(prep[:, 8:10], prep[:, 32:160].rearrange("p (a n) -> p a n", a=2), AX.X,
                                        ALU.add).then_inc(par_d, 1)
                nc.vector.tensor_tensor(sm(GSUB), par[:, PA["subln"]:PA["subln"] + 1],
                                        par[:, PA["one_minus_init"]:PA["one_minus_init"] + 1], ALU.mult)
                dve.wait_ge(par_a, l * 2 + 2)
                step(nc.vector.tensor_tensor(sm(NLAM), prep[:, 17:18], prep[:, 16:17], ALU.subtract))
                nc.vector.tensor_tensor(sm(NLAM), sm(NLAM), par[:, PA["init"]:PA["init"] + 1], ALU.subtract)
                step(nc.vector.tensor_tensor(prep[:, 0:8], prep[:, 0:8], prep[:, 24:32], ALU.add))
                nc.vector.tensor_scalar(sm(SP_POS, 8), prep[:, 0:8], 8.0, None, ALU.mult)
                step(nc.vector.tensor_scalar(sm(SP_NEG, 8), prep[:, 0:8], -8.0, None, ALU.mult))

                for t in range(T_K + 1, T_V):
                    after(t)
                operand_lo(1, hi_part, op_ready, lambda c: par[:, PA["mix_pre"] + c:PA["mix_pre"] + c + 1])
                for t in range(T_V, T_QK):
                    after(t)
                dve.wait_ge(rope_in, 2 * 16)

                def rope(i):
                    def evac():
                        bank = (T_QK + i) % 4
                        if i >= 2:
                            dve.wait_ge(rope_turned, l * 8 + i - 1)
                        if i:
                            dve.wait_ge(rope_ready, l * 8 + i)
                        for b in range(TB):
                            z = psum[:, bank, b * 256:(b + 1) * 256]
                            zg = z.rearrange("p (g h n) -> p g h n", g=4, h=2)
                            za = rope_a[:, b * 256:(b + 1) * 256]
                            zb = rope_b[:, b * 256:(b + 1) * 256].rearrange("p (g h n) -> p g h n", g=4, h=2)
                            nc.vector.tensor_tensor(za.rearrange("p (g n) -> p g n", n=32), z.rearrange("p (g n) -> p g n", n=32),
                                                    cos[:, b:b + 1, :].to_broadcast([P, 8, 32]), ALU.mult)
                            s4 = sin[:, b:b + 1, :].to_broadcast([P, 4, 32])
                            nc.vector.scalar_tensor_tensor(zb[:, :, 0, :], zg[:, :, 1, :], -1.0, s4, ALU.mult, ALU.mult)
                            ins = nc.vector.tensor_tensor(zb[:, :, 1, :], zg[:, :, 0, :], s4, ALU.mult)
                        ins.then_inc(dve_evac, 1)
                        dve.wait_ge(dve_evac, l * N_DVE_EVAC + i + 1)
                        nc.vector.tensor_tensor(rot[:, i % 2, :], rope_a, rope_b, ALU.add).then_inc(rope_ready, 1)
                    return evac

                def x_softmax(h):
                    dve.wait_ge(x_scores, l * X_HEADS + h + 1)
                    nc.vector.tensor_reduce(sm(NMAX, 2), psum[:, 4, :].rearrange("p (b n) -> p b n", b=TB), AX.X, ALU.max,
                                            negate=True).then_inc(x_max, 1)
                    dve.wait_ge(x_exp, l * X_HEADS + h + 1)
                    step(nc.vector.reciprocal(sm(RZ, 2), sm(ZSUM, 2)))
                    for b in range(TB):
                        ins = nc.vector.tensor_scalar(expd[:, b, :], expd[:, b, :], sm(RZ + b), None, ALU.mult)
                    ins.then_inc(x_probs, 1)

                def x_lo(h):
                    hi_part()
                    nc.vector.tensor_tensor(op_lo[0][:, 2 * h:2 * h + 2, :], psum[:, 7, :].rearrange("p (a n) -> p a n", a=2),
                                            op_hi[0][:, 2 * h:2 * h + 2, :].bitcast(F32), ALU.subtract).then_inc(op_ready, 1)

                for i in range(8):
                    after(T_QK + i, rope(i))
                    if i % 2 == 0:
                        x_softmax(i // 2)
                        if i:
                            x_lo(i // 2 - 1)
                after(T_AV)
                x_lo(3)
                nc.vector.memset(zx[:, :, 0:4], 0.0).then_inc(zx_padded, 1)
                for t in range(T_AV + 1, T_ZX):
                    after(t)

                def add_branch(t0, n, first, last=False):
                    def evac():
                        cols = slice(n * 512, (n + 1) * 512)
                        if first:
                            nc.vector.tensor_tensor(merged[:, cols], psum[:, (t0 + n) % 4, :], gate[:, cols], ALU.mult).then_inc(dve_evac, 1)
                            return
                        prod = expd[:, 0:2, :].rearrange("p a n -> p (a n)")
                        if last and n:
                            dve.wait_ge(merged_part, l * 4 + n)
                        nc.vector.tensor_tensor(prod, psum[:, (t0 + n) % 4, :], gate[:, cols], ALU.mult).then_inc(dve_evac, 1)
                        dve.wait_ge(dve_evac, l * N_DVE_EVAC + DVE_EVAC[t0 + n])
                        ins = nc.vector.tensor_tensor(merged[:, cols], merged[:, cols], prod, ALU.add)
                        if last:
                            ins.then_inc(merged_part, 1)
                        else:
                            step(ins)
                    return evac

                def conv(c0):
                    for k in range(4):
                        for c in (c0, c0 + 1):
                            w = par[:, PA["conv_w"] + k * KC + c:PA["conv_w"] + k * KC + c + 1]
                            src = zx[:, c, 1 + k:1 + k + S]
                            if k == 0:
                                ins = nc.vector.tensor_scalar(xc[:, c, :], src, w, par[:, PA["conv_b"] + c:PA["conv_b"] + c + 1],
                                                              ALU.mult, ALU.add)
                            else:
                                ins = nc.vector.scalar_tensor_tensor(xc[:, c, :], src, w, xc[:, c, :], ALU.mult, ALU.add)
                        if k < 3:
                            step(ins)
                    ins.then_inc(conv_done, 1)

                for h in range(A_HEADS):
                    t = T_ZX + 2 * h
                    dve.wait_ge(d_scores, l * A_HEADS + h + 1)
                    for b in range(TB):
                        n = (b + 1) * P
                        ins = nc.vector.tensor_reduce(small[:, NMAX + b:NMAX + b + 3:2], psum[:, 4:6, b * 256:b * 256 + n], AX.X,
                                                      ALU.max, negate=True)
                    ins.then_inc(d_max, 1)
                    dve.wait_ge(d_exp, l * A_HEADS + h + 1)
                    step(nc.vector.reciprocal(sm(RZ, 4), sm(ZSUM, 4)))
                    nc.vector.tensor_scalar(sm(R2, 2), sm(RZ + 2, 2), sm(NLAM), None, ALU.mult)
                    for b in range(TB):
                        ins = nc.vector.tensor_scalar(expd[:, b, 0:(b + 1) * P], expd[:, b, 0:(b + 1) * P], sm(RZ + b), None, ALU.mult)
                    step(ins)
                    for b in range(TB):
                        n = (b + 1) * P
                        ins = nc.vector.scalar_tensor_tensor(expd[:, b, 0:n], expd[:, 2 + b, 0:n], sm(R2 + b), expd[:, b, 0:n],
                                                             ALU.mult, ALU.add)
                    ins.then_inc(d_probs, 1)
                    for u in (t, t + 1):
                        if u >= T_PM:
                            if u == T_PM:
                                dve.wait_ge(mem_gate, l + 1)
                            after(u, add_branch(T_PM, u - T_PM, True))
                        else:
                            after(u)
                        if u == t and 2 <= h < 6:
                            dve.wait_ge(act_evac, l * N_ACT_EVAC + ACT_EVAC[T_ZX + h - 2])
                            if h == 2:
                                dve.wait_ge(zx_padded, l + 1)
                            conv(2 * (h - 2))

                dve.wait_ge(d_kept, l * A_HEADS + A_HEADS)
                step(nc.vector.tensor_tensor(B[4][:], B[6][:], B[6][:], ALU.mult))
                ins = nc.vector.tensor_reduce(prep[:, 32:48], B[4][:].rearrange("p (a n) -> p a n", n=P), AX.X, ALU.add)
                ins.then_inc(sub_ss, 1)
                dve.wait_ge(norm_sd, l * NORM_COUNT + (NORM_AT[SUB] + 1))
                step(nc.vector.reciprocal(prep[:, 48:64], prep[:, 48:64]))
                heads = B[6][:].rearrange("p (a n) -> p a n", n=P)
                nc.vector.tensor_tensor(heads, heads, prep[:, 48:64].unsqueeze(2).to_broadcast([P, 16, P]), ALU.mult).then_inc(norm_x, 1)
                after(T_GA)
                after(T_GA + 1)
                after(T_GA + 2)
                operand_lo(0, hi_part, op_ready, lambda c: sm(GSUB))
                after(T_GA + 3)
                after(T_PA, add_branch(T_PA, 0, False))

                dve.wait_ge(lru_ta, l + 1)
                step(nc.vector.tensor_tensor(B[6][:], B[2][:], B[2][:], ALU.mult))
                nc.vector.scalar_tensor_tensor(B[4][:], B[6][:], 1.0, B[4][:], ALU.add, ALU.mult).then_inc(lru_v, 1)
                after(T_PA + 1, add_branch(T_PA, 1, False))
                step(nc.vector.tensor_tensor(B[3][:], B[3][:], B[1][:], ALU.mult))
                dve.wait_ge(lru_s, l + 1)
                nc.vector.tensor_tensor(B[3][:], B[3][:], B[4][:], ALU.mult).then_inc(lru_u, 1)
                after(T_PA + 2, add_branch(T_PA, 2, False))
                dve.wait_ge(lru_u, l + 1)
                for c in range(KC):
                    ins = nc.vector.tensor_tensor_scan(lru[:, c, :], r_g[:, c, :], i_g[:, c, :], 0.0, ALU.mult, ALU.add)
                step(ins)
                dve.wait_ge(gelu_done, l + 1)
                nc.vector.tensor_tensor(B[6][:], B[6][:], B[5][:], ALU.mult).then_inc(lru_y, 1)
                after(T_PA + 3, add_branch(T_PA, 3, False))
                after(T_GL)
                hi_part()
                for c in range(0, KC, 2):
                    nc.vector.tensor_tensor(op_lo[0][:, c:c + 2, :], feat(B[6])[:, c:c + 2, :], op_hi[0][:, c:c + 2, :].bitcast(F32),
                                            ALU.subtract).then_inc(op_ready, 1)
                for t in range(T_GL + 1, T_PL):
                    after(t)
                for n in range(4):
                    if n < 3:
                        after(T_PL + n, add_branch(T_PL, n, False, True))
                    else:
                        dve.wait_ge(tile_done, T + (T_PL + n + 1))
                        add_branch(T_PL, n, False, True)()
                    hi_part()
                    nc.vector.tensor_tensor(op_lo[1][:, 2 * n:2 * n + 2, :], feat(merged)[:, 2 * n:2 * n + 2, :],
                                            op_hi[1][:, 2 * n:2 * n + 2, :].bitcast(F32), ALU.subtract).then_inc(op_ready, 1)
                after(T_PL + 3)

                def gained(n):
                    def evac():
                        cols = slice(n * 256, (n + 1) * 256)
                        dve.wait_ge(out_ss, l * 5 + n + 1)
                        if n == 0:
                            dve.wait_ge(gain_in, l * 16 + 16)
                        nc.vector.tensor_tensor(y_tok[:, :, cols], psum[:, n, :].rearrange("p (b n) -> p b n", b=TB),
                                                gains[:, 0:1, cols].to_broadcast([P, TB, 256]), ALU.mult).then_inc(dve_evac, 1)
                    return evac

                def add_normed(k, b):
                    col = 4 + 4 * k + b
                    dve.wait_ge(post_sd, l * 4 + (2 * k + b + 1))
                    step(nc.vector.reciprocal(sm(RS + col), sm(SD + col)))
                    dve.wait_ge(post_gained, l * 4 + (2 * k + b + 1))
                    nc.vector.scalar_tensor_tensor(x[:, b, :], y_tok[:, b, :], sm(RS + col), x[:, b, :],
                                                   ALU.mult, ALU.add).then_inc(x_ready, 1)

                for n in range(3):
                    after(T_OUT + n, gained(n))
                dve.wait_ge(dve_evac, l * N_DVE_EVAC + N_DVE_EVAC)
                for b in range(TB):
                    dve.wait_ge(out_ss, l * 5 + (4 + b))
                    nc.vector.tensor_reduce(sm(VAR + b), sm(SS + 8 + 4 * b, 4), AX.X, ALU.add).then_inc(post_var, 1)
                    nc.vector.tensor_tensor(y_tok[:, b, 768:1024], psum[:, OUT_BANKS[b], 0:256], gains[:, 0, 768:1024],
                                            ALU.mult).then_inc(post_gained, 1)
                    add_normed(0, b)
                for b in range(TB):
                    diagonal(b, 6, (norm_sd, l * NORM_COUNT + (NORM_AT[MLP] + b + 1)), step, norm_x)
                after(T_OUT + 3)
                operand_lo(0, hi_part, op_ready, lambda c: par[:, PA["mlp_pre"] + c:PA["mlp_pre"] + c + 1])

                def after_mlp(t, i=None):
                    at = T if i is None else T + i * 4
                    dve.wait_ge(tile_done, at + (t + 1))
                    if t % 2 == 0:
                        rest(at + (t + 2), (t + 2) % 4)

                def hidden(j, slot):
                    dve.wait_ge(relu_done, l * A_UP + (j + 1))
                    nc.vector.tensor_tensor(squared[:, slot, :], relu_u[:, slot, :], relu_u[:, slot, :], ALU.mult).then_inc(squared_done, 1)
                    dve.wait_ge(squared_done, l * A_UP + (j + 1))
                    hi = op_hi[1][:, 2 * slot:2 * slot + 2, :].rearrange("p a t -> p (a t)")
                    lo = op_lo[1][:, 2 * slot:2 * slot + 2, :].rearrange("p a t -> p (a t)")
                    nc.vector.tensor_copy(hi, squared[:, slot, :]).then_inc(ffn_hi, 1)
                    dve.wait_ge(ffn_hi, l * A_UP + (j + 1))
                    nc.vector.tensor_tensor(lo, squared[:, slot, :], hi.bitcast(F32), ALU.subtract).then_inc(ffn_ready, 1)

                after_mlp(T_UP)
                hidden(0, 0)
                after_mlp(T_UP + 1)
                hidden(1, 1)
                with dve.Fori(0, A_UP // 2 - 1) as i:
                    after_mlp(T_UP + 2, i)
                    after_mlp(T_UP + 3, i)
                    hidden(i * 2 + 2, 0)
                    after_mlp(T_UP + 4, i)
                    after_mlp(T_UP + 5, i)
                    hidden(i * 2 + 3, 1)
                dve.wait_ge(par_in, l * 16 + 32)
                dve.wait_ge(mem_loaded, l * 16 + 16)
                for c in range(KC):
                    hi_part()
                    ins = nc.vector.scalar_tensor_tensor(
                        op_lo[0][:, c, :], feat(B[6])[:, c, :], par[:, PA["mem"] + c:PA["mem"] + c + 1],
                        op_hi[0][:, c, :].bitcast(F32), ALU.mult, ALU.subtract)
                    if c % 2:
                        ins.then_inc(op_ready, 1)
                after_mlp(A_TILES - 2)
                for b in range(TB):
                    dve.wait_ge(post_ss, l * 2 + b + 1)
                    nc.vector.tensor_tensor(y_tok[:, b, :], psum[:, 4 + 2 * b:6 + 2 * b, :].rearrange("p a n -> p (a n)"),
                                            gains[:, 1, :], ALU.mult).then_inc(post_gained, 1)
                    add_normed(1, b)
                assert step.n == DVE_STEPS, step.n

            T0 = DEPTH * A_TILES
            bstep = Steps(dve, b_step, 0)
            bhis = [0]

            def hi_b(n=1):
                bhis[0] += n
                dve.wait_ge(b_hi, bhis[0])

            def after_b(t, evac=None):
                dve.wait_ge(tile_done, T0 + t + 1)
                if evac:
                    evac()
                if t % 2 == 0 and T0 + t + 2 < N_TILES:
                    rest(T0 + t + 2, (t + 2) % 4)

            dve.wait_ge(op_ready, DEPTH * 4 * N_OPS + 4)
            for b in range(TB):
                diagonal(b, 0, (b_sd, b + 1), bstep, b_x)
            operand_lo(0, hi_b, b_ready, lambda c: par[:, PB["mix"] + c:PB["mix"] + c + 1])
            for t in range(N_FEAT + N_TOK):
                after_b(t)

            dve.wait_ge(b_evac_a, N_FEAT + N_TOK)
            dve.wait_ge(b_masks_in, 16)
            f = prep[:, 0:8].rearrange("p (b h) -> p b h", b=TB)
            bstep(nc.vector.tensor_tensor(f, v_b[:, :, F_COL:F_COL + 4],
                                          par[:, PB["fox_b"]:PB["fox_b"] + 4].unsqueeze(1).to_broadcast([P, TB, 4]), ALU.add))
            nc.vector.scalar_tensor_tensor(prep[:, 8:16], prep[:, 0:8], -1.0, prep[:, 0:8], ALU.mult, ALU.min).then_inc(f_in, 1)

            def index_add(h):
                dve.wait_ge(ix_relu, h + 1)
                for u in range(TB):
                    n = (u + 1) * P
                    w = v_b[:, u, W_COL + h:W_COL + h + 1]
                    r = expd[:, 2 * (h % 2) + u, 0:n]
                    if h == 0:
                        ins = nc.vector.tensor_scalar(index[:, u, 0:n], r, w, None, ALU.mult)
                    else:
                        ins = nc.vector.scalar_tensor_tensor(index[:, u, 0:n], r, w, index[:, u, 0:n], ALU.mult, ALU.add)
                ins.then_inc(ix_added, 1)
                dve.wait_ge(ix_added, h + 1)

            after_b(T2_GATE)
            for h in range(4):
                index_add(h)
            after_b(T2_GATE + 1)
            for h in range(4, IDX_HEADS):
                index_add(h)
            dve.wait_ge(f_ln, 2)
            bstep(nc.vector.scalar_tensor_tensor(log_f, prep[:, 0:8], 0.0, prep[:, 8:16], ALU.min, ALU.subtract))
            nc.vector.tensor_copy(log_f_wide, log_f.unsqueeze(2).to_broadcast([P, 8, P])).then_inc(f_wide, 1)
            for u in range(TB):
                own = index[:, u, u * P:(u + 1) * P]
                ins = nc.vector.scalar_tensor_tensor(own, causal, OUTSIDE / NEG, own, ALU.mult, ALU.add)
            bstep(ins)

            def take_eight():
                for u in range(TB):
                    ins = nc.vector.max(sm(SS + 8 * u, 8), index[:, u, 0:(u + 1) * P])
                bstep(ins)
                for u in range(TB):
                    s = index[:, u, 0:(u + 1) * P]
                    ins = nc.vector.match_replace(s, sm(SS + 8 * u, 8), s, REPLACED)
                bstep(ins)

            def sb_mask(h):
                dve.wait_ge(sb_ln, 3 * h + 3)
                m = expd[:, 2 * (h % 2):2 * (h % 2) + 2, :].rearrange("p a n -> p (a n)")
                bstep(nc.vector.scalar_tensor_tensor(m[:, 0:384], psum[:, 4 + h % 2, 0:384], 0.0, m[:, 0:384], ALU.max, ALU.add))
                nc.vector.tensor_tensor(m[:, 0:P], m[:, 0:P], before01, ALU.mult)
                nc.vector.tensor_tensor(m[:, 256:384], m[:, 256:384], before01, ALU.mult).then_inc(sb_masked, 1)

            def branch_lo(b, k):
                hi_b()
                nc.vector.tensor_tensor(op_lo[1][:, k, :], psum[:, 7, k * S:(k + 1) * S], op_hi[1][:, k, :].bitcast(F32),
                                        ALU.subtract).then_inc(b_ready, 1)

            def gate_product(b, n):
                dve.wait_ge(gate_open, 4 * b + n + 1)
                if n < 3:
                    dve.wait_ge(b_bank, 3 * b + n + 1)
                else:
                    dve.wait_ge(tile_done, T0 + T2_GATE + 5 * (b + 1))
                cols = slice(n * 512, (n + 1) * 512)
                dst = gate if b else merged
                nc.vector.tensor_tensor(dst[:, cols], psum[:, n, :], gate[:, cols], ALU.mult).then_inc(b_evac_d, 1)

            def add_product(b, n, signal):
                dve.wait_ge(b_evac_d, 4 * b + n + 1)
                cols = slice(n * 512, (n + 1) * 512)
                ins = nc.vector.tensor_tensor(merged[:, cols], merged[:, cols], gate[:, cols], ALU.add)
                if signal:
                    ins.then_inc(signal, 1)

            def mix_branch(b):
                for n in range(5):
                    if n < 4:
                        gate_product(b, n)
                    if n and b:
                        add_product(b, n - 1, b_mixed if n == 4 else None)
                if b == 0:
                    dve.wait_ge(b_evac_d, 4)
                    nc.vector.sem_inc(b_mixed, 1)
                else:
                    dve.wait_ge(b_mixed, b + 1)

            sb_mask(0)
            for h in range(4):
                if h % 2 == 0:
                    after_b(T2_GATE + 2 + h // 2)
                if h < 3:
                    sb_mask(h + 1)
                if h % 2:
                    branch_lo(0, h // 2)
                take_eight()

            def s_softmax(b, h):
                g = 4 * (b - 1) + h
                dve.wait_ge(s_scores, g + 1)
                e = 2 * (h % 2)
                if b == 1 and h == 0:
                    dve.wait_ge(bias_in, 16 * 16)
                for u in range(TB):
                    n = (u + 1) * P
                    sc, dst = psum[:, 4 + h % 2, u * 256:u * 256 + n], expd[:, e + u, 0:n]
                    if b == 2:
                        ins = nc.vector.scalar_tensor_tensor(dst, sc, c_col[:, 4 * u + h:4 * u + h + 1], minus_c_row[:, h, 0:n], ALU.add, ALU.add)
                    else:
                        ins = nc.vector.tensor_tensor(dst, sc, bias_b[h + (4 if b == 3 else 0)][:, u, 0:n], ALU.add)
                bstep(ins)
                if b == 2:
                    for u in range(TB):
                        own = expd[:, e + u, u * P:(u + 1) * P]
                        ins = nc.vector.tensor_tensor(own, own, causal, ALU.add)
                    bstep(ins)
                for u in range(TB):
                    ins = nc.vector.tensor_reduce(sm(NMAX + e + u), expd[:, e + u, 0:(u + 1) * P], AX.X, ALU.max, negate=True)
                ins.then_inc(s_max, 1)
                dve.wait_ge(s_exp, g + 1)
                bstep(nc.vector.reciprocal(sm(RZ + e, 2), sm(ZSUM + e, 2)))
                for u in range(TB):
                    p = expd[:, e + u, 0:(u + 1) * P]
                    ins = nc.vector.tensor_scalar(p, p, sm(RZ + e + u), None, ALU.mult)
                ins.then_inc(s_probs, 1)

            def keep_taken(h):
                for u in range(TB):
                    n = (u + 1) * P
                    ins = nc.vector.scalar_tensor_tensor(bias_b[4 + h][:, u, 0:n], index[:, u, 0:n], -NEG, bias_b[4 + h][:, u, 0:n],
                                                         ALU.mult, ALU.add)
                return ins

            for b in range(1, 4):
                mix_branch(b - 1)
                s_softmax(b, 0)
                after_b(T2_GATE + 5 * b - 1)
                for h in range(4):
                    if h < 3:
                        s_softmax(b, h + 1)
                    else:
                        branch_lo(b, 1)
                    after_b(T2_GATE + 5 * b + h)
                    if b == 1:
                        take_eight()
                    if b == 2:
                        if h == 0:
                            for u in range(TB):
                                s = index[:, u, 0:(u + 1) * P]
                                ins = nc.vector.tensor_scalar(s, s, REPLACED, 1.0, ALU.is_equal, ALU.subtract)
                            bstep(ins)
                        bstep(keep_taken(h))
                    if h == 1:
                        branch_lo(b, 0)

            def out_lo(n):
                hi_b()
                nc.vector.tensor_tensor(op_lo[0][:, 2 * n:2 * n + 2, :], feat(merged)[:, 2 * n:2 * n + 2, :],
                                        op_hi[0][:, 2 * n:2 * n + 2, :].bitcast(F32), ALU.subtract).then_inc(b_ready, 1)

            for n in range(4):
                gate_product(3, n)
                add_product(3, n, out_part)
                if n:
                    out_lo(n - 1)
            out_lo(3)
            after_b(T2_GATE + 19)

            def add_out(n):
                def evac():
                    dst = x[:, :, n * 256:(n + 1) * 256]
                    nc.vector.tensor_tensor(dst, dst, psum[:, n, :].rearrange("p (b n) -> p b n", b=TB), ALU.add).then_inc(x_part, 1)
                return evac

            for n in range(3):
                after_b(T2_OUT + n, add_out(n))
            for b in range(TB):
                if b == 0:
                    dve.wait_ge(half_done, 2 * DEPTH + 1)
                else:
                    dve.wait_ge(tile_done, T0 + T2_OUT + 4)
                dst = x[:, b, 768:1024]
                nc.vector.tensor_tensor(dst, dst, psum[:, OUT_BANKS[b], 0:256], ALU.add).then_inc(x_part, 1)
                dve.wait_ge(xb_ss, 4 + b)
                nc.vector.tensor_reduce(sm(VAR + b), sm(SS + 8 + 4 * b, 4), AX.X, ALU.add).then_inc(xb_sum, 1)
                diagonal(b, 2, (b_sd, 3 + b), bstep, b_x)
            nc.vector.memset(padded[:, :, :, 0:2], 0.0).then_inc(pads_zero, 1)
            after_b(T2_OUT + 3)
            operand_lo(0, hi_b, b_ready, lambda c: par[:, PB["ffn"] + c:PB["ffn"] + c + 1])

            def f_convolve(j):
                dve.wait_ge(f_evac, 2 * j + 2)
                if j >= 2:
                    dve.wait_ge(f_gated, j - 1)
                for k in range(3):
                    for i in range(4):
                        w = PB["conv_w"] + (k * B_UP + j) * 4 + i
                        src, acc = padded[:, j % 2, i, k:k + S], conved[:, j % 2, i, :]
                        if k == 0:
                            cb = PB["conv_b"] + 4 * j + i
                            ins = nc.vector.tensor_scalar(acc, src, par[:, w:w + 1], par[:, cb:cb + 1], ALU.mult, ALU.add)
                        else:
                            ins = nc.vector.scalar_tensor_tensor(acc, src, par[:, w:w + 1], acc, ALU.mult, ALU.add)
                    if k < 2:
                        bstep(ins)
                ins.then_inc(f_conv, 1)

            def f_operand(j):
                dve.wait_ge(f_gelu, j + 1)
                s = j % 2
                u = conved[:, s, 2:4, :].rearrange("p a t -> p (a t)")
                dve.wait_ge(f_conv, j + 1)
                if j >= 2:
                    dve.wait_ge(f_ready, j - 1)
                nc.vector.tensor_tensor(gated[:, s, :], gelu_g[:, s, :], u, ALU.mult).then_inc(f_gated, 1)
                dve.wait_ge(f_gated, j + 1)
                o = j % 4
                hi = op_hi[1][:, 2 * o:2 * o + 2, :].rearrange("p a t -> p (a t)")
                lo = op_lo[1][:, 2 * o:2 * o + 2, :].rearrange("p a t -> p (a t)")
                nc.vector.tensor_copy(hi, gated[:, s, :]).then_inc(f_hi, 1)
                dve.wait_ge(f_hi, j + 1)
                nc.vector.tensor_tensor(lo, gated[:, s, :], hi.bitcast(F32), ALU.subtract).then_inc(f_ready, 1)

            for i, (kind, j) in enumerate(FFN_ORDER[:-1]):
                t = FFN_AT[kind, j]
                after_b(t)
                if kind == "up":
                    after_b(t + 1)
                    f_convolve(j)
                    if FFN_ORDER[i + 1][0] == "up":
                        f_operand(j)
                elif j < B_UP - 3:
                    f_operand(j + 1)
                elif j == B_UP - 3:
                    f_operand(B_UP - 1)
            dve.wait_ge(final_in, 16)
            for b in range(TB):
                if b == 0:
                    dve.wait_ge(half_done, 2 * DEPTH + 2)
                else:
                    dve.wait_ge(tile_done, T0 + B_TILES)
                nc.vector.tensor_tensor(x[:, b, :], x[:, b, :], psum[:, 4 + 2 * b:6 + 2 * b, :].rearrange("p a n -> p (a n)"),
                                        ALU.add).then_inc(x_b, 1)
            for b in range(TB):
                dve.wait_ge(b_sd, 5 + b)
                bstep(nc.vector.reciprocal(sm(RS + 4 + b), sm(SD + 4 + b)))
                for n in range(2):
                    cols = slice(n * 512, (n + 1) * 512)
                    nc.vector.scalar_tensor_tensor(y_tok[:, b, cols], x[:, b, cols], sm(RS + 4 + b), merged[:, cols], ALU.mult,
                                                   ALU.mult).then_inc(y_done, 1)


def _col_tiles(w):
    n = w.shape[1] // 256
    return w.reshape(KC, P, n, 256).transpose(2, 1, 0, 3).reshape(n, P, TILE)


def _row_tiles(w):
    n = w.shape[0] // 256
    return w.reshape(n, 2, P, D).transpose(0, 2, 1, 3).reshape(n, P, TILE)


def _feat_vector(v):
    return np.ascontiguousarray(v.reshape(-1, P).T)


def _weight_stream(a):
    stream = np.empty((N_TILES, P, TILE), np.float32)
    at = 0

    def put(tiles):
        nonlocal at
        stream[at:at + len(tiles)] = tiles
        at += len(tiles)

    for l in range(DEPTH):
        q, k, v, zx, zy, xq, g = np.split(a["w_in"][l], np.cumsum([D] * 6), axis=1)
        put(_col_tiles(a["w_kv_mem"][l]))
        for w in (xq, q, k, v, zx, zy):
            put(_col_tiles(w))
        for branch, w in ((2, "w_proj_mem"), (0, "w_proj_attn"), (1, "w_proj_lru")):
            put(_col_tiles(g[:, branch * D:(branch + 1) * D]))
            put(_col_tiles(a[w][l]))
        put(_col_tiles(a["w_out"][l]))
        ups, downs = _col_tiles(a["w_mlp_up"][l]), _row_tiles(a["w_mlp_down"][l])
        put(ups[0:1])
        for j in range(A_UP):
            if j + 1 < A_UP:
                put(ups[j + 1:j + 2])
            put(downs[j:j + 1])
    assert at == DEPTH * A_TILES
    _block_b_tiles(a, put)
    assert at == N_TILES
    return stream


def _rope_tables():
    half = A_HD // 2
    inv = (np.float32(1.0) / (np.float32(10000.0) ** (np.arange(half, dtype=np.float32) / np.float32(half)))).astype(np.float32)
    ang = np.arange(S, dtype=np.float32)[:, None] * inv[None, :]
    both = [f(ang).astype(np.float32).reshape(TB, P, half).transpose(1, 0, 2) for f in (np.cos, np.sin)]
    return [np.ascontiguousarray(t) for t in both]


def _params(a):
    par = np.zeros((DEPTH + 1, P, N_PAR), np.float32)

    def put(l, table, name, v):
        par[l, :, table[name]:table[name] + v.shape[1]] = v

    for l in range(DEPTH):
        init = 0.8 - 0.6 * math.exp(-0.3 * l)
        for name, v in (("mix_pre", a["norm_mix_pre"]), ("mlp_pre", a["norm_mlp_pre"]), ("mem", a["norm_mem"]),
                        ("b_gate", a["b_gate"]), ("conv_w", a["conv_w"]), ("conv_b", a["conv_b"]), ("rg_ba", a["rg_ba"]),
                        ("rg_bi", a["rg_bi"]), ("rg_lambda", a["rg_lambda"]), ("subln", a["diff_subln"])):
            put(l, PA, name, _feat_vector(v[l]))
        put(l, PA, "one_minus_init", np.full((P, 1), 1.0 - init, np.float32))
        put(l, PA, "init", np.full((P, 1), init, np.float32))
        for name, pair in (("lambda_q", ("lambda_q1", "lambda_q2")), ("lambda_k", ("lambda_k1", "lambda_k2"))):
            row = np.concatenate([a[n][l] for n in pair])
            put(l, PA, name, np.broadcast_to(row, (P, 128)))
    _block_b_params(a, lambda name, v: put(DEPTH, PB, name, v))
    return par


B_SIZES = [256] * 9 + [4, 256, 64, 64, 256, 32, 8]


def _block_b_tiles(a, put):
    (sq, sk, sv, mq, mk, mv, fq, fk, fv, ff, dq, dk, dv, iq, ik, iw) = np.split(a["w_in_2"][0], np.cumsum(B_SIZES)[:-1], axis=1)
    pad = lambda w, n: np.concatenate([w, np.zeros((D, n - w.shape[1]), np.float32)], axis=1)
    put(_col_tiles(pad(np.concatenate([sq, sk, mq, mk, fq, fk, dq, dk, dk, ik, ik, ik, ik, iq], axis=1), N_FEAT * 256)))
    put(_col_tiles(pad(np.concatenate([sv, mv, fv, dv, iw, ff], axis=1), N_TOK * 256)))
    for b in range(4):
        put(_col_tiles(a["w_gate_2"][0, b]))
        put(_row_tiles(a["w_branch_2"][0, b]))
    put(_col_tiles(a["w_out_2"][0]))
    gs, us = _col_tiles(a["w_up_2"][0][:, :B_FF]), _col_tiles(a["w_up_2"][0][:, B_FF:])
    downs = _row_tiles(a["w_down_2"][0])
    for kind, j in FFN_ORDER:
        if kind == "up":
            put(gs[j:j + 1])
            put(us[j:j + 1])
        else:
            put(downs[j:j + 1])


def _block_b_params(a, put):
    put("mix", _feat_vector(a["norm_mix_g_2"][0]))
    put("ffn", _feat_vector(a["norm_ffn_g_2"][0]))
    put("fox_b", np.broadcast_to(a["fox_b_f_2"][0], (P, 4)))
    for name, v in (("conv_w", a["conv_w_2"][0]), ("conv_b", a["conv_b_2"][0])):
        v = v.reshape(-1, 2, B_UP, 2, P).transpose(0, 2, 1, 3, 4)
        put(name, _feat_vector(v))


def _masks():
    p, j = np.arange(P)[:, None], np.arange(P)[None, :]
    one = np.ones((P, P))
    m = [p <= j, one, -(p >= j).astype(float), -one, p < j, np.where(p < j, 0.0, NEG), np.where(j <= p, 0.0, NEG)]
    return np.ascontiguousarray(np.stack(m, axis=1).astype(np.float32).reshape(P, 7 * P))


def _t5_constants():
    n = 255 - np.arange(512)
    near = np.maximum(n, 1).astype(np.float32)
    large = 16 + (np.log(near / np.float32(16)) / np.float32(math.log(128 / 16)) * np.float32(16)).astype(np.int32)
    bucket = np.where(np.maximum(n, 0) < 16, np.maximum(n, 0), np.minimum(large, 31))
    rows = np.zeros((33, 512), np.float32)
    rows[bucket, np.arange(512)] = 1.0
    rows[32] = np.where(n < 0, NEG, 0.0)
    return rows


def kernel(**a):
    import concourse.bacc as bacc
    from concourse.bass_utils import run_bass_kernel_spmd

    a = {k: np.asarray(v) for k, v in a.items()}

    def tok(v):
        return np.ascontiguousarray(v.reshape(TB, P, -1).transpose(1, 0, 2))

    cos, sin = _rope_tables()
    arrays = {
        "stream": _weight_stream(a), "x_in": tok(a["x"][0]), "mem_in": tok(a["mem"][0]).reshape(P, TB * D), "params": _params(a),
        "post_gain": np.ascontiguousarray(np.broadcast_to(
            np.stack([a["norm_mix_post"], a["norm_mlp_post"]], 1).reshape(DEPTH, 1, 2 * D), (DEPTH, P, 2 * D))),
        "rg_w": np.ascontiguousarray(np.stack([a["rg_wa"], a["rg_wi"]], 1).transpose(0, 3, 1, 2, 4).reshape(DEPTH, P, 2048)),
        "cos_in": cos, "sin_in": sin, "ident_in": np.eye(P, dtype=np.float32), "masks_in": _masks(),
        "t5_in": np.concatenate([_t5_constants(), np.concatenate([a["t5_bias_2"], np.ones((1, 8), np.float32)])], axis=1),
        "final_gain": np.ascontiguousarray(np.broadcast_to(a["norm_final_g_2"], (P, D))),
    }
    nc = bacc.Bacc("TRN2", target_bir_lowering=False, num_devices=1)
    args = {k: nc.dram_tensor(k, v.shape, mybir.dt.from_np(v.dtype), kind="ExternalInput").ap() for k, v in arrays.items()}
    args["out"] = nc.dram_tensor("out", (P, TB, D), F32, kind="ExternalOutput").ap()
    build(nc, **args)
    got = run_bass_kernel_spmd(nc, [arrays], core_ids=[0]).results[0]["out"]
    return got.transpose(1, 0, 2).reshape(1, S, D)
```
